# Optimizing a Trainium2 kernel written in Bass

```python
import math
import jax, jax.numpy as jnp
from jax import lax
import numpy as np

D_MODEL = 1024
BATCH = 1
SEQ = 1024
DEPTH = 1
DEC_BATCH = 8
DEC_SEQ = 16
PAST_LEN = 1024

CHUNK = 64
N_HEADS = 8
HEAD_DIM = 64
ATTN_W = N_HEADS * HEAD_DIM
N_IDX_HEADS = 8
IDX_DIM = 64
TOPK_MAX = 256
CONV_CH = 512
CONV_K = 31
FFN_HIDDEN = -(-8 * D_MODEL // (3 * 256)) * 256
NUM_BUCKETS = 32
MAX_DISTANCE = 128
Q_BLOCK = 128
EPS = 1e-6
NEG = -1e30
IN_SIZES = (ATTN_W, ATTN_W, ATTN_W, N_IDX_HEADS * IDX_DIM, IDX_DIM, N_IDX_HEADS, 2 * CONV_CH, D_MODEL, D_MODEL)
IN_COLS = 3 * ATTN_W + N_IDX_HEADS * IDX_DIM + IDX_DIM + N_IDX_HEADS + 2 * CONV_CH + 2 * D_MODEL

kernel_name = "hybrid_dsa_conformer_stream_step"

def _rmsnorm(x, g):
    xf = x.astype(jnp.float32)
    y = xf * lax.rsqrt(jnp.mean(xf * xf, axis=-1, keepdims=True) + EPS)
    return (y * g.astype(jnp.float32)).astype(x.dtype)

def _layernorm(x, g, b):
    xf = x.astype(jnp.float32)
    mu = jnp.mean(xf, axis=-1, keepdims=True)
    var = jnp.mean(jnp.square(xf - mu), axis=-1, keepdims=True)
    y = (xf - mu) * lax.rsqrt(var + EPS) * g.astype(jnp.float32) + b.astype(jnp.float32)
    return y.astype(x.dtype)

def _rel_bucket(rel):
    nb = NUM_BUCKETS // 2
    max_exact = nb // 2
    ret = jnp.where(rel > 0, nb, 0)
    n = jnp.abs(rel)
    nf = jnp.maximum(n, 1).astype(jnp.float32)
    large = max_exact + (jnp.log(nf / max_exact) / math.log(MAX_DISTANCE / max_exact) * (nb - max_exact)).astype(jnp.int32)
    large = jnp.minimum(large, nb - 1)
    return ret + jnp.where(n < max_exact, n, large)

def _gather_rows(a, idx):
    return jax.vmap(lambda ab, ib: ab[ib])(a, idx)

def _sparse_attention(q, iq, iw, q_pos, keys, vals, ikeys, k_pos, rel_bias, top_k):
    idx_logits = jnp.einsum('bqhd,bsd->bqhs', iq, ikeys).astype(jnp.float32) * (IDX_DIM ** -0.5)
    score = jnp.einsum('bqhs,bqh->bqs', jax.nn.relu(idx_logits), iw.astype(jnp.float32))
    admissible = (k_pos[None, :] // CHUNK) <= (q_pos[:, None] // CHUNK)
    score = jnp.where(admissible[None], score, NEG)
    _, sel = lax.top_k(score, top_k)
    k_sel = _gather_rows(keys, sel)
    v_sel = _gather_rows(vals, sel)
    sel_pos = k_pos[sel]
    valid = (sel_pos // CHUNK) <= (q_pos[None, :, None] // CHUNK)
    bias = rel_bias[_rel_bucket(sel_pos - q_pos[None, :, None])].astype(jnp.float32)
    logits = jnp.einsum('bqhd,bqkhd->bqhk', q, k_sel).astype(jnp.float32) * (HEAD_DIM ** -0.5)
    logits = logits + jnp.moveaxis(bias, -1, 2)
    logits = jnp.where(valid[:, :, None, :], logits, NEG)
    p = jax.nn.softmax(logits, axis=-1).astype(vals.dtype)
    return jnp.einsum('bqhk,bqkhd->bqhd', p, v_sel)

def _layer(x, pos0, past_k, past_v, past_ik, past_conv, rel_bias,
           norm_mix_g, w_in, q_norm_g, k_norm_g, idx_k_norm_g, conv_dw_w, conv_dw_b, conv_ln_g, conv_ln_b,
           w_conv_out, w_attn_out, w_out, norm_ffn_g, w_ffn_gate, w_ffn_up, w_ffn_down):
    B, T, _ = x.shape
    h = _rmsnorm(x, norm_mix_g)
    proj = h @ w_in
    splits = []
    off = 0
    for s in IN_SIZES[:-1]:
        off += s
        splits.append(off)
    q, k, v, iq, ik, iw, glu, ga, gc = jnp.split(proj, splits, axis=-1)
    q = _rmsnorm(q.reshape(B, T, N_HEADS, HEAD_DIM), q_norm_g)
    k = _rmsnorm(k.reshape(B, T, N_HEADS, HEAD_DIM), k_norm_g)
    v = v.reshape(B, T, N_HEADS, HEAD_DIM)
    iq = iq.reshape(B, T, N_IDX_HEADS, IDX_DIM)
    ik = _rmsnorm(ik, idx_k_norm_g)
    iw = iw * (N_IDX_HEADS ** -0.5)

    keys = jnp.concatenate([past_k, k], axis=1)
    vals = jnp.concatenate([past_v, v], axis=1)
    ikeys = jnp.concatenate([past_ik, ik], axis=1)
    L = keys.shape[1]
    top_k = min(TOPK_MAX, L // 4)
    k_pos = jnp.arange(L, dtype=jnp.int32)
    q_pos = pos0 + jnp.arange(T, dtype=jnp.int32)
    qb = min(Q_BLOCK, T)
    nb = T // qb

    def blocks(a):
        return jnp.moveaxis(a.reshape((B, nb, qb) + a.shape[2:]), 1, 0)

    attn = lax.map(
        lambda blk: _sparse_attention(blk[0], blk[1], blk[2], blk[3], keys, vals, ikeys, k_pos, rel_bias, top_k),
        (blocks(q), blocks(iq), blocks(iw), q_pos.reshape(nb, qb)))
    attn = jnp.moveaxis(attn, 0, 1).reshape(B, T, ATTN_W)
    attn_out = attn @ w_attn_out

    ga_in, gb_in = jnp.split(glu, 2, axis=-1)
    u = ga_in * jax.nn.sigmoid(gb_in)
    u_full = jnp.concatenate([past_conv, u], axis=1)
    c = lax.conv_general_dilated(u_full, conv_dw_w.astype(u_full.dtype), (1,), 'VALID',
                                 dimension_numbers=('NWC', 'WIO', 'NWC'), feature_group_count=CONV_CH)
    c = jax.nn.silu(_layernorm(c + conv_dw_b, conv_ln_g, conv_ln_b))
    conv_out = c @ w_conv_out

    merged = jax.nn.sigmoid(ga) * attn_out + jax.nn.sigmoid(gc) * conv_out
    x = x + merged @ w_out
    h2 = _rmsnorm(x, norm_ffn_g)
    x = x + (jax.nn.silu(h2 @ w_ffn_gate) * (h2 @ w_ffn_up)) @ w_ffn_down
    return x, k, v, ik, u_full[:, -(CONV_K - 1):]

def setup_inputs(seed: int = 0) -> dict:
    key = jax.random.key(seed)
    ks = jax.random.split(key, 26)
    f32 = jnp.float32

    def nrm(k, shape, scale):
        return jax.random.normal(k, shape, f32) * scale

    def gain(k, shape):
        return 1.0 + 0.05 * jax.random.normal(k, shape, f32)

    return {
        "x_prompt": nrm(ks[0], (BATCH, SEQ, D_MODEL), 1.0),
        "x_sample": nrm(ks[1], (DEC_BATCH, DEC_SEQ, D_MODEL), 1.0),
        "cache_k": nrm(ks[2], (DEPTH, DEC_BATCH, PAST_LEN, N_HEADS, HEAD_DIM), 1.0),
        "cache_v": nrm(ks[3], (DEPTH, DEC_BATCH, PAST_LEN, N_HEADS, HEAD_DIM), 1.0),
        "cache_idx_k": nrm(ks[4], (DEPTH, DEC_BATCH, PAST_LEN, IDX_DIM), 1.0),
        "state_conv": nrm(ks[5], (DEPTH, DEC_BATCH, CONV_K - 1, CONV_CH), 0.5),
        "rel_bias": nrm(ks[6], (NUM_BUCKETS, N_HEADS), 0.5),
        "norm_mix_g": gain(ks[7], (DEPTH, D_MODEL)),
        "w_in": nrm(ks[8], (DEPTH, D_MODEL, IN_COLS), D_MODEL ** -0.5),
        "q_norm_g": gain(ks[9], (DEPTH, HEAD_DIM)),
        "k_norm_g": gain(ks[10], (DEPTH, HEAD_DIM)),
        "idx_k_norm_g": gain(ks[11], (DEPTH, IDX_DIM)),
        "conv_dw_w": nrm(ks[12], (DEPTH, CONV_K, 1, CONV_CH), CONV_K ** -0.5),
        "conv_dw_b": nrm(ks[13], (DEPTH, CONV_CH), 0.02),
        "conv_ln_g": gain(ks[14], (DEPTH, CONV_CH)),
        "conv_ln_b": nrm(ks[15], (DEPTH, CONV_CH), 0.02),
        "w_conv_out": nrm(ks[16], (DEPTH, CONV_CH, D_MODEL), CONV_CH ** -0.5),
        "w_attn_out": nrm(ks[17], (DEPTH, ATTN_W, D_MODEL), ATTN_W ** -0.5),
        "w_out": nrm(ks[18], (DEPTH, D_MODEL, D_MODEL), D_MODEL ** -0.5),
        "norm_ffn_g": gain(ks[19], (DEPTH, D_MODEL)),
        "w_ffn_gate": nrm(ks[20], (DEPTH, D_MODEL, FFN_HIDDEN), D_MODEL ** -0.5),
        "w_ffn_up": nrm(ks[21], (DEPTH, D_MODEL, FFN_HIDDEN), D_MODEL ** -0.5),
        "w_ffn_down": nrm(ks[22], (DEPTH, FFN_HIDDEN, D_MODEL), FFN_HIDDEN ** -0.5),
    }

def reference(x_prompt, x_sample, cache_k, cache_v, cache_idx_k, state_conv, rel_bias,
              norm_mix_g, w_in, q_norm_g, k_norm_g, idx_k_norm_g, conv_dw_w, conv_dw_b, conv_ln_g, conv_ln_b,
              w_conv_out, w_attn_out, w_out, norm_ffn_g, w_ffn_gate, w_ffn_up, w_ffn_down):
    Bp = x_prompt.shape[0]
    past_len = cache_k.shape[2]
    yp = x_prompt
    ys = x_sample
    kp_l, vp_l, ikp_l, cp_l = [], [], [], []
    ks_l, vs_l, iks_l, cs_l = [], [], [], []
    for l in range(DEPTH):
        lw = (norm_mix_g[l], w_in[l], q_norm_g[l], k_norm_g[l], idx_k_norm_g[l], conv_dw_w[l], conv_dw_b[l],
              conv_ln_g[l], conv_ln_b[l], w_conv_out[l], w_attn_out[l], w_out[l], norm_ffn_g[l],
              w_ffn_gate[l], w_ffn_up[l], w_ffn_down[l])
        empty_kv = jnp.zeros((Bp, 0, N_HEADS, HEAD_DIM), yp.dtype)
        empty_ik = jnp.zeros((Bp, 0, IDX_DIM), yp.dtype)
        zero_conv = jnp.zeros((Bp, CONV_K - 1, CONV_CH), yp.dtype)
        yp, kp, vp, ikp, cp = _layer(yp, 0, empty_kv, empty_kv, empty_ik, zero_conv, rel_bias, *lw)
        kp_l.append(kp); vp_l.append(vp); ikp_l.append(ikp); cp_l.append(cp)
        ys, kn, vn, ikn, cn = _layer(ys, past_len, cache_k[l], cache_v[l], cache_idx_k[l], state_conv[l],
                                     rel_bias, *lw)
        ks_l.append(kn); vs_l.append(vn); iks_l.append(ikn); cs_l.append(cn)
    new_k_prompt = jnp.stack(kp_l)
    new_v_prompt = jnp.stack(vp_l)
    new_idx_k_prompt = jnp.stack(ikp_l)
    new_conv_prompt = jnp.stack(cp_l)
    new_k_sample = jnp.stack(ks_l)
    new_v_sample = jnp.stack(vs_l)
    new_idx_k_sample = jnp.stack(iks_l)
    new_conv_sample = jnp.stack(cs_l)
    return (yp, ys, new_k_prompt, new_v_prompt, new_idx_k_prompt, new_conv_prompt,
            new_k_sample, new_v_sample, new_idx_k_sample, new_conv_sample)


_drawn_inputs = setup_inputs


def setup_inputs(seed=0):
    import zlib

    import numpy as np

    out = dict(_drawn_inputs(seed))
    spreads = {}
    factors = {'q_norm_g': 8.0, 'conv_dw_b': 4.082, 'conv_ln_g': 2.869, 'conv_ln_b': 7.909}
    for name, (base, spread) in spreads.items():
        noise = np.random.default_rng([zlib.crc32(name.encode()), seed]).standard_normal(out[name].shape)
        drawn = base * np.exp(spread * noise) if base else spread * noise
        out[name] = __import__('jax').numpy.asarray(drawn.astype(out[name].dtype))
    for name, factor in factors.items():
        out[name] = (out[name] * factor).astype(out[name].dtype)
    return out
```

```python
import math
from contextlib import ExitStack

import numpy as np
import concourse.bass as bass
from concourse import mybir

F32 = mybir.dt.float32
F32R = mybir.dt.float32r
ALU = mybir.AluOpType
ACT = mybir.ActivationFunctionType
AX = mybir.AxisListType

P = 128
D = 1024
NP = 1024
NS, QS = 8, 16
PAST = 1024
NTOK = NP + NS * QS
NT = NTOK // P
PB = NP // P
G = 384
NG = NTOK // G
H, HD = 8, 64
HP = H // 2
AW = H * HD
CH = 512
CT = CH // P
CK = 31
HIST = CK - 1
FF = -(-8 * D // (3 * 256)) * 256
FT = FF // P
KD = D // P
TOPK = 256
CHUNK = 64
NB = 32
EPS = 1e-6
NEG = -1e30
TAKEN = -3e38
LS = PAST + NS * QS
RMIN = -(2 * P - 1)
RN = 3 * P
IDXC = H * HD
ISC = (HD ** -0.5) * (H ** -0.5)
UP = HIST + NP
US = HIST + QS
UW = UP + NS * US


SLAB = 53184


def bucket_rows():
    rel = np.arange(RMIN, RMIN + RN)
    n = np.abs(rel)
    nf = np.maximum(n, 1).astype(np.float32)
    large = 8 + (np.log(nf / np.float32(8)) / np.float32(math.log(16)) * np.float32(8)).astype(np.int32)
    b = np.where(rel > 0, 16, 0) + np.where(n < 8, n, np.minimum(large, 15))
    return (b[None, :] == np.arange(NB)[:, None]).astype(np.float32)


class Chain:

    def __init__(self, eng, sem):
        self.eng, self.sem, self.n, self.base, self.i, self.per = eng, sem, 0, 0, None, 0

    def add(self, ins):
        ins.then_inc(self.sem, 1)
        self.n += 1

    def loop(self, i, per):
        self.base, self.n, self.i, self.per = self.base + self.n, 0, i, per

    def done(self, trips):
        assert self.n == self.per, (self.n, self.per)
        self.base, self.n, self.i = self.base + trips * self.per, 0, None

    def wait(self):
        at = self.base + self.n
        self.eng.wait_ge(self.sem, at if self.i is None else self.i * self.per + at)

    def link(self, ins):
        self.add(ins)
        self.wait()


def build(nc, A, O):
    with ExitStack() as ctx:
        sbuf0 = -(-nc.sbuf_base // 32) * 32
        ps = ctx.enter_context(nc.psum_tensor("ps", [P, 8 * 512], F32))

        def sem(name):
            return ctx.enter_context(nc.semaphore(name))

        at = [0]
        bufs = [0]

        def take(n, off=None):
            if off is None:
                off = at[0]
                at[0] += n
            return place(n, off, F32)

        def take_r(n, off):
            return place(n, off, F32R)

        def place(n, off, dtype):
            assert off + n <= SLAB
            bufs[0] += 1
            return nc.alloc_sbuf_tensor_at(f"buf{bufs[0]}", [P, n], dtype, offset=sbuf0 + 4 * off)[:]

        def bank(b, n=512, w=1):
            return ps[:, 512 * b:512 * (b + w - 1) + n]

        ident = take(P)
        ones = take(P)
        gmix = take(D)
        qg, kg = take(AW), take(AW)
        ikg = take(HD)
        small = take(400)
        iwN = take(NT * H).rearrange("p (t h) -> p t h", t=NT)
        delta = take(QS)
        newneg = take(P)
        mhalf = small[:, 0:16]
        ss = small[:, 16:32]
        ms = small[:, 32:48]
        rstd = small[:, 48:64]
        iwS = small[:, 64:72]
        cw = small[:, 72:72 + CT * CK].rearrange("p (j k) -> p j k", j=CT)
        cb = small[:, 196:200]
        lng = small[:, 200:204]
        lnb = small[:, 204:208]
        mx = small[:, 208:224]
        nmx = small[:, 224:240]
        sm = small[:, 240:256]
        rc = small[:, 256:272]
        m8 = small[:, 272:280]
        epsc = small[:, 280:281]
        per_d = small[:, 281:282]
        eps8 = small[:, 384:392]
        per_hd = small[:, 392:400]
        ssq = small[:, 288:320]
        msq = small[:, 320:352]
        rsq = small[:, 352:384]
        o_h = at[0]
        hT = take(KD * NTOK).rearrange("p (k t) -> p k t", k=KD)
        o_q = at[0]
        qT = take(HP * NTOK).rearrange("p (c t) -> p c t", c=HP)
        o_k = at[0]
        kT = take(HP * NTOK).rearrange("p (c t) -> p c t", c=HP)
        score = {b: take((b + 1) * P) for b in range(2, PB)}
        scoreS = take(LS)
        uT = take(CT * UW).rearrange("p (j t) -> p j t", j=CT)
        o_w = at[0]

        iqT = take(HP * NTOK, o_q).rearrange("p (c t) -> p c t", c=HP)
        wiq = take(KD * IDXC, o_k).rearrange("p (k c) -> p k c", k=KD)
        xb = take(3 * D, o_w).rearrange("p (s d) -> p s d", s=3)
        hb = take(3 * D, o_w + 3 * D).rearrange("p (s d) -> p s d", s=3)
        o = o_w + 6 * D
        ikc = take(NS * 8 * HD, o).rearrange("p (s k d) -> p s k d", s=NS, k=8)
        o += NS * 8 * HD
        ikcT = take(2 * PAST, o).rearrange("p (s t) -> p s t", s=2)
        o += 2 * PAST
        ikT = take(NTOK, o)
        o += NTOK
        rl = take(2 * LS, o_w).rearrange("p (s t) -> p s t", s=2)
        ikwN = take(NT * 72, o_w + 3 * LS).rearrange("p (t c) -> p t c", t=NT)
        ikn = take(NT * P, o_w + 3 * LS + 648).rearrange("p (t c) -> p t c", t=NT)
        assert 4 * LS + 648 <= 6 * D
        iqS = take(H * P, o).rearrange("p (s h q) -> p s h q", s=NS, h=H)
        o += H * P
        wikw = take(KD * 72, o).rearrange("p (k c) -> p k c", k=KD)
        o += KD * 72
        SW = take(NS * P, o).rearrange("p (s t) -> p s t", s=NS)
        o += NS * P
        st = take(2 * CH, o).rearrange("p (s c) -> p s c", s=2)
        o += 2 * CH
        ikwT = take(NTOK, o)
        o += NTOK

        wglu = take(4 * KD * P, o_k).rearrange("p (s g k c) -> p s g k c", s=2, g=2, k=KD)
        wqkv = [take(KD * AW, o_w).rearrange("p (k c) -> p k c", k=KD),
                take(KD * AW, o_w + 6 * D).rearrange("p (k c) -> p k c", k=KD)]
        wgate = take(2 * KD * P, o_w + KD * AW).rearrange("p (s k c) -> p s k c", s=2, k=KD)
        gb = take(2 * NTOK, o_w + 6 * D).rearrange("p (s t) -> p s t", s=2)
        o = o_w + 6 * D + KD * AW
        sqc = take(CT * NTOK, o).rearrange("p (j t) -> p j t", j=CT)
        hs = take(3 * D, o).rearrange("p (s k t) -> p s k t", s=3, k=KD)
        raw = take(3 * AW, o + 3 * D).rearrange("p (s c) -> p s c", s=3)
        qn = take(3 * AW, o + 3 * D + 3 * AW).rearrange("p (s c) -> p s c", s=3)
        o = o_w + 17088
        assert o >= o_w + 6 * D + KD * AW + 3 * D + 6 * AW
        sigb = take(NTOK, o).rearrange("p (c t) -> p c t", c=NG)
        acc = take(NTOK, o)
        acopy = take(NTOK, o + NTOK).rearrange("p (c t) -> p c t", c=NG)
        us = take(CT * P, o + NTOK).rearrange("p (j t) -> p j t", j=CT)
        uo = take(CH, o + NTOK + CH)
        ut = take(CH, o + NTOK + 2 * CH)
        uSamp = uT[:, :, UP:].rearrange("p j (s t) -> p j s t", s=NS)
        cT = uT[:, :, 0:NTOK]
        NLOG = (PB - 2) * H

        onehot = take(RN, o_w + 18240)
        relb = take(H, o_w + 18240 + RN)
        brow = take(RN, o_w + 18240 + RN + H)
        bfar = take(1, o_w + 18240 + 2 * RN + H)
        vN = take(NT * AW, o_h).rearrange("p (t c) -> p t c", t=NT)
        attnT = take(HP * NTOK, o_h + NT * AW).rearrange("p (c t) -> p c t", c=HP)
        lp = take(2 * LS, o_w).rearrange("p (s t) -> p s t", s=2)
        pT = take(2 * LS, o_w + 2 * LS).rearrange("p (s t) -> p s t", s=2)
        biasS = take(LS, o_w + 4 * LS)
        o = o_w + 5 * LS
        kc = take(2 * 4 * AW, o).rearrange("p (s k c) -> p s k c", s=2, k=4)
        o += 8 * AW
        vc = take(2 * 8 * AW, o).rearrange("p (s k c) -> p s k c", s=2, k=8)
        o += 16 * AW
        near = take(H * 2 * P, o).rearrange("p (h j) -> p h j", h=H)
        msel = take(NS * P, o).rearrange("p (s m) -> p s m", s=NS)
        nb = [uT[:, e, NTOK:NTOK + 2 * P] for e in range(2)]
        mask0 = uT[:, 2, NTOK:NTOK + 2 * P]
        kcT = take(HP * PAST, o_h).rearrange("p (c t) -> p c t", c=HP)
        o_s = o_k + HP * NTOK
        qbd = take(NS * HP * P, o_s).rearrange("p (s c m) -> p s c m", s=NS, c=HP)
        mergedT = take(KD * NTOK, o_q).rearrange("p (k t) -> p k t", k=KD)
        wab = take(2 * KD * P, o_w).rearrange("p (s k c) -> p s k c", s=2, k=KD)
        gt = take(4 * NTOK, o_w + 2 * KD * P).rearrange("p (s g t) -> p s g t", s=2, g=2)
        o = o_w + 2 * KD * P + 4 * NTOK
        part = take(2 * 2 * G, o).rearrange("p (s g t) -> p s g t", s=2, g=2)
        wout = take(KD * D, o_w + KD * NTOK).rearrange("p (k c) -> p k c", k=KD)
        hs2 = take(3 * D, o_s).rearrange("p (s k t) -> p s k t", s=3, k=KD)
        xs = take(3 * D, o_s + PB * (PB + 1) // 2 * P - 3 * P + LS).rearrange("p (s d) -> p s d", s=3)
        x1 = take(NT * D, o_h).rearrange("p (t d) -> p t d", t=NT)
        h2hi = take_r(KD * NTOK, o_w).rearrange("p (k t) -> p k t", k=KD)
        h2lo = take_r(KD * NTOK, o_q).rearrange("p (k t) -> p k t", k=KD)
        o = o_s
        wraw = take(2 * 2 * D, o).rearrange("p (s n) -> p s n", s=2)
        wguhi = take_r(2 * 2 * D, o + 4 * D).rearrange("p (s n) -> p s n", s=2)
        sg = take(2 * G, o + 8 * D).rearrange("p (s t) -> p s t", s=2)
        fhi = take_r(2 * G, o + 8 * D + 2 * G).rearrange("p (s t) -> p s t", s=2)
        flo = take_r(2 * G, o + 8 * D + 4 * G).rearrange("p (s t) -> p s t", s=2)
        assert o + 8 * D + 6 * G <= o_w
        o = o_w + KD * NTOK
        wgulo = take_r(2 * 2 * D, o).rearrange("p (s n) -> p s n", s=2)
        wdraw = take(2 * D, o + 4 * D).rearrange("p (s n) -> p s n", s=2)
        wdlo = take_r(2 * D, o + 4 * D).rearrange("p (s n) -> p s n", s=2)
        wdhi = take_r(2 * D, o + 6 * D).rearrange("p (s n) -> p s n", s=2)
        ys = take(3 * D, o + 8 * D).rearrange("p (s d) -> p s d", s=3)
        units = [(b, h) for b in range(PB) for h in range(H)]

        s = {}

        def S(name):
            if name not in s:
                s[name] = sem(name)
            return s[name]

        block = ctx.enter_context(nc.Block())

        def tok(t, n=P):
            return bass.ds(t * n, n)

        NCONST = 17

        @block.sync
        def _(sp):
            def const(dst, src):
                sp.dma_start(dst, src).then_inc(S("const_in"), 16)

            const(ident, A["ident"])
            const(gmix, A["norm_mix_g"].partition_broadcast(P))
            for j in range(3):
                sp.dma_start(xb[:, j], A["x"][tok(j), :]).then_inc(S(f"x_in{j}"), 16)
            const(qg, A["qg"].partition_broadcast(P))
            const(kg, A["kg"].partition_broadcast(P))
            const(ikg, A["idx_k_norm_g"].partition_broadcast(P))
            const(delta, A["delta"])
            const(newneg, A["newneg"])
            const(wikw, A["w_ikw"])
            const(cw, A["conv_w"])
            const(cb, A["conv_b"])
            const(lng, A["conv_ln_g"])
            const(lnb, A["conv_ln_b"])
            for c in range(2):
                const(st[0:120, c], A["state"][120 * c:120 * c + 120, :])
            const(onehot[0:NB], A["onehot"])
            const(relb[0:NB], A["rel_bias"])
            const(wiq, A["w_iq"])
            with sp.Fori(1, NG) as i:
                for j in range(3):
                    sp.wait_ge(S("h_made"), i * 3 + j - 2)
                    sp.dma_start(xb[:, j], A["x"][tok(i * 3 + j), :]).then_inc(S(f"x_in{j}"), 16)
            sp.dma_start(ikc, A["cache_ik"]).then_inc(S("ikc_in"), 16)

            sp.wait_ge(S("brow_made"), 1)
            sp.dma_start(A["bias_scr"], brow[0:H].unsqueeze(1).to_broadcast([H, P, RN])).then_inc(S("bias_out"), 16)

            sp.wait_ge(S("ikn_made"), 2)
            sp.dma_start(O["ik"].rearrange("(t p) d -> p t d", p=P), ikn[:, :, 0:HD]).then_inc(S("ik_out"), 16)
            sp.wait_ge(S("iw_made"), 1)
            sp.dma_start(A["iw_scr"], iwN[:, NT - 1]).then_inc(S("iw_out"), 16)
            sp.wait_ge(S("iw_out"), 16)
            for h in range(H):
                sp.dma_start(iwS[h * QS:(h + 1) * QS, :],
                             A["iw_scr"].rearrange("(s q) h -> h q s", q=QS)[h],
                             allow_slow_non_contiguous=True).then_inc(S("iws_in"), 16)
            sp.wait_ge(S("iq_made"), NG * (HP + 1))
            for h in range(H):
                sp.dma_start(iqS[0:HD, :, h], iqT[64 * (h % 2):64 * (h % 2) + 64, h // 2, NP:NTOK]
                             .rearrange("p (s q) -> p s q", s=NS)).then_inc(S("iqs_in"), 16)
            sp.wait_ge(S("iq_done"), NG * (HP + 1))
            for j in range(CT):
                if j >= 2:
                    sp.wait_ge(S("glu_a_done"), NG * (j - 1))
                sp.dma_start(wglu[:, j % 2], A["w_glu"][j]).then_inc(S(f"wglu_in{j % 2}"), 16)
                if j == 1:
                    sp.wait_ge(S("score_done"), PB - 1)
                    for c in range(2):
                        sp.dma_start(wqkv[c], A["w_qkv"][c]).then_inc(S(f"wqkv_in{c}"), 16)

            def copy_h(c, i, first):
                for j in range(3):
                    if not first:
                        sp.wait_ge(S("qkv_done"), c * NT + i * 3 + j - 2)
                    sp.dma_start(hs[:, j], hT[:, :, tok(i * 3 + j)]).then_inc(S(f"hs_in{j}"), 16)

            for c in range(3):
                copy_h(c, 0, c == 0)
                if c == 1:
                    sp.dma_start(wqkv[0], A["w_qkv"][2]).then_inc(S("wqkv_in0"), 16)
                if c == 2:
                    for e in range(2):
                        sp.dma_start(wgate[:, e], A["w_gates"][e]).then_inc(S(f"wgate_in{e}"), 16)
                with sp.Fori(1, NG) as i:
                    copy_h(c, i, False)
            with sp.Fori(1, KD) as i:
                for e in range(2):
                    sp.wait_ge(S("gate_done"), (i * 2 + e - 1) * NG)
                    sp.dma_start(wgate[:, e], A["w_gates"][bass.ds(i * 2 + e, 1)].rearrange("o p k c -> p (o k) c"))\
                        .then_inc(S(f"wgate_in{e}"), 16)
            so = O["conv_sample"].rearrange("(s t) c -> s t c", s=NS)
            sp.dma_start(so[:, 0:HIST - QS], A["state"].rearrange("(s t) c -> s t c", s=NS)[:, QS:HIST])\
                .then_inc(S("out_state"), 16)
            sp.wait_ge(S("uo_made"), 2)
            sp.dma_start(so[:, HIST - QS:HIST], uo).then_inc(S("out_state"), 16)
            sp.dma_start(O["conv_prompt"], ut[0:HIST]).then_inc(S("out_state"), 16)
            def skewed(h):
                flat = A["bias_scr"].rearrange("h q r -> (h q r)")
                at0 = h * P * RN + P - 1
                return flat[at0:at0 + P * (RN - 1)].rearrange("(q r) -> q r", r=RN - 1)

            sp.wait_ge(S("bias_out"), 16)
            sp.wait_ge(S("out_state"), 48)
            sp.wait_ge(S("c_made"), CT)
            for j in range(3):
                sp.wait_ge(S(f"v_out{j}"), 16 * NG)
            for e in range(2):
                sp.wait_ge(S(f"gate_out{e}"), 16 * KD)
            for t in range(NT):
                sp.dma_start(vN[:, t], O["v"][tok(t), :]).then_inc(S("vN_in"), 16)
            for h in range(H):
                sp.dma_start(near[:, h], skewed(h)[:, 0:2 * P]).then_inc(S("near_in"), 16)
            sp.wait_ge(S("biasS_zero"), 1)
            for h in range(H):
                r = slice(h * QS, (h + 1) * QS)
                sp.dma_start(biasS[r, PAST - P:PAST], skewed(h)[0:QS, 0:P]).then_inc(S("biasS_in"), 16)
                sp.dma_start(biasS[r, PAST:LS].rearrange("p (s q) -> p s q", s=NS),
                             skewed(h)[0:QS, P:P + QS].unsqueeze(1).to_broadcast([QS, NS, QS]))\
                    .then_inc(S("biasS_in"), 16)
            for st_ in range(NS):
                ck = A["cache_k"][st_].rearrange("(f k p) c -> f p k c", f=2, p=P)
                for f in range(2):
                    if st_ >= 1:
                        sp.wait_ge(S("kc_turned"), 8 * (st_ - 1) + 4 * f + 4)
                    sp.dma_start(kc[:, f], ck[f]).then_inc(S(f"kc_in{f}"), 16)
                if st_ >= 2:
                    sp.wait_ge(S("pvS_done"), st_ - 1)
                sp.dma_start(vc[:, st_ % 2], A["cache_v"][st_].rearrange("(k p) c -> p k c", p=P))\
                    .then_inc(S(f"vc_in{st_ % 2}"), 16)
                if st_ == 0:
                    sp.wait_ge(S("nb_made"), len(units))
                    sp.dma_start(msel, A["msel"]).then_inc(S("msel_in"), 16)
            sp.dma_start(gmix, A["norm_ffn_g"].partition_broadcast(P)).then_inc(S("gffn_in"), 16)
            sp.wait_ge(S("attn_made"), len(units) // 2 + 5 * NS)

            def merge_in(i, e):
                ct = i * 2 + e
                sp.dma_start(wab[:, e], A["w_ab"][bass.ds(ct, 1)].rearrange("o p k c -> p (o k) c"))\
                    .then_inc(S(f"wab_in{e}"), 16)
                for g in range(2):
                    sp.dma_start(gt[:, e, g], A["gate_scr"][bass.ds(ct + g * KD, 1)].rearrange("o p t -> p (o t)"))\
                        .then_inc(S(f"gt_in{e}{g}"), 16)

            for e in range(2):
                merge_in(0, e)
            sp.dma_start(wout, A["w_out"]).then_inc(S("wout_in"), 16)
            with sp.Fori(1, KD // 2) as i:
                for e in range(2):
                    sp.wait_ge(S("merged"), (i * 2 + e - 1) * NG)
                    merge_in(i, e)
            sp.wait_ge(S("merged"), KD * NG)

            def copy_m(i, first):
                for j in range(3):
                    if not first:
                        sp.wait_ge(S("wo_done"), i * 3 + j - 2)
                        sp.wait_ge(S("h2_turned"), i * 3 + j - 2)
                    sp.dma_start(hs2[:, j], mergedT[:, :, tok(i * 3 + j)]).then_inc(S(f"hs2_in{j}"), 16)
                    sp.dma_start(xs[:, j], A["x"][tok(i * 3 + j), :]).then_inc(S(f"xs_in{j}"), 16)

            copy_m(0, True)
            with sp.Fori(1, NG) as i:
                copy_m(i, False)
            sp.wait_ge(S("wo_done"), NT)
            sp.wait_ge(S("h2_turned"), NT)

            def w_tile(ct):
                return A["w_ffn"][bass.ds(ct, 1)].rearrange("o p n -> p (o n)")

            def gu_in(ct, e):
                sp.dma_start(wraw[:, e], w_tile(ct)[:, 0:2 * D]).then_inc(S(f"wgu_in{e}"), 16)

            def pair_in(g, i, first=False):
                for e in range(2):
                    u = g * FT + i * 2 + e
                    if not (first and e == 0):
                        sp.wait_ge(S("wgu_split"), u)
                    gu_in(i * 2 + e + 1, 1 - e)
                    if not first:
                        sp.wait_ge(S("down_done"), u - 1)
                    sp.dma_start(wdraw[:, e], w_tile(i * 2 + e)[:, 2 * D:3 * D]).then_inc(S(f"wd_in{e}"), 16)

            def y_out(g):
                for tt in range(3):
                    sp.wait_ge(S("y_made"), g * 6 + tt * 2 + 2)
                    sp.dma_start(O["y"][tok(g * 3 + tt), :], ys[:, tt]).then_inc(S(f"y_out{tt}"), 16)

            gu_in(0, 0)
            pair_in(0, 0, True)
            with sp.Fori(1, FT // 2) as i:
                pair_in(0, i)
            with sp.Fori(1, NG) as g:
                pair_in(g, 0)
                y_out(g - 1)
                with sp.Fori(1, FT // 2) as i:
                    pair_in(g, i)
            y_out(NG - 1)
            sp.wait_ge(S("wgu_in0"), 16 * (NG * FT // 2 + 1))
            sp.wait_ge(S("ik_out"), 16)
            for j in range(3):
                sp.wait_ge(S(f"k_out{j}"), 16 * NG)
                sp.wait_ge(S(f"y_out{j}"), 16 * NG)

        @block.tensor
        def _(pe):
            mm = nc.tensor.matmul

            def mm3(dst, whi, wlo, xhi, xlo, start, stop):
                mm(dst, whi, xhi, start=start, stop=False)
                mm(dst, whi, xlo, start=False, stop=False)
                return mm(dst, wlo, xhi, start=False, stop=stop)

            pe.wait_ge(S("const_in"), 16 * NCONST)
            mm(bank(7, RN)[0:H], relb[0:NB], onehot[0:NB]).then_inc(S("bias_done"), 1)

            def norm_group(i, first):
                for j in range(3):
                    pe.wait_ge(S("h_made"), i * 3 + j + 1)
                    if not first:
                        pe.wait_ge(S("hT_made"), (i * 3 + j - 2) * 2)
                    for k in range(KD):
                        l = nc.tensor.transpose(bank(2 * j, w=2)[:, k * P:(k + 1) * P], hb[:, j, k * P:(k + 1) * P],
                                                ident)
                    l.then_inc(S("h_turned"), 1)
                pe.wait_ge(S("hT_made"), (i * 3 + 3) * 2)
                for c in range(HP + 1):
                    if not (first and c < 2):
                        pe.wait_ge(S("iq_made"), i * (HP + 1) + c - 1)
                    for k in range(KD):
                        if c < HP:
                            w, dst = wiq[:, k, c * P:(c + 1) * P], bank(6 + c % 2, G)
                        else:
                            w, dst = wikw[:, k, :], bank(6 + c % 2, G)[0:72]
                        l = mm(dst, w, hT[:, k, tok(i, G)], start=k == 0, stop=k == KD - 1)
                    l.then_inc(S("iq_done"), 1)

            norm_group(0, True)
            with pe.Fori(1, NG) as i:
                pe.wait_ge(S("iq_made"), i * (HP + 1))
                norm_group(i, False)
            pe.wait_ge(S("hT_made"), 2 * NT)
            for c in range(2):
                for j in range(CT):
                    l = nc.tensor.transpose(bank(c)[:, j * P:j * P + 120], st[0:120, c, j * P:(j + 1) * P],
                                            ident[0:120, 0:120])
            l.then_inc(S("state_turned"), 1)
            pe.wait_ge(S("iq_made"), NG * (HP + 1))
            for t in range(NT):
                l = nc.tensor.transpose(bank(2 + t // 5)[:, (t % 5) * 72:(t % 5) * 72 + 72],
                                        ikwT[0:72, tok(t)], ident[0:72, 0:72])
            l.then_inc(S("ikw_turned"), 1)

            def turn_ikc(st_):
                if st_ == 0:
                    pe.wait_ge(S("ikc_in"), 16)
                    pe.wait_ge(S("state_made"), 2)
                else:
                    pe.wait_ge(S("ikcT_made"), 2 * st_)
                for k in range(8):
                    l = nc.tensor.transpose(bank(k // 4)[0:64, (k % 4) * P:(k % 4 + 1) * P], ikc[:, st_, k], ident)
                l.then_inc(S("ikc_turned"), 1)

            turn_ikc(0)
            pe.wait_ge(S("ikn_made"), 2)
            for t in range(NT):
                l = nc.tensor.transpose(bank(2, w=3)[:, t * P:(t + 1) * P], ikn[:, t], ident)
            l.then_inc(S("ikn_turned"), 1)
            pe.wait_ge(S("ikT_made"), 3)

            n = 0
            for b in range(2, PB):
                L = (b + 1) * P
                for h in range(H):
                    r = slice(64 * (h % 2), 64 * (h % 2) + 64)
                    if n >= 3:
                        pe.wait_ge(S("relu_done"), n - 2)
                    base = 2 + 2 * (n % 3)
                    for o0 in range(0, L, 512):
                        w = min(512, L - o0)
                        l = mm(bank(base, w=2)[:, o0:o0 + w], iqT[r, h // 2, tok(b)], ikT[r, o0:o0 + w])
                    l.then_inc(S("logit_done"), 1)
                    n += 1
            pe.wait_ge(S("relu_done"), n)
            pe.wait_ge(S("iqs_in"), 16 * H)
            pe.wait_ge(S("sw_made"), NS + 1)

            def sum_heads(st_):
                pe.wait_ge(S("relu_done"), n + st_ + 1)
                for o0, w in ((0, 512), (512, 512), (1024, 128)):
                    l = mm(bank(5, w=3)[:, o0:o0 + w], SW[:, st_], rl[:, st_ % 2, o0:o0 + w],
                           start=st_ == 0, stop=st_ == NS - 1)
                l.then_inc(S("heads_summed"), 1)

            for st_ in range(NS):
                pe.wait_ge(S("ikcT_made"), 2 * st_ + 2)
                if st_:
                    pe.wait_ge(S("relu_done"), n + st_)
                q = iqS[0:HD, st_]
                for o0 in (0, 512):
                    mm(bank(2, w=3)[:, o0:o0 + 512], q, ikcT[0:HD, st_ % 2, o0:o0 + 512])
                mm(bank(4, P), q, ikT[0:HD, NP:NTOK]).then_inc(S("logit_done"), 1)
                if st_ + 1 < NS:
                    turn_ikc(st_ + 1)
                if st_:
                    sum_heads(st_ - 1)
            sum_heads(NS - 1)

            pe.wait_ge(S("score_done"), PB - 1)

            def glu(j, e, first):
                pe.wait_ge(S(f"wglu_in{e}"), (j // 2) * 16 + 16)
                for g, done, made, b0 in ((1, "glu_b_done", "sigb_made", 3), (0, "glu_a_done", "a_made", 0)):
                    for c in range(NG):
                        if not first:
                            pe.wait_ge(S(made), (j - 1) * NG + c + 1)
                        for k in range(KD):
                            l = mm(bank(b0 + c, G), wglu[:, e, g, k], hT[:, k, tok(c, G)],
                                   start=k == 0, stop=k == KD - 1)
                        l.then_inc(S(done), 1)

            for j in range(CT):
                glu(j, j % 2, j == 0)
            pe.wait_ge(S("us_made"), 1)
            for j in range(CT):
                nc.tensor.transpose(bank(6)[:, j * P:(j + 1) * P], us[:, j], ident)
            for j in range(CT):
                l = nc.tensor.transpose(bank(7)[0:HIST, j * P:(j + 1) * P], uT[:, j, NP:NP + HIST], ident)
            l.then_inc(S("u_turned"), 1)
            pe.wait_ge(S("sigb_made"), NG * CT)
            pe.wait_ge(S("a_made"), NG * CT)

            def turn(c, t, j, first):
                pe.wait_ge(S("qn_made"), c * NT + t + 1)
                if not first:
                    pe.wait_ge(S("turn_made"), c * NT + t - 2)
                for p in range(HP):
                    l = nc.tensor.transpose(bank(3 + j)[:, p * P:(p + 1) * P], qn[:, j, p * P:(p + 1) * P], ident)
                l.then_inc(S("qk_turned"), 1)

            def project(c, i, before):
                for j in range(3):
                    n = c * NT + i * 3 + j
                    pe.wait_ge(S(f"hs_in{j}"), (c * NG + i + 1) * 16)
                    if not (c == 0 and before is None):
                        pe.wait_ge(S("qkv_evac"), n - 2)
                    for k in range(KD):
                        l = mm(bank(j), hs[:, j, k], wqkv[c % 2][:, k], start=k == 0, stop=k == KD - 1)
                    l.then_inc(S("qkv_done"), 1)
                    if j == 0 and before is not None:
                        bc, bt = before
                        if bc < 2:
                            turn(bc, bt, 2, bc == 0 and isinstance(bt, int) and bt < 3)
                    if j > 0 and c < 2:
                        turn(c, i * 3 + j - 1, j - 1, c == 0 and before is None)

            for c in range(3):
                pe.wait_ge(S(f"wqkv_in{c % 2}"), 16 * (c // 2 + 1))
                project(c, 0, None if c == 0 else (c - 1, NT - 1))
                if c == 0:
                    project(c, 1, (c, 2))
                    project(c, 2, (c, 5))
                else:
                    with pe.Fori(1, NG) as i:
                        project(c, i, (c, i * 3 - 1))

            def gate(i, first):
                for e in range(2):
                    pe.wait_ge(S(f"wgate_in{e}"), i * 16 + 16)
                    for c in range(NG):
                        if not first:
                            pe.wait_ge(S("gate_made"), (i * 2 + e - 2) * NG + c + 1)
                        for k in range(KD):
                            l = mm(bank(3 * e + c, G), wgate[:, e, k], hT[:, k, tok(c, G)],
                                   start=k == 0, stop=k == KD - 1)
                        l.then_inc(S("gate_done"), 1)

            pe.wait_ge(S("qkv_evac"), 3 * NT)
            pe.wait_ge(S("turn_made"), 2 * NT)
            gate(0, True)
            with pe.Fori(1, KD) as i:
                gate(i, False)
            pe.wait_ge(S("gate_made"), 2 * KD * NG)
            pe.wait_ge(S("conv_made"), CT)
            for c in range(NG):
                for j in range(CT):
                    l = mm(bank(c, G), ones, cT[:, j, tok(c, G)], start=j == 0, stop=j == CT - 1)
                l.then_inc(S("csum_done"), 1)
            for c in range(NG):
                pe.wait_ge(S("sq_made"), c + 1)
                for j in range(CT):
                    l = mm(bank(3 + c, G), ones, sqc[:, j, tok(c, G)], start=j == 0, stop=j == CT - 1)
                l.then_inc(S("sqsum_done"), 1)

            pe.wait_ge(S("c_made"), CT)
            pe.wait_ge(S("vN_in"), 16 * NT)
            N = len(units)

            def rows(h):
                return slice(64 * (h % 2), 64 * (h % 2) + 64)

            def logits(n):
                b, h = units[n]
                L = (b + 1) * P
                if n >= 2:
                    pe.wait_ge(S("biased"), n - 1)
                for o0 in range(0, L, 512):
                    w = min(512, L - o0)
                    l = mm(bank(2 * (n % 2), w=2)[:, o0:o0 + w], qT[rows(h), h // 2, tok(b)],
                           kT[rows(h), h // 2, o0:o0 + w])
                l.then_inc(S("qk_done"), 1)

            def turn_p(n):
                pe.wait_ge(S("p_made"), n + 1)
                if n:
                    pe.wait_ge(S("pT_made"), n)
                for k in range(units[n][0] + 1):
                    l = nc.tensor.transpose(bank(4, w=2)[:, tok(k)], lp[:, n % 2, tok(k)], ident)
                l.then_inc(S("p_turned"), 1)

            def weighted(n):
                b, h = units[n]
                pe.wait_ge(S("pT_made"), n + 1)
                if h % 2 == 0 and n >= 4:
                    pe.wait_ge(S("attn_made"), n // 2 - 1)
                for k in range(b + 1):
                    l = mm(bank(6 + (n // 2) % 2)[rows(h), 0:P], vN[:, k, h * HD:(h + 1) * HD],
                           pT[:, n % 2, tok(k)], start=k == 0, stop=k == b)
                l.then_inc(S("pv_done"), 1)

            for n in range(N + 2):
                if n < N:
                    logits(n)
                if n >= 2:
                    weighted(n - 2)
                if 1 <= n <= N:
                    turn_p(n - 1)

            def turn_k(st_, ks):
                for k in ks:
                    m = 8 * st_ + k
                    pe.wait_ge(S(f"kc_in{k // 4}"), 16 * (st_ + 1))
                    if m >= 2:
                        pe.wait_ge(S(f"kcT_made{m % 2}"), m // 2)
                    for c in range(HP):
                        l = nc.tensor.transpose(bank(m % 2)[:, c * P:(c + 1) * P],
                                                kc[:, k // 4, k % 4, c * P:(c + 1) * P], ident)
                    l.then_inc(S("kc_turned"), 1)

            def logits_s(st_):
                for e in range(2):
                    pe.wait_ge(S(f"kcT_made{e}"), 4 * (st_ + 1))
                if st_ >= 1:
                    pe.wait_ge(S("biased"), N + st_)
                    pe.wait_ge(S("pT_made"), N + st_)
                for o0, w in ((0, 512), (512, 512), (PAST, P)):
                    dst = bank(2, w=3)[:, o0:o0 + w]
                    for c in range(HP):
                        keys = kcT[:, c, o0:o0 + w] if o0 < PAST else kT[:, c, NP:NTOK]
                        mm(dst, qbd[:, st_, c], keys, start=c == 0, stop=False)
                    l = mm(dst, msel[:, st_], scoreS[:, o0:o0 + w], start=False, stop=True)
                l.then_inc(S("qk_done"), 1)

            def turn_ps(st_):
                pe.wait_ge(S("p_made"), N + st_ + 1)
                pe.wait_ge(S("pT_made"), N + st_)
                for k in range(9):
                    dst = bank(5, w=2)[:, tok(k)] if k < 8 else bank(4)[:, P:2 * P]
                    l = nc.tensor.transpose(dst, lp[:, st_ % 2, tok(k)], ident)
                l.then_inc(S("p_turned"), 1)

            def weighted_s(st_):
                pe.wait_ge(S("pT_made"), N + st_ + 1)
                pe.wait_ge(S(f"vc_in{st_ % 2}"), 16 * (st_ // 2 + 1))
                pe.wait_ge(S("attn_made"), N // 2 + 5 * st_)
                for c in range(HP):
                    for k in range(9):
                        v = vc[:, st_ % 2, k] if k < 8 else vN[:, NT - 1]
                        l = mm(bank(7)[:, c * P:(c + 1) * P], v[:, c * P:(c + 1) * P], pT[:, st_ % 2, tok(k)],
                               start=k == 0, stop=k == 8)
                l.then_inc(S("pvS_done"), 1)

            pe.wait_ge(S("attn_made"), N // 2)
            pe.wait_ge(S("qbd_made"), H)
            pe.wait_ge(S("msel_in"), 16)
            for st_ in range(NS + 1):
                if st_ < NS:
                    turn_k(st_, range(4))
                if st_:
                    turn_ps(st_ - 1)
                if st_ < NS:
                    turn_k(st_, range(4, 8))
                if st_:
                    weighted_s(st_ - 1)
                if st_ < NS:
                    logits_s(st_)

            pe.wait_ge(S("attn_made"), N // 2 + 5 * NS)

            def branches(i, first):
                for e in range(2):
                    pe.wait_ge(S(f"wab_in{e}"), i * 16 + 16)
                    for c in range(NG):
                        if not (first and e == 0):
                            pe.wait_ge(S("merged"), (i * 2 + e - 1) * NG + c + 1)
                        for g, src in ((0, attnT), (1, cT)):
                            for k in range(HP):
                                l = mm(bank(3 * g + c, G), wab[:, e, 4 * g + k], src[:, k, tok(c, G)],
                                       start=k == 0, stop=k == HP - 1)
                        l.then_inc(S("ab_done"), 1)

            branches(0, True)
            with pe.Fori(1, KD // 2) as i:
                branches(i, False)

            def turn_h2(t, j, first):
                pe.wait_ge(S("h2_made"), t + 1)
                if not first:
                    pe.wait_ge(S("h2T_split"), t * 2)
                for k in range(KD):
                    l = nc.tensor.transpose(bank(6, w=2)[:, tok(k)], xs[:, j, k * P:(k + 1) * P], ident)
                l.then_inc(S("h2_turned"), 1)

            def out_tile(i, first):
                for j in range(3):
                    t = i * 3 + j
                    pe.wait_ge(S(f"hs2_in{j}"), i * 16 + 16)
                    if not first:
                        pe.wait_ge(S("x1_made"), (t - 2) * 2)
                    for f in range(2):
                        for k in range(KD):
                            l = mm(bank(2 * j + f), hs2[:, j, k], wout[:, k, 512 * f:512 * f + 512],
                                   start=k == 0, stop=k == KD - 1)
                    l.then_inc(S("wo_done"), 1)
                    if not (first and j == 0):
                        turn_h2(t - 1, (j + 2) % 3, first and j == 1)

            pe.wait_ge(S("wout_in"), 16)
            pe.wait_ge(S("merged"), KD * NG)
            out_tile(0, True)
            with pe.Fori(1, NG) as i:
                out_tile(i, False)
            turn_h2(NT - 1, 2, False)

            def gate_up(g, ct, e):
                pe.wait_ge(S("wgu_split"), g * FT + ct + 1)
                for f, made, done in ((0, "silu_made", "g_done"), (1, "f_made", "u_done")):
                    if not (isinstance(ct, int) and ct == 0):
                        pe.wait_ge(S(made), g * FT + ct)
                    for k in range(KD):
                        c = slice((8 * f + k) * P, (8 * f + k + 1) * P)
                        l = mm3(bank(6 + f, G), wguhi[:, e, c], wgulo[:, e, c], h2hi[:, k, tok(g, G)],
                                h2lo[:, k, tok(g, G)], k == 0, k == KD - 1)
                    l.then_inc(S(done), 1)

            def down(g, ct, e, first=False, last=False):
                pe.wait_ge(S("wd_split"), g * FT + ct + 1)
                pe.wait_ge(S("f_split"), g * FT + ct + 1)
                if first and not (isinstance(g, int) and g == 0):
                    pe.wait_ge(S("y_made"), g * 6)
                for tt in range(3):
                    for f in range(2):
                        c = slice(512 * f, 512 * f + 512)
                        l = mm3(bank(2 * tt + f), fhi[:, e, tok(tt)], flo[:, e, tok(tt)], wdhi[:, e, c], wdlo[:, e, c],
                                first, last)
                l.then_inc(S("down_done"), 1)

            pe.wait_ge(S("h2T_split"), 2 * NT)
            pe.wait_ge(S("x1_made"), 2 * NT)
            def group(g):
                gate_up(g, 0, 0)
                gate_up(g, 1, 1)
                down(g, 0, 0, first=True)
                with pe.Fori(1, FT // 2) as i:
                    gate_up(g, i * 2, 0)
                    down(g, i * 2 - 1, 1)
                    gate_up(g, i * 2 + 1, 1)
                    down(g, i * 2, 0)
                down(g, FT - 1, 1, last=True)

            group(0)
            with pe.Fori(1, NG) as g:
                group(g)

        @block.scalar
        def _(act):
            ac = nc.scalar.activation

            def norm_group(i, first):
                for j in range(3):
                    act.wait_ge(S(f"x_in{j}"), i * 16 + 16)
                    if not first:
                        act.wait_ge(S("h_turned"), i * 3 + j - 2)
                    ac(hb[:, j], xb[:, j], ACT.Square, accum_out=ss[:, j:j + 1]).then_inc(S("ss_made"), 1)
                for j in range(3):
                    act.wait_ge(S("h_turned"), i * 3 + j + 1)
                    for c in range(2):
                        ac(hT[:, 4 * c:4 * c + 4, tok(i * 3 + j)], bank(2 * j + c).rearrange("p (k t) -> p k t", k=4),
                           ACT.Copy).then_inc(S("hT_made"), 1)
                for c in range(HP + 1):
                    act.wait_ge(S("iq_done"), i * (HP + 1) + c + 1)
                    if c < HP:
                        l = ac(iqT[:, c, tok(i, G)], bank(6 + c % 2, G), ACT.Copy)
                    else:
                        l = ac(ikwT[0:72, tok(i, G)], bank(6 + c % 2, G)[0:72], ACT.Copy)
                    l.then_inc(S("iq_made"), 1)

            norm_group(0, True)
            with act.Fori(1, NG) as i:
                norm_group(i, False)
            act.wait_ge(S("state_turned"), 1)
            for c in range(2):
                ac(uT[:, :, UP:].rearrange("p j (s t) -> p j s t", s=NS)[:, :, 4 * c:4 * c + 4, 0:HIST],
                   bank(c).rearrange("p (j t) -> p j t", j=CT)[:, :, 0:120].rearrange("p j (s t) -> p j s t", s=4),
                   ACT.Copy).then_inc(S("state_made"), 1)
            act.wait_ge(S("ikw_turned"), 1)
            ac(ikwN[:, 0:5], bank(2, 360).rearrange("p (t c) -> p t c", c=72), ACT.Copy).then_inc(S("ikwN_made"), 1)
            ac(ikwN[:, 5:9], bank(3, 288).rearrange("p (t c) -> p t c", c=72), ACT.Copy).then_inc(S("ikwN_made"), 1)

            def ikc_evac(st_):
                act.wait_ge(S("ikc_turned"), st_ + 1)
                if st_ >= 2:
                    act.wait_ge(S("logit_done"), NLOG + st_ - 1)
                for c in range(2):
                    ac(ikcT[0:64, st_ % 2, 512 * c:512 * c + 512], bank(c)[0:64], ACT.Copy)\
                        .then_inc(S("ikcT_made"), 1)

            NLOG = 6 * H
            ikc_evac(0)
            act.wait_ge(S("ikn_turned"), 1)
            for c in range(3):
                w = min(512, NTOK - 512 * c)
                ac(ikT[:, 512 * c:512 * c + w], bank(2 + c, w), ACT.Copy).then_inc(S("ikT_made"), 1)
            n = 0
            for b in range(2, PB):
                for h in range(H):
                    act.wait_ge(S("logit_done"), n + 1)
                    if n >= 2:
                        act.wait_ge(S("term_added"), n - 1)
                    ac(rl[:, n % 2, 0:(b + 1) * P], bank(2 + 2 * (n % 3), w=2)[:, 0:(b + 1) * P], ACT.Relu)\
                        .then_inc(S("relu_done"), 1)
                    n += 1
            act.wait_ge(S("term_added"), n)
            for st_ in range(NS):
                act.wait_ge(S("logit_done"), n + st_ + 1)
                if st_ >= 2:
                    act.wait_ge(S("heads_summed"), st_ - 1)
                ac(rl[:, st_ % 2], bank(2, w=3, n=128), ACT.Relu).then_inc(S("relu_done"), 1)
                if st_ + 1 < NS:
                    ikc_evac(st_ + 1)

            act.wait_ge(S("bias_out"), 16)
            for j in range(CT):
                if j:
                    act.wait_ge(S("u_made"), 2 * j)
                else:
                    act.wait_ge(S("ikn_turned"), 1)
                for c in range(NG):
                    act.wait_ge(S("glu_b_done"), j * NG + c + 1)
                    ac(sigb[:, c], bank(3 + c, G), ACT.Sigmoid).then_inc(S("sigb_made"), 1)
                for c in range(NG):
                    act.wait_ge(S("glu_a_done"), j * NG + c + 1)
                    ac(acopy[:, c], bank(c, G), ACT.Copy).then_inc(S("a_made"), 1)
            act.wait_ge(S("u_turned"), 1)
            ac(uo, bank(6), ACT.Copy).then_inc(S("uo_made"), 1)
            ac(ut[0:HIST], bank(7)[0:HIST], ACT.Copy).then_inc(S("uo_made"), 1)

            def turned(c, t, j):
                act.wait_ge(S("qk_turned"), c * NT + t + 1)
                if c == 0:
                    act.dma_start(O["k"][tok(t), :], qn[:, j]).then_inc(S(f"k_out{j}"), 16)
                ac((kT if c == 0 else qT)[:, :, tok(t)], bank(3 + j).rearrange("p (c t) -> p c t", c=HP), ACT.Copy)\
                    .then_inc(S("turn_made"), 1)

            def evac(c, i, before):
                for j in range(3):
                    n = c * NT + i * 3 + j
                    act.wait_ge(S("qkv_done"), n + 1)
                    if not (c == 0 and before is None):
                        if c < 2 or before[0] < 2:
                            act.wait_ge(S("qn_made"), n - 2)
                        else:
                            act.wait_ge(S(f"v_out{j}"), i * 16)
                    l = ac(raw[:, j], bank(j), ACT.Copy)
                    if c < 2:
                        l.then_inc(S("raw_made"), 1)
                        act.wait_ge(S("raw_made"), n + 1)
                        for h in range(H):
                            l = ac(bank(j)[:, h * HD:(h + 1) * HD], bank(j)[:, h * HD:(h + 1) * HD], ACT.Square,
                                   accum_out=ssq[:, j * H + h:j * H + h + 1])
                    l.then_inc(S("qkv_evac"), 1)
                    if c == 2:
                        act.wait_ge(S("qkv_evac"), n + 1)
                        act.dma_start(O["v"][tok(i * 3 + j), :], raw[:, j]).then_inc(S(f"v_out{j}"), 16)
                    if j == 0 and before is not None and before[0] < 2:
                        turned(before[0], before[1], 2)
                    if j > 0 and c < 2:
                        turned(c, i * 3 + j - 1, j - 1)

            for c in range(3):
                evac(c, 0, None if c == 0 else (c - 1, NT - 1))
                with act.Fori(1, NG) as i:
                    evac(c, i, (c, i * 3 - 1))

            def gate(i, first):
                for e in range(2):
                    if not first:
                        act.wait_ge(S(f"gate_out{e}"), i * 16)
                    for c in range(NG):
                        act.wait_ge(S("gate_done"), (i * 2 + e) * NG + c + 1)
                        ac(gb[:, e, tok(c, G)], bank(3 * e + c, G), ACT.Sigmoid).then_inc(S("gate_made"), 1)
                    act.wait_ge(S("gate_made"), (i * 2 + e + 1) * NG)
                    act.dma_start(A["gate_scr"][bass.ds(i * 2 + e, 1)].rearrange("o p t -> p (o t)"), gb[:, e])\
                        .then_inc(S(f"gate_out{e}"), 16)

            gate(0, True)
            with act.Fori(1, KD) as i:
                gate(i, False)
            for j in range(3):
                act.wait_ge(S(f"v_out{j}"), 16 * NG)
            for c in range(NG):
                act.wait_ge(S("d_made"), CT * (c + 1))
                ac(sqc[:, :, tok(c, G)], cT[:, :, tok(c, G)], ACT.Square).then_inc(S("sq_made"), 1)
            for c in range(NG):
                act.wait_ge(S("sqsum_done"), c + 1)
                ac(acc[:, tok(c, G)], bank(3 + c, G), ACT.Sqrt, scale=1.0 / CH, bias=epsc).then_inc(S("std_made"), 1)
            for j in range(CT):
                act.wait_ge(S("dn_made"), j + 1)
                ac(cT[:, j], cT[:, j], ACT.Silu, scale=lng[:, j:j + 1], bias=lnb[:, j:j + 1]).then_inc(S("c_made"), 1)

            N = len(units)

            def exps(n, L):
                act.wait_ge(S("nmx_made"), n + 1)
                ac(lp[:, n % 2, 0:L], lp[:, n % 2, 0:L], ACT.Exp, bias=nmx[:, n % 2:n % 2 + 1],
                   accum_out=sm[:, n % 2:n % 2 + 1]).then_inc(S("exp_done"), 1)

            for e in range(2):
                act.wait_ge(S(f"gate_out{e}"), 16 * KD)
            for n in range(N + 2):
                if n < N:
                    exps(n, (units[n][0] + 1) * P)
                if n >= 2 and n % 2:
                    b, h = units[n - 2]
                    act.wait_ge(S("pv_done"), n - 1)
                    ac(attnT[:, h // 2, tok(b)], bank(6 + ((n - 2) // 2) % 2, P), ACT.Copy).then_inc(S("attn_made"), 1)
                if 1 <= n <= N:
                    L = (units[n - 1][0] + 1) * P
                    act.wait_ge(S("p_turned"), n)
                    if n >= 3:
                        act.wait_ge(S("pv_done"), n - 2)
                    ac(pT[:, (n - 1) % 2, 0:L], bank(4, w=2)[:, 0:L], ACT.Copy).then_inc(S("pT_made"), 1)

            def kct(st_, ks):
                for k in ks:
                    if k % 2 == 0:
                        if st_ == 0 and k == 0:
                            act.wait_ge(S("pv_done"), N)
                        if st_ and k == 0:
                            act.wait_ge(S("qk_done"), N + st_)
                        act.wait_ge(S("kc_turned"), 8 * st_ + k + 1)
                        ac(kcT[:, :, tok(k)], bank(0).rearrange("p (c t) -> p c t", c=HP), ACT.Copy)\
                            .then_inc(S("kcT_made0"), 1)

            for st_ in range(NS + 1):
                if st_ < NS:
                    kct(st_, range(4))
                if st_:
                    act.wait_ge(S("p_turned"), N + st_)
                    if st_ >= 3:
                        act.wait_ge(S("pvS_done"), st_ - 2)
                    ac(pT[:, (st_ - 1) % 2, 0:PAST], bank(5, w=2), ACT.Copy)
                    ac(pT[:, (st_ - 1) % 2, PAST:LS], bank(4)[:, P:2 * P], ACT.Copy).then_inc(S("pT_made"), 1)
                if st_ < NS:
                    kct(st_, range(4, 8))
                    exps(N + st_, LS)

            def turned_h2(t):
                act.wait_ge(S("h2_turned"), t + 1)
                for f in range(2):
                    ac(h2hi[:, 4 * f:4 * f + 4, tok(t)], bank(6 + f).rearrange("p (k t) -> p k t", k=4), ACT.Copy)\
                        .then_inc(S("h2T_made"), 1)

            def squares(i, first):
                for j in range(3):
                    t = i * 3 + j
                    act.wait_ge(S("x1_made"), (t + 1) * 2)
                    ac(xs[:, j], x1[:, bass.ds(t, 1)].rearrange("p o d -> p (o d)"), ACT.Square,
                       accum_out=ss[:, j:j + 1]).then_inc(S("ss2_made"), 1)
                    if not (first and j == 0):
                        turned_h2(t - 1)

            squares(0, True)
            with act.Fori(1, NG) as i:
                squares(i, False)
            turned_h2(NT - 1)
            def gu_high(m, e):
                act.wait_ge(S(f"wgu_in{e}"), m * 16)
                ac(wguhi[:, e], wraw[:, e], ACT.Copy).then_inc(S("wgu_high"), 1)

            act.wait_ge(S("h2_turned"), NT)
            gu_high(1, 0)
            with act.Fori(0, NG) as g:
                with act.Fori(0, FT // 2) as i:
                    for e in range(2):
                        u = g * FT + i * 2 + e
                        act.wait_ge(S("g_done"), u + 1)
                        ac(sg[:, e], bank(6, G), ACT.Silu).then_inc(S("silu_made"), 1)
                        gu_high(g * (FT // 2) + i + 1 + e, 1 - e)
                        act.wait_ge(S("f_made"), u + 1)
                        ac(fhi[:, e], sg[:, e], ACT.Copy).then_inc(S("f_high"), 1)
                        act.wait_ge(S(f"wd_in{e}"), (g * (FT // 2) + i) * 16 + 16)
                        ac(wdhi[:, e], wdraw[:, e], ACT.Copy).then_inc(S("wd_high"), 1)

        @block.vector
        def _(dve):
            ve = nc.vector

            def low(lo, x, hi):
                return ve.tensor_tensor(lo, x, hi.bitcast(F32), ALU.subtract)

            ch = Chain(dve, S("dve_chain"))
            ve.memset(ones, 1.0).then_inc(S("ones_made"), 1)
            ve.memset(uT[:, :, 0:HIST], 0.0).then_inc(S("zeros_made"), 1)
            ch.add(ve.memset(SW, 0.0))
            dve.wait_ge(S("const_in"), 16 * NCONST)
            dve.wait_ge(S("bias_done"), 1)
            ch.link(ve.tensor_copy(bfar[0:H], bank(7, 1)[0:H]))
            ve.tensor_scalar(brow[0:H], bank(7, RN)[0:H], bfar[0:H], None, ALU.subtract).then_inc(S("brow_made"), 1)

            def norm_group(i):
                for j in range(3):
                    dve.wait_ge(S("rstd_made"), i * 3 + j + 1)
                    ve.scalar_tensor_tensor(hb[:, j], xb[:, j], rstd[:, j:j + 1], gmix, ALU.mult, ALU.mult)\
                        .then_inc(S("h_made"), 1)

            norm_group(0)
            with dve.Fori(1, NG) as i:
                norm_group(i)
            dve.wait_ge(S("ikwN_made"), 2)
            ve.tensor_scalar(iwN, ikwN[:, :, HD:72], ISC, None, ALU.mult).then_inc(S("iw_made"), 1)
            ch.link(ve.tensor_tensor(ikn[:, :, 0:HD], ikwN[:, :, 0:HD], ikwN[:, :, 0:HD], ALU.mult))
            ve.tensor_reduce(ssq[:, 0:NT], ikn[:, :, 0:HD], AX.X, ALU.add).then_inc(S("ssik_made"), 1)
            dve.wait_ge(S("rik_made"), 1)
            ch.link(ve.tensor_tensor(ikwN[:, :, 0:HD], ikwN[:, :, 0:HD],
                                     rsq[:, 0:NT].unsqueeze(2).to_broadcast([P, NT, HD]), ALU.mult))
            for c in range(2):
                ve.tensor_tensor(ikn[:, :, 64 * c:64 * c + 64], ikwN[:, :, 0:HD],
                                 ikg.unsqueeze(1).to_broadcast([P, NT, HD]), ALU.mult).then_inc(S("ikn_made"), 1)
            dve.wait_ge(S("iws_in"), 16 * H)
            ch.wait()
            for st_ in range(NS):
                ve.tensor_scalar(SW[:, st_, st_ * QS:(st_ + 1) * QS], delta, iwS[:, st_:st_ + 1], None, ALU.mult)\
                    .then_inc(S("sw_made"), 1)
            ve.memset(m8, 0.0).then_inc(S("sw_made"), 1)
            dve.wait_ge(S("iw_made"), 1)
            n = 0
            for b in range(2, PB):
                L = (b + 1) * P
                for h in range(H):
                    dve.wait_ge(S("relu_done"), n + 1)
                    r, w = rl[:, n % 2, 0:L], iwN[:, b, h:h + 1]
                    if h == 0:
                        l = ve.tensor_scalar(score[b], r, w, None, ALU.mult)
                    else:
                        dve.wait_ge(S("term_added"), n)
                        l = ve.scalar_tensor_tensor(score[b], r, w, score[b], ALU.mult, ALU.add)
                    l.then_inc(S("term_added"), 1)
                    n += 1
                dve.wait_ge(S("term_added"), n)
                ve.memset(score[b][0:CHUNK, L - CHUNK:L], NEG).then_inc(S("score_done"), 1)
            dve.wait_ge(S("heads_summed"), NS)
            ch.add(ve.tensor_copy(scoreS[:, 0:PAST], bank(5, w=2)))
            ve.tensor_tensor(scoreS[:, PAST:LS], bank(7, P), newneg, ALU.add).then_inc(S("score_done"), 1)
            dve.wait_ge(S("score_done"), PB - 1)
            ch.wait()
            for sc in [score[b] for b in range(2, PB)] + [scoreS]:
                for _ in range(TOPK // 8):
                    ch.link(ve.max(m8, sc))
                    ch.link(ve.match_replace(sc, m8, sc, TAKEN))
                ve.tensor_scalar(sc, sc, TAKEN, NEG, ALU.is_gt, ALU.mult).then_inc(S("mask_made"), 1)
            dve.wait_ge(S("u_turned"), 1)
            dve.wait_ge(S("u_made"), 2 * CT)
            for j in range(CT):
                ap = acc[:, 0:NP]
                as_ = acc[:, NP:NTOK].rearrange("p (s q) -> p s q", s=NS)
                for d in range(CK):
                    up, usamp, w = uT[:, j, d:d + NP], uSamp[:, j, :, d:d + QS], cw[:, j, d:d + 1]
                    if d == 0:
                        ch.add(ve.tensor_scalar(ap, up, w, cb[:, j:j + 1], ALU.mult, ALU.add))
                        ch.add(ve.tensor_scalar(as_, usamp, w, cb[:, j:j + 1], ALU.mult, ALU.add))
                    else:
                        ch.add(ve.scalar_tensor_tensor(ap, up, w, ap, ALU.mult, ALU.add))
                        ch.add(ve.scalar_tensor_tensor(as_, usamp, w, as_, ALU.mult, ALU.add))
                    ch.wait()
                ve.tensor_copy(cT[:, j], acc).then_inc(S("conv_made"), 1)
                dve.wait_ge(S("conv_made"), j + 1)
            for c in range(NG):
                dve.wait_ge(S("csum_done"), c + 1)
                for j in range(CT):
                    ve.scalar_tensor_tensor(cT[:, j, tok(c, G)], bank(c, G), -1.0 / CH, cT[:, j, tok(c, G)],
                                            ALU.mult, ALU.add).then_inc(S("d_made"), 1)
            dve.wait_ge(S("std_made"), NG)
            ch.link(ve.reciprocal(acc, acc))
            for j in range(CT):
                dve.wait_ge(S("sq_made"), NG)
                ve.tensor_tensor(cT[:, j], cT[:, j], acc, ALU.mult).then_inc(S("dn_made"), 1)

            for e in range(2):
                dve.wait_ge(S(f"gate_out{e}"), 16 * KD)
            dve.wait_ge(S("c_made"), CT)
            ve.memset(biasS, 0.0).then_inc(S("biasS_zero"), 1)
            N = len(units)

            def normalize(n, L):
                e = n % 2
                dve.wait_ge(S("exp_done"), n + 1)
                ch.link(ve.reciprocal(rc[:, e:e + 1], sm[:, e:e + 1]))
                ve.tensor_scalar(lp[:, e, 0:L], lp[:, e, 0:L], rc[:, e:e + 1], None, ALU.mult)\
                    .then_inc(S("p_made"), 1)

            def bias_max(dst, src, add, e, start):
                return ve.tensor_tensor_reduce(dst, src, add, 1.0, start, ALU.add, ALU.max, mx[:, e:e + 1])

            def negate(n):
                dve.wait_ge(S("biased"), n + 1)
                ve.tensor_scalar(nmx[:, n % 2:n % 2 + 1], mx[:, n % 2:n % 2 + 1], -1.0, None, ALU.mult)\
                    .then_inc(S("nmx_made"), 1)

            for n in range(N + 1):
                if n:
                    normalize(n - 1, (units[n - 1][0] + 1) * P)
                if n < N:
                    b, h = units[n]
                    e, L = n % 2, (b + 1) * P
                    far = max(L - 2 * P, 0)
                    src = bank(2 * e, w=2)
                    dve.wait_ge(S("qk_done"), n + 1)
                    if n >= 2:
                        dve.wait_ge(S("p_turned"), n - 1)
                        dve.wait_ge(S("nmx_made"), n - 1)
                    start = -3e38
                    if far:
                        ch.link(bias_max(lp[:, e, 0:far], src[:, 0:far], score[b][:, 0:far], 2 + e, -3e38))
                        start = mx[:, 2 + e:3 + e]
                    dve.wait_ge(S("nb_made"), n + 1)
                    bias_max(lp[:, e, far:L], src[:, far:L], nb[e][:, 2 * P - (L - far):2 * P], e, start)\
                        .then_inc(S("biased"), 1)
                    negate(n)
            dve.wait_ge(S("nb_made"), N)
            dve.wait_ge(S("p_turned"), N)
            ch.link(ve.memset(qbd, 0.0))
            for h in range(H):
                r = slice(64 * (h % 2), 64 * (h % 2) + 64)
                ve.tensor_copy(qbd[r, :, h // 2, h * QS:(h + 1) * QS],
                               qT[r, h // 2, NP:NTOK].rearrange("p (s q) -> p s q", s=NS)).then_inc(S("qbd_made"), 1)
            dve.wait_ge(S("biasS_in"), 16 * 2 * H)

            def kct(st_, ks):
                for k in ks:
                    if k % 2:
                        if k == 1:
                            if st_:
                                dve.wait_ge(S("qk_done"), N + st_)
                            else:
                                dve.wait_ge(S("pv_done"), N)
                        dve.wait_ge(S("kc_turned"), 8 * st_ + k + 1)
                        ve.tensor_copy(kcT[:, :, tok(k)], bank(1).rearrange("p (c t) -> p c t", c=HP))\
                            .then_inc(S("kcT_made1"), 1)

            def outputs(st_):
                dve.wait_ge(S("pvS_done"), st_ + 1)
                for par in range(2):
                    r = slice(64 * par, 64 * par + 64)
                    t = slice(NP + st_ * QS, NP + (st_ + 1) * QS)
                    o = bank(7)[r, QS * par:QS * par + 480].rearrange("p (c x) -> p c x", x=160)
                    ve.tensor_copy(attnT[r, 0:3, t], o[:, :, 0:QS]).then_inc(S("attn_made"), 1)
                    ve.tensor_copy(attnT[r, 3, t], bank(7)[r, 480 + QS * par:496 + QS * par])\
                        .then_inc(S("attn_made"), 1)
                ve.memset(m8, 0.0).then_inc(S("attn_made"), 1)

            for st_ in range(NS + 1):
                n = N + st_
                if st_:
                    normalize(n - 1, LS)
                if st_ < NS:
                    kct(st_, range(8))
                if st_:
                    outputs(st_ - 1)
                if st_ < NS:
                    dve.wait_ge(S("qk_done"), n + 1)
                    dve.wait_ge(S("p_turned"), n - 1)
                    bias_max(lp[:, n % 2], bank(2, w=3, n=P), biasS, n % 2, -3e38).then_inc(S("biased"), 1)
                    negate(n)

            def gated(i, first):
                for e in range(2):
                    for g in range(2):
                        dve.wait_ge(S(f"gt_in{e}{g}"), i * 16 + 16)
                    for c in range(NG):
                        m = (i * 2 + e) * NG + c
                        q = (e * NG + c) % 2
                        dve.wait_ge(S("ab_done"), m + 1)
                        if not (first and e == 0 and c < 2):
                            dve.wait_ge(S("merged"), m - 1)
                        for g in range(2):
                            ve.tensor_tensor(part[:, q, g], bank(3 * g + c, G), gt[:, e, g, tok(c, G)], ALU.mult)\
                                .then_inc(S("parts"), 1)
                        dve.wait_ge(S("parts"), m * 2 + 2)
                        ve.tensor_tensor(mergedT[:, bass.ds(i * 2 + e, 1), tok(c, G)], part[:, q, 0:1],
                                         part[:, q, 1:2], ALU.add).then_inc(S("merged"), 1)

            gated(0, True)
            with dve.Fori(1, KD // 2) as i:
                gated(i, False)

            dve.wait_ge(S("gffn_in"), 16)

            def normed(t, j):
                dve.wait_ge(S("rstd2_made"), t + 1)
                ve.scalar_tensor_tensor(xs[:, j], x1[:, bass.ds(t, 1)].rearrange("p o d -> p (o d)"),
                                        rstd[:, j:j + 1], gmix, ALU.mult, ALU.mult).then_inc(S("h2_made"), 1)

            def h2_low(t):
                dve.wait_ge(S("h2T_made"), t * 2 + 2)
                for f in range(2):
                    low(h2lo[:, 4 * f:4 * f + 4, tok(t)], bank(6 + f).rearrange("p (k t) -> p k t", k=4),
                        h2hi[:, 4 * f:4 * f + 4, tok(t)]).then_inc(S("h2T_split"), 1)

            def residual(i, first):
                for j in range(3):
                    t = i * 3 + j
                    dve.wait_ge(S("wo_done"), t + 1)
                    dve.wait_ge(S(f"xs_in{j}"), i * 16 + 16)
                    for f in range(2):
                        r = slice(512 * f, 512 * f + 512)
                        ve.tensor_tensor(x1[:, bass.ds(t, 1), r], bank(2 * j + f).unsqueeze(1),
                                         xs[:, j:j + 1, r], ALU.add).then_inc(S("x1_made"), 1)
                    if not (first and j == 0):
                        h2_low(t - 1)
                    normed(t, j)

            residual(0, True)
            with dve.Fori(1, NG) as i:
                residual(i, False)
            h2_low(NT - 1)
            def gu_low(m, e):
                dve.wait_ge(S("wgu_high"), m)
                low(wgulo[:, e], wraw[:, e], wguhi[:, e]).then_inc(S("wgu_split"), 1)

            dve.wait_ge(S("wo_done"), NT)
            gu_low(1, 0)

            def hidden(g, first):
                with dve.Fori(0, FT // 2) as i:
                    for e in range(2):
                        u = g * FT + i * 2 + e
                        dve.wait_ge(S("u_done"), u + 1)
                        dve.wait_ge(S("silu_made"), u + 1)
                        ve.tensor_tensor(sg[:, e], sg[:, e], bank(7, G), ALU.mult).then_inc(S("f_made"), 1)
                        gu_low(u + 2, 1 - e)
                        dve.wait_ge(S("f_high"), u + 1)
                        low(flo[:, e], sg[:, e], fhi[:, e]).then_inc(S("f_split"), 1)
                        dve.wait_ge(S("wd_high"), u + 1)
                        low(wdlo[:, e], wdraw[:, e], wdhi[:, e]).then_inc(S("wd_split"), 1)
                dve.wait_ge(S("down_done"), (g + 1) * FT)
                for tt in range(3):
                    if not first:
                        dve.wait_ge(S(f"y_out{tt}"), g * 16)
                    for f in range(2):
                        r = slice(512 * f, 512 * f + 512)
                        ve.tensor_tensor(ys[:, tt:tt + 1, r], bank(2 * tt + f).unsqueeze(1),
                                         x1[:, bass.ds(g * 3 + tt, 1), r], ALU.add).then_inc(S("y_made"), 1)

            hidden(0, True)
            with dve.Fori(1, NG) as g:
                hidden(g, False)

        @block.gpsimd
        def _(pool):
            gp = nc.gpsimd
            ch = Chain(pool, S("pool_chain"))
            ch.add(gp.memset(mhalf, -0.5))
            ch.add(gp.memset(epsc, EPS))
            ch.add(gp.memset(eps8, EPS))
            ch.add(gp.memset(per_d, 1.0 / D))
            ch.add(gp.memset(per_hd, 1.0 / HD))
            ch.wait()
            pool.wait_ge(S("const_in"), 16 * NCONST)
            ch.link(gp.tensor_scalar(qg, qg, HD ** -0.5, 0.0, ALU.mult, ALU.add))

            def norm_group(i):
                for j in range(3):
                    pool.wait_ge(S("ss_made"), i * 3 + j + 1)
                    ch.link(gp.tensor_tensor(ms[:, j:j + 1], ss[:, j:j + 1], per_d, ALU.mult))
                    ch.link(gp.tensor_tensor(ms[:, j:j + 1], ms[:, j:j + 1], epsc, ALU.add))
                    gp.tensor_tensor(rstd[:, j:j + 1], ms[:, j:j + 1], mhalf[:, 0:1], ALU.pow)\
                        .then_inc(S("rstd_made"), 1)

            norm_group(0)
            with pool.Fori(1, NG) as i:
                ch.loop(i - 1, 6)
                norm_group(i)
            ch.done(NG - 1)
            pool.wait_ge(S("ssik_made"), 1)
            ch.link(gp.tensor_scalar(msq[:, 0:NT], ssq[:, 0:NT], 1.0 / HD, EPS, ALU.mult, ALU.add))
            gp.tensor_tensor(rsq[:, 0:NT], msq[:, 0:NT], mhalf[:, 0:NT], ALU.pow).then_inc(S("rik_made"), 1)
            pool.wait_ge(S("state_made"), 2)
            for j in range(CT):
                pool.wait_ge(S("a_made"), NG * (j + 1))
                pool.wait_ge(S("sigb_made"), NG * (j + 1))
                a, b = (v.rearrange("p c t -> p (c t)") for v in (acopy, sigb))
                gp.tensor_tensor(uT[:, j, HIST:UP], a[:, 0:NP], b[:, 0:NP], ALU.mult).then_inc(S("u_made"), 1)
                gp.tensor_tensor(uSamp[:, j, :, HIST:US], a[:, NP:NTOK].rearrange("p (s q) -> p s q", s=NS),
                                 b[:, NP:NTOK].rearrange("p (s q) -> p s q", s=NS), ALU.mult).then_inc(S("u_made"), 1)
            pool.wait_ge(S("u_made"), 2 * CT)
            for j in range(CT):
                l = gp.tensor_copy(us[:, j].rearrange("p (s q) -> p s q", s=NS), uSamp[:, j, :, HIST:US])
            l.then_inc(S("us_made"), 1)

            def qk_norm(c, i, first):
                for j in range(3):
                    n = c * NT + i * 3 + j
                    pool.wait_ge(S("qkv_evac"), n + 1)
                    if c < 2:
                        q3 = raw[:, j].rearrange("p (h d) -> p h d", h=H)
                        r = slice(j * H, (j + 1) * H)
                        ch.link(gp.tensor_tensor(msq[:, r], ssq[:, r], per_hd, ALU.mult))
                        ch.link(gp.tensor_tensor(msq[:, r], msq[:, r], eps8, ALU.add))
                        ch.link(gp.tensor_tensor(rsq[:, r], msq[:, r], mhalf[:, 0:H], ALU.pow))
                        ch.link(gp.tensor_tensor(q3, q3, rsq[:, r].unsqueeze(2).to_broadcast([P, H, HD]), ALU.mult))
                        if not (c == 0 and first):
                            pool.wait_ge(S("qk_turned"), n - 2)
                            if c == 0:
                                pool.wait_ge(S(f"k_out{j}"), i * 16)
                            else:
                                pool.wait_ge(S(f"k_out{j}"), NG * 16)
                        gp.tensor_tensor(qn[:, j], raw[:, j], kg if c == 0 else qg, ALU.mult).then_inc(S("qn_made"), 1)

            for c in range(2):
                qk_norm(c, 0, True)
                with pool.Fori(1, NG) as i:
                    ch.loop(i - 1, 12)
                    qk_norm(c, i, False)
                ch.done(NG - 1)
            pool.wait_ge(S("c_made"), CT)
            ch.link(gp.memset(mask0, 0.0))
            ch.link(gp.memset(mask0[0:CHUNK, 2 * P - CHUNK:2 * P], NEG))
            pool.wait_ge(S("near_in"), 16 * H)
            for n, (b, h) in enumerate(units):
                if n >= 2:
                    pool.wait_ge(S("biased"), n - 1)
                if b >= 2:
                    pool.wait_ge(S("mask_made"), b - 1)
                m = mask0 if b < 2 else score[b][:, (b - 1) * P:(b + 1) * P]
                gp.tensor_tensor(nb[n % 2], m, near[:, h], ALU.add).then_inc(S("nb_made"), 1)

            def norm2_group(i):
                for j in range(3):
                    pool.wait_ge(S("ss2_made"), i * 3 + j + 1)
                    ch.link(gp.tensor_tensor(ms[:, j:j + 1], ss[:, j:j + 1], per_d, ALU.mult))
                    ch.link(gp.tensor_tensor(ms[:, j:j + 1], ms[:, j:j + 1], epsc, ALU.add))
                    gp.tensor_tensor(rstd[:, j:j + 1], ms[:, j:j + 1], mhalf[:, 0:1], ALU.pow)\
                        .then_inc(S("rstd2_made"), 1)

            with pool.Fori(0, NG) as i:
                ch.loop(i, 6)
                norm2_group(i)
            ch.done(NG)


def layouts(i):
    w_in = i["w_in"][0]
    o_iq = 3 * AW
    cat = lambda *a: np.ascontiguousarray(np.concatenate(a, axis=0))
    con = np.ascontiguousarray
    k_first = lambda w: con(w.reshape(-1, P, w.shape[1]).transpose(1, 0, 2))
    cols = lambda w: con(w.reshape(-1, P, w.shape[1] // P, P).transpose(2, 1, 0, 3))
    o_ik = o_iq + IDXC
    o_glu = o_ik + HD + H
    out = {
        "x": cat(i["x_prompt"][0], i["x_sample"].reshape(-1, D)),
        "ident": np.eye(P, dtype=np.float32),
        "delta": con(np.tile(np.eye(QS, dtype=np.float32), (H, 1))),
        "newneg": np.where(np.kron(np.eye(NS), np.ones((QS, QS))) > 0, 0.0, NEG).astype(np.float32),
        "msel": con(np.einsum("ab,qr->aqbr", np.eye(NS), np.eye(QS))[:, :, :, None, :].repeat(H, 3)
                    .reshape(P, NS, P).astype(np.float32)),
        "onehot": bucket_rows(),
        "rel_bias": con(i["rel_bias"]),
        "cache_k": con(i["cache_k"][0].reshape(NS, PAST, AW)),
        "cache_v": con(i["cache_v"][0].reshape(NS, PAST, AW)),
        "norm_mix_g": con(i["norm_mix_g"][0]),
        "qg": con(np.tile(i["q_norm_g"][0], H)),
        "kg": con(np.tile(i["k_norm_g"][0], H)),
        "idx_k_norm_g": con(i["idx_k_norm_g"][0]),
        "w_iq": k_first(w_in[:, o_iq:o_ik]),
        "w_ikw": k_first(w_in[:, o_ik:o_glu]),
        "conv_w": con(i["conv_dw_w"][0, :, 0].T.reshape(CT, P, CK).transpose(1, 0, 2)),
        "conv_b": con(i["conv_dw_b"][0].reshape(CT, P).T),
        "conv_ln_g": con(i["conv_ln_g"][0].reshape(CT, P).T),
        "conv_ln_b": con(i["conv_ln_b"][0].reshape(CT, P).T),
        "w_glu": con(np.stack([cols(w_in[:, o_glu:o_glu + CH]), cols(w_in[:, o_glu + CH:o_glu + 2 * CH])], axis=2)),
        "w_qkv": con(np.stack([k_first(w_in[:, o:o + AW]) for o in (AW, 0, 2 * AW)])),
        "w_gates": cols(w_in[:, o_glu + 2 * CH:]),
        "w_ab": cols(cat(i["w_attn_out"][0], i["w_conv_out"][0])),
        "w_out": k_first(i["w_out"][0]),
        "norm_ffn_g": con(i["norm_ffn_g"][0]),
        "w_ffn": con(np.concatenate([cols(i["w_ffn_gate"][0]).reshape(FT, P, D), cols(i["w_ffn_up"][0]).reshape(FT, P, D),
                                     i["w_ffn_down"][0].reshape(FT, P, D)], axis=2)[list(range(FT)) + [0]]),
        "state": con(i["state_conv"][0].reshape(NS * HIST, CH)),
        "cache_ik": con(i["cache_idx_k"][0].reshape(NS, 8, P, HD).transpose(2, 0, 1, 3)),
    }
    return out


SCRATCH = {"iw_scr": (P, H), "gate_scr": (2 * KD, P, NTOK), "bias_scr": (H, P, RN)}
OUTS = {"y": (NTOK, D), "k": (NTOK, AW), "v": (NTOK, AW), "ik": (NTOK, HD),
        "conv_prompt": (HIST, CH), "conv_sample": (NS * HIST, CH)}


def kernel(**inputs):
    import concourse.bacc as bacc
    from concourse.bass_utils import run_bass_kernel_spmd

    nc = bacc.Bacc("TRN2", target_bir_lowering=False, num_devices=1)
    arrays = {f"in_{k}": v for k, v in layouts({k: np.asarray(v) for k, v in inputs.items()}).items()}
    A = {k[3:]: nc.dram_tensor(k, v.shape, mybir.dt.from_np(v.dtype), kind="ExternalInput").ap()
         for k, v in arrays.items()}
    A.update({k: nc.dram_tensor(k, sh, F32, kind="Internal").ap() for k, sh in SCRATCH.items()})
    O = {k: nc.dram_tensor(f"out_{k}", sh, F32, kind="ExternalOutput").ap() for k, sh in OUTS.items()}
    build(nc, A, O)
    r = run_bass_kernel_spmd(nc, [arrays], core_ids=[0]).results[0]
    y, k, v, ik, cp, cs = (r[f"out_{n}"] for n in ("y", "k", "v", "ik", "conv_prompt", "conv_sample"))
    return (y[:NP].reshape(1, NP, D), y[NP:].reshape(NS, QS, D),
            k[:NP].reshape(1, 1, NP, H, HD), v[:NP].reshape(1, 1, NP, H, HD), ik[:NP].reshape(1, 1, NP, HD),
            cp.reshape(1, 1, HIST, CH),
            k[NP:].reshape(1, NS, QS, H, HD), v[NP:].reshape(1, NS, QS, H, HD), ik[NP:].reshape(1, NS, QS, HD),
            cs.reshape(1, NS, HIST, CH))
```

```python
import math
from contextlib import ExitStack

import numpy as np
import concourse.bass as bass
from concourse import mybir

F32 = mybir.dt.float32
F32R = mybir.dt.float32r
ALU = mybir.AluOpType
ACT = mybir.ActivationFunctionType
AX = mybir.AxisListType

P = 128
D = 1024
NP = 1024
NS, QS = 8, 16
PAST = 1024
NTOK = NP + NS * QS
NT = NTOK // P
PB = NP // P
G = 384
NG = NTOK // G
H, HD = 8, 64
HP = H // 2
AW = H * HD
CH = 512
CT = CH // P
CK = 31
HIST = CK - 1
FF = -(-8 * D // (3 * 256)) * 256
FT = FF // P
KD = D // P
TOPK = 256
CHUNK = 64
NB = 32
EPS = 1e-6
NEG = -1e30
TAKEN = -3e38
LS = PAST + NS * QS
RMIN = -(2 * P - 1)
RN = 3 * P
IDXC = H * HD
ISC = (HD ** -0.5) * (H ** -0.5)
UP = HIST + NP
US = HIST + QS
UW = UP + NS * US


SLAB = 53184


def bucket_rows():
    rel = np.arange(RMIN, RMIN + RN)
    n = np.abs(rel)
    nf = np.maximum(n, 1).astype(np.float32)
    large = 8 + (np.log(nf / np.float32(8)) / np.float32(math.log(16)) * np.float32(8)).astype(np.int32)
    b = np.where(rel > 0, 16, 0) + np.where(n < 8, n, np.minimum(large, 15))
    return (b[None, :] == np.arange(NB)[:, None]).astype(np.float32)


class Chain:

    def __init__(self, eng, sem):
        self.eng, self.sem, self.n, self.base, self.i, self.per = eng, sem, 0, 0, None, 0

    def add(self, ins):
        ins.then_inc(self.sem, 1)
        self.n += 1

    def loop(self, i, per):
        self.base, self.n, self.i, self.per = self.base + self.n, 0, i, per

    def done(self, trips):
        assert self.n == self.per, (self.n, self.per)
        self.base, self.n, self.i = self.base + trips * self.per, 0, None

    def wait(self):
        at = self.base + self.n
        self.eng.wait_ge(self.sem, at if self.i is None else self.i * self.per + at)

    def link(self, ins):
        self.add(ins)
        self.wait()


def build(nc, A, O):
    with ExitStack() as ctx:
        sbuf0 = -(-nc.sbuf_base // 32) * 32
        ps = ctx.enter_context(nc.psum_tensor("ps", [P, 8 * 512], F32))

        def sem(name):
            return ctx.enter_context(nc.semaphore(name))

        at = [0]
        bufs = [0]

        def take(n, off=None):
            if off is None:
                off = at[0]
                at[0] += n
            return place(n, off, F32)

        def take_r(n, off):
            return place(n, off, F32R)

        def place(n, off, dtype):
            assert off + n <= SLAB
            bufs[0] += 1
            return nc.alloc_sbuf_tensor_at(f"buf{bufs[0]}", [P, n], dtype, offset=sbuf0 + 4 * off)[:]

        def bank(b, n=512, w=1):
            return ps[:, 512 * b:512 * (b + w - 1) + n]

        ident = take(P)
        ones = take(P)
        gmix = take(D)
        qg, kg = take(AW), take(AW)
        ikg = take(HD)
        small = take(400)
        iwN = take(NT * H).rearrange("p (t h) -> p t h", t=NT)
        delta = take(QS)
        newneg = take(P)
        mhalf = small[:, 0:16]
        ss = small[:, 16:32]
        ms = small[:, 32:48]
        rstd = small[:, 48:64]
        iwS = small[:, 64:72]
        cw = small[:, 72:72 + CT * CK].rearrange("p (j k) -> p j k", j=CT)
        cb = small[:, 196:200]
        lng = small[:, 200:204]
        lnb = small[:, 204:208]
        mx = small[:, 208:224]
        nmx = small[:, 224:240]
        sm = small[:, 240:256]
        rc = small[:, 256:272]
        m8 = small[:, 272:280]
        epsc = small[:, 280:281]
        per_d = small[:, 281:282]
        eps8 = small[:, 384:392]
        per_hd = small[:, 392:400]
        ssq = small[:, 288:320]
        msq = small[:, 320:352]
        rsq = small[:, 352:384]
        o_h = at[0]
        hT = take(KD * NTOK).rearrange("p (k t) -> p k t", k=KD)
        o_q = at[0]
        qT = take(HP * NTOK).rearrange("p (c t) -> p c t", c=HP)
        o_k = at[0]
        kT = take(HP * NTOK).rearrange("p (c t) -> p c t", c=HP)
        score = {b: take((b + 1) * P) for b in range(2, PB)}
        scoreS = take(LS)
        uT = take(CT * UW).rearrange("p (j t) -> p j t", j=CT)
        o_w = at[0]

        iqT = take(HP * NTOK, o_q).rearrange("p (c t) -> p c t", c=HP)
        wiq = take(KD * IDXC, o_k).rearrange("p (k c) -> p k c", k=KD)
        xb = take(3 * D, o_w).rearrange("p (s d) -> p s d", s=3)
        hb = take(3 * D, o_w + 3 * D).rearrange("p (s d) -> p s d", s=3)
        o = o_w + 6 * D
        ikcT = take(4 * PAST, o).rearrange("p (s t) -> p s t", s=4)
        o += 6 * PAST
        ikT = take(NTOK, o)
        o += NTOK
        rl = take(2 * LS, o_w).rearrange("p (s t) -> p s t", s=2)
        ikwN = take(NT * 72, o_w + 3 * LS).rearrange("p (t c) -> p t c", t=NT)
        ikn = take(NT * P, o_w + 3 * LS + 648).rearrange("p (t c) -> p t c", t=NT)
        assert 4 * LS + 648 <= 6 * D
        iqS = take(H * P, o).rearrange("p (s h q) -> p s h q", s=NS, h=H)
        o += H * P
        wikw = take(KD * 72, o).rearrange("p (k c) -> p k c", k=KD)
        o += KD * 72
        SW = take(NS * P, o).rearrange("p (s t) -> p s t", s=NS)
        o += NS * P
        st = take(2 * CH, o).rearrange("p (s c) -> p s c", s=2)
        o += 2 * CH
        ikwT = take(NTOK, o)
        o += NTOK

        wglu = take(4 * KD * P, o_k).rearrange("p (s g k c) -> p s g k c", s=2, g=2, k=KD)
        wqkv = [take(KD * AW, o_w).rearrange("p (k c) -> p k c", k=KD),
                take(KD * AW, o_w + 6 * D).rearrange("p (k c) -> p k c", k=KD)]
        wgate = take(2 * KD * P, o_w + KD * AW).rearrange("p (s k c) -> p s k c", s=2, k=KD)
        gb = take(2 * NTOK, o_w + 6 * D).rearrange("p (s t) -> p s t", s=2)
        o = o_w + 6 * D + KD * AW
        sqc = take(CT * NTOK, o).rearrange("p (j t) -> p j t", j=CT)
        hs = take(3 * D, o).rearrange("p (s k t) -> p s k t", s=3, k=KD)
        raw = take(3 * AW, o + 3 * D).rearrange("p (s c) -> p s c", s=3)
        qn = take(3 * AW, o + 3 * D + 3 * AW).rearrange("p (s c) -> p s c", s=3)
        o = o_w + 17088
        assert o >= o_w + 6 * D + KD * AW + 3 * D + 6 * AW
        sigb = take(NTOK, o).rearrange("p (c t) -> p c t", c=NG)
        acc = take(NTOK, o)
        acc_pool = take(NTOK, o + NTOK)
        tap = take(NTOK, o + 2 * NTOK)
        acopy = take(NTOK, o + NTOK).rearrange("p (c t) -> p c t", c=NG)
        us = take(CT * P, o + NTOK).rearrange("p (j t) -> p j t", j=CT)
        uo = take(CH, o + NTOK + CH)
        ut = take(CH, o + NTOK + 2 * CH)
        uSamp = uT[:, :, UP:].rearrange("p j (s t) -> p j s t", s=NS)
        cT = uT[:, :, 0:NTOK]
        NLOG = (PB - 2) * H

        onehot = take(RN, o_w + 18240)
        relb = take(H, o_w + 18240 + RN)
        brow = take(RN, o_w + 18240 + RN + H)
        bfar = take(1, o_w + 18240 + 2 * RN + H)
        vN = take(NT * AW, o_h).rearrange("p (t c) -> p t c", t=NT)
        attnT = take(HP * NTOK, o_h + NT * AW).rearrange("p (c t) -> p c t", c=HP)
        lp = take(2 * LS, o_w).rearrange("p (s t) -> p s t", s=2)
        pT = take(2 * LS, o_w + 2 * LS).rearrange("p (s t) -> p s t", s=2)
        biasS = take(LS, o_w + 4 * LS)
        o = o_w + 5 * LS
        kcT = [take(HP * PAST, b).rearrange("p (c t) -> p c t", c=HP) for b in (o, o_h)]
        o += 8 * AW
        vc = take(2 * 8 * AW, o).rearrange("p (s k c) -> p s k c", s=2, k=8)
        o += 16 * AW
        lpP = [lp[:, 0], lp[:, 1], vc[:, 1].rearrange("p k c -> p (k c)")[:, 0:LS]]
        near = take(H * 2 * P, o + 2 * H * QS).rearrange("p (h j) -> p h j", h=H)
        maskS = take(2 * LS, o).rearrange("p (s t) -> p s t", s=2)
        nb = [uT[:, e, NTOK:NTOK + 2 * P] for e in range(2)]
        mask0 = uT[:, 2, NTOK:NTOK + 2 * P]
        o_s = o_k + HP * NTOK
        qbd = take(NS * HP * P, o_s).rearrange("p (s c m) -> p s c m", s=NS, c=HP)
        mergedT = take(KD * NTOK, o_q).rearrange("p (k t) -> p k t", k=KD)
        wab = take(2 * KD * P, o_w).rearrange("p (s k c) -> p s k c", s=2, k=KD)
        gt = take(4 * NTOK, o_w + 2 * KD * P).rearrange("p (s g t) -> p s g t", s=2, g=2)
        o = o_w + 2 * KD * P + 4 * NTOK
        part = take(2 * 2 * G, o).rearrange("p (s g t) -> p s g t", s=2, g=2)
        attnhi = take_r(HP * NTOK, o_h).rearrange("p (c t) -> p c t", c=HP)
        attnlo = take_r(HP * NTOK, o_h + NT * AW).rearrange("p (c t) -> p c t", c=HP)
        chi = take_r(CT * NTOK, o_s).rearrange("p (j t) -> p j t", j=CT)
        clo = take_r(CT * UW, o_w - CT * UW).rearrange("p (j t) -> p j t", j=CT)[:, :, 0:NTOK]
        wabhi = take_r(2 * KD * P, o + 4 * G).rearrange("p (s k c) -> p s k c", s=2, k=KD)
        wablo = take_r(2 * KD * P, o_w).rearrange("p (s k c) -> p s k c", s=2, k=KD)
        wout = take(KD * D, o + 4 * G + 2 * KD * P).rearrange("p (k c) -> p k c", k=KD)
        hs2 = take(3 * D, o_s).rearrange("p (s k t) -> p s k t", s=3, k=KD)
        xs = take(3 * D, o_s + PB * (PB + 1) // 2 * P - 3 * P + LS).rearrange("p (s d) -> p s d", s=3)
        x1 = take(NT * D, o_h).rearrange("p (t d) -> p t d", t=NT)
        h2hi = take_r(KD * NTOK, o_w).rearrange("p (k t) -> p k t", k=KD)
        h2lo = take_r(KD * NTOK, o_q).rearrange("p (k t) -> p k t", k=KD)
        o = o_s
        wraw = take(2 * 2 * D, o).rearrange("p (s n) -> p s n", s=2)
        wguhi = take_r(2 * 2 * D, o + 4 * D).rearrange("p (s n) -> p s n", s=2)
        sg = take(2 * G, o + 8 * D).rearrange("p (s t) -> p s t", s=2)
        fhi = take_r(2 * G, o + 8 * D + 2 * G).rearrange("p (s t) -> p s t", s=2)
        flo = take_r(2 * G, o + 8 * D + 4 * G).rearrange("p (s t) -> p s t", s=2)
        assert o + 8 * D + 6 * G <= o_w
        o = o_w + KD * NTOK
        wgulo = take_r(2 * 2 * D, o).rearrange("p (s n) -> p s n", s=2)
        wdraw = take(2 * D, o + 4 * D).rearrange("p (s n) -> p s n", s=2)
        wdlo = take_r(2 * D, o + 4 * D).rearrange("p (s n) -> p s n", s=2)
        wdhi = take_r(2 * D, o + 6 * D).rearrange("p (s n) -> p s n", s=2)
        ys = take(3 * D, o + 8 * D).rearrange("p (s d) -> p s d", s=3)
        units = [(b, h) for b in range(PB) for h in range(H)]

        s = {}

        def S(name):
            if name not in s:
                s[name] = sem(name)
            return s[name]

        block = ctx.enter_context(nc.Block())

        def tok(t, n=P):
            return bass.ds(t * n, n)

        NCONST = 15

        @block.sync
        def _(sp):
            def const(dst, src):
                sp.dma_start(dst, src).then_inc(S("const_in"), 16)

            sp.dma_start(ident, A["ident"]).then_inc(S("first_in"), 16)
            sp.dma_start(gmix, A["norm_mix_g"].partition_broadcast(P)).then_inc(S("first_in"), 16)
            for j in range(3):
                sp.dma_start(xb[:, j], A["x"][tok(j), :]).then_inc(S(f"x_in{j}"), 16)
            const(relb[0:NB], A["rel_bias"])
            const(onehot[0:NB], A["onehot"])
            const(wiq, A["w_iq"])
            const(wikw, A["w_ikw"])
            const(qg, A["qg"].partition_broadcast(P))
            const(kg, A["kg"].partition_broadcast(P))
            const(ikg, A["idx_k_norm_g"].partition_broadcast(P))
            const(delta, A["delta"])
            const(newneg, A["newneg"])
            const(cw, A["conv_w"])
            const(cb, A["conv_b"])
            const(lng, A["conv_ln_g"])
            const(lnb, A["conv_ln_b"])
            for c in range(2):
                const(st[0:120, c], A["state"][120 * c:120 * c + 120, :])
            with sp.Fori(1, NG) as i:
                for j in range(3):
                    sp.wait_ge(S("h_made"), i * 3 + j - 2)
                    sp.dma_start(xb[:, j], A["x"][tok(i * 3 + j), :]).then_inc(S(f"x_in{j}"), 16)
            for st_ in range(4):
                sp.dma_start(ikcT[0:HD, st_], A["cache_ik"][st_]).then_inc(S(f"ikc_in{st_}"), 16)

            sp.wait_ge(S("brow_made"), 1)
            sp.dma_start(A["bias_scr"], brow[0:H].unsqueeze(1).to_broadcast([H, P, RN])).then_inc(S("bias_out"), 16)

            sp.wait_ge(S("ikn_made"), 2)
            sp.dma_start(O["ik"].rearrange("(t p) d -> p t d", p=P), ikn[:, :, 0:HD]).then_inc(S("ik_out"), 16)
            sp.wait_ge(S("iw_made"), 1)
            sp.dma_start(A["iw_scr"], iwN[:, NT - 1]).then_inc(S("iw_out"), 16)
            sp.wait_ge(S("iw_out"), 16)
            for h in range(H):
                sp.dma_start(iwS[h * QS:(h + 1) * QS, :],
                             A["iw_scr"].rearrange("(s q) h -> h q s", q=QS)[h],
                             allow_slow_non_contiguous=True).then_inc(S("iws_in"), 16)
            sp.wait_ge(S("iq_made"), NG * (HP + 1))
            for h in range(H):
                sp.dma_start(iqS[0:HD, :, h], iqT[64 * (h % 2):64 * (h % 2) + 64, h // 2, NP:NTOK]
                             .rearrange("p (s q) -> p s q", s=NS)).then_inc(S("iqs_in"), 16)
            sp.wait_ge(S("iq_done"), NG * (HP + 1))
            for j in range(CT):
                if j >= 2:
                    sp.wait_ge(S("glu_a_done"), NG * (j - 1))
                sp.dma_start(wglu[:, j % 2], A["w_glu"][j]).then_inc(S(f"wglu_in{j % 2}"), 16)
                if j == 1:
                    for st_ in range(4, NS):
                        sp.wait_ge(S("logit_done"), NLOG + st_ - 3)
                        sp.dma_start(ikcT[0:HD, st_ - 4], A["cache_ik"][st_]).then_inc(S(f"ikc_in{st_ - 4}"), 16)
                    sp.wait_ge(S("score_done"), PB - 1)
                    for c in range(2):
                        sp.dma_start(wqkv[c], A["w_qkv"][c]).then_inc(S(f"wqkv_in{c}"), 16)

            def copy_h(c, i, first):
                for j in range(3):
                    if not first:
                        sp.wait_ge(S("qkv_done"), c * NT + i * 3 + j - 2)
                    sp.dma_start(hs[:, j], hT[:, :, tok(i * 3 + j)]).then_inc(S(f"hs_in{j}"), 16)

            for c in range(3):
                copy_h(c, 0, c == 0)
                if c == 0:
                    so = O["conv_sample"].rearrange("(s t) c -> s t c", s=NS)
                    sp.dma_start(so[:, 0:HIST - QS], A["state"].rearrange("(s t) c -> s t c", s=NS)[:, QS:HIST])\
                        .then_inc(S("out_state"), 16)
                    sp.wait_ge(S("uo_made"), 2)
                    sp.dma_start(so[:, HIST - QS:HIST], uo).then_inc(S("out_state"), 16)
                    sp.dma_start(O["conv_prompt"], ut[0:HIST]).then_inc(S("out_state"), 16)
                if c == 1:
                    sp.dma_start(wqkv[0], A["w_qkv"][2]).then_inc(S("wqkv_in0"), 16)
                if c == 2:
                    for e in range(2):
                        sp.dma_start(wgate[:, e], A["w_gates"][e]).then_inc(S(f"wgate_in{e}"), 16)
                with sp.Fori(1, NG) as i:
                    copy_h(c, i, False)
            with sp.Fori(1, KD) as i:
                for e in range(2):
                    sp.wait_ge(S("gate_done"), (i * 2 + e - 1) * NG)
                    sp.dma_start(wgate[:, e], A["w_gates"][bass.ds(i * 2 + e, 1)].rearrange("o p k c -> p (o k) c"))\
                        .then_inc(S(f"wgate_in{e}"), 16)
            def skewed(h):
                flat = A["bias_scr"].rearrange("h q r -> (h q r)")
                at0 = h * P * RN + P - 1
                return flat[at0:at0 + P * (RN - 1)].rearrange("(q r) -> q r", r=RN - 1)

            sp.wait_ge(S("mask_made"), PB - 1)
            sp.dma_start(A["mask_scr"], scoreS).then_inc(S("mask_out"), 16)
            sp.wait_ge(S("bias_out"), 16)
            sp.wait_ge(S("conv_pool_made"), 1)
            for h in range(H):
                sp.dma_start(near[:, h], skewed(h)[:, 0:2 * P]).then_inc(S("near_in"), 16)
            for j in range(3):
                sp.wait_ge(S(f"v_out{j}"), 16 * NG)
            sp.wait_ge(S("gate_done"), 2 * KD * NG)
            for t in range(NT):
                sp.dma_start(vN[:, t], O["v"][tok(t), :]).then_inc(S("vN_in_first" if t < 2 else "vN_in"), 16)
            sp.wait_ge(S("biasS_zero"), 1)
            for h in range(H):
                r = slice(h * QS, (h + 1) * QS)
                sp.dma_start(biasS[r, PAST - P:PAST], skewed(h)[0:QS, 0:P]).then_inc(S("biasS_in"), 16)
                sp.dma_start(biasS[r, PAST:LS].rearrange("p (s q) -> p s q", s=NS),
                             skewed(h)[0:QS, P:P + QS].unsqueeze(1).to_broadcast([QS, NS, QS]))\
                    .then_inc(S("biasS_in"), 16)
            sp.wait_ge(S("c_made"), NG * CT)
            for e in range(2):
                sp.wait_ge(S(f"gate_out{e}"), 16 * KD)
            sp.wait_ge(S("mask_out"), 16)

            def stream_in(st_):
                if st_ >= 2:
                    sp.wait_ge(S("qk_done"), len(units) + st_ - 1)
                sp.dma_start(kcT[st_ % 2], A["cache_k"][st_]).then_inc(S(f"kc_in{st_ % 2}"), 16)

            def values_in(st_):
                if st_ >= 2:
                    sp.wait_ge(S("pvS_done"), st_ - 1)
                sp.dma_start(vc[:, st_ % 2], A["cache_v"][st_].rearrange("(k p) c -> p k c", p=P))\
                    .then_inc(S(f"vc_in{st_ % 2}"), 16)

            def mask_in(st_):
                if st_ >= 2:
                    sp.wait_ge(S("biased"), len(units) + st_ - 1)
                sp.dma_start(maskS[:, st_ % 2], A["mask_scr"][st_ * QS:(st_ + 1) * QS].unsqueeze(0)
                             .to_broadcast([H, QS, LS])).then_inc(S(f"maskS_in{st_ % 2}"), 16)

            stream_in(0)
            values_in(0)
            sp.wait_ge(S("nb_made"), len(units))
            mask_in(0)
            mask_in(1)
            sp.wait_ge(S("pv_done"), len(units))
            stream_in(1)
            values_in(1)
            for st_ in range(2, NS):
                stream_in(st_)
                mask_in(st_)
                values_in(st_)
            sp.dma_start(gmix, A["norm_ffn_g"].partition_broadcast(P)).then_inc(S("gffn_in"), 16)
            sp.wait_ge(S("attn_made"), len(units) // 2 + 5 * NS)

            def merge_in(i, e):
                ct = i * 2 + e
                sp.dma_start(wab[:, e], A["w_ab"][bass.ds(ct, 1)].rearrange("o p k c -> p (o k) c"))\
                    .then_inc(S(f"wab_in{e}"), 16)
                for g in range(2):
                    sp.dma_start(gt[:, e, g], A["gate_scr"][bass.ds(ct + g * KD, 1)].rearrange("o p t -> p (o t)"))\
                        .then_inc(S(f"gt_in{e}{g}"), 16)

            for e in range(2):
                merge_in(0, e)
            sp.dma_start(wout, A["w_out"]).then_inc(S("wout_in"), 16)
            with sp.Fori(1, KD // 2) as i:
                for e in range(2):
                    sp.wait_ge(S("merged"), (i * 2 + e - 1) * NG)
                    merge_in(i, e)
            sp.wait_ge(S("merged"), KD * NG)

            def copy_m(i, first):
                for j in range(3):
                    if not first:
                        sp.wait_ge(S("wo_done"), i * 3 + j - 2)
                        sp.wait_ge(S("h2_turned"), i * 3 + j - 2)
                    sp.dma_start(hs2[:, j], mergedT[:, :, tok(i * 3 + j)]).then_inc(S(f"hs2_in{j}"), 16)
                    sp.dma_start(xs[:, j], A["x"][tok(i * 3 + j), :]).then_inc(S(f"xs_in{j}"), 16)

            copy_m(0, True)
            with sp.Fori(1, NG) as i:
                copy_m(i, False)
            sp.wait_ge(S("wo_done"), NT)
            sp.wait_ge(S("h2_turned"), NT)

            def w_tile(ct):
                return A["w_ffn"][bass.ds(ct, 1)].rearrange("o p n -> p (o n)")

            def gu_in(ct, e):
                sp.dma_start(wraw[:, e], w_tile(ct)[:, 0:2 * D]).then_inc(S(f"wgu_in{e}"), 16)

            def pair_in(g, i, first=False):
                for e in range(2):
                    u = g * FT + i * 2 + e
                    if not (first and e == 0):
                        sp.wait_ge(S("wgu_split"), u)
                    gu_in(i * 2 + e + 1, 1 - e)
                    if not first:
                        sp.wait_ge(S("down_done"), u - 1)
                    sp.dma_start(wdraw[:, e], w_tile(i * 2 + e)[:, 2 * D:3 * D]).then_inc(S(f"wd_in{e}"), 16)

            def y_out(g):
                for tt in range(3):
                    sp.wait_ge(S("y_made"), g * 6 + tt * 2 + 2)
                    sp.dma_start(O["y"][tok(g * 3 + tt), :], ys[:, tt]).then_inc(S(f"y_out{tt}"), 16)

            gu_in(0, 0)
            pair_in(0, 0, True)
            with sp.Fori(1, FT // 2) as i:
                pair_in(0, i)
            with sp.Fori(1, NG) as g:
                pair_in(g, 0)
                y_out(g - 1)
                with sp.Fori(1, FT // 2) as i:
                    pair_in(g, i)
            y_out(NG - 1)
            sp.wait_ge(S("wgu_in0"), 16 * (NG * FT // 2 + 1))
            sp.wait_ge(S("ik_out"), 16)
            for j in range(3):
                sp.wait_ge(S(f"k_out{j}"), 16 * NG)
                sp.wait_ge(S(f"y_out{j}"), 16 * NG)

        @block.tensor
        def _(pe):
            mm = nc.tensor.matmul

            def mm3(dst, whi, wlo, xhi, xlo, start, stop):
                mm(dst, whi, xhi, start=start, stop=False)
                mm(dst, whi, xlo, start=False, stop=False)
                return mm(dst, wlo, xhi, start=False, stop=stop)

            pe.wait_ge(S("first_in"), 16 * 2)

            def norm_group(i, first):
                for j in range(3):
                    pe.wait_ge(S("h_made"), i * 3 + j + 1)
                    if not first:
                        pe.wait_ge(S("hT_made"), (i * 3 + j - 2) * 2)
                    for k in range(KD):
                        l = nc.tensor.transpose(bank(2 * j, w=2)[:, k * P:(k + 1) * P], hb[:, j, k * P:(k + 1) * P],
                                                ident)
                    l.then_inc(S("h_turned"), 1)
                pe.wait_ge(S("hT_made"), (i * 3 + 3) * 2)
                if first:
                    pe.wait_ge(S("const_in"), 16 * NCONST)
                    mm(bank(7, RN)[0:H], relb[0:NB], onehot[0:NB]).then_inc(S("bias_done"), 1)
                    pe.wait_ge(S("brow_made"), 1)
                for c in range(HP + 1):
                    if not (first and c < 2):
                        pe.wait_ge(S("iq_made"), i * (HP + 1) + c - 1)
                    for k in range(KD):
                        if c < HP:
                            w, dst = wiq[:, k, c * P:(c + 1) * P], bank(6 + c % 2, G)
                        else:
                            w, dst = wikw[:, k, :], bank(6 + c % 2, G)[0:72]
                        l = mm(dst, w, hT[:, k, tok(i, G)], start=k == 0, stop=k == KD - 1)
                    l.then_inc(S("iq_done"), 1)

            norm_group(0, True)
            with pe.Fori(1, NG) as i:
                pe.wait_ge(S("iq_made"), i * (HP + 1))
                norm_group(i, False)
            pe.wait_ge(S("hT_made"), 2 * NT)
            for c in range(2):
                for j in range(CT):
                    l = nc.tensor.transpose(bank(c)[:, j * P:j * P + 120], st[0:120, c, j * P:(j + 1) * P],
                                            ident[0:120, 0:120])
            l.then_inc(S("state_turned"), 1)
            pe.wait_ge(S("iq_made"), NG * (HP + 1))
            for t in range(NT):
                l = nc.tensor.transpose(bank(2 + t // 5)[:, (t % 5) * 72:(t % 5) * 72 + 72],
                                        ikwT[0:72, tok(t)], ident[0:72, 0:72])
            l.then_inc(S("ikw_turned"), 1)

            pe.wait_ge(S("ikn_made"), 2)
            for t in range(NT):
                l = nc.tensor.transpose(bank(2, w=3)[:, t * P:(t + 1) * P], ikn[:, t], ident)
            l.then_inc(S("ikn_turned"), 1)
            pe.wait_ge(S("ikT_made"), 3)

            n = 0
            for b in range(2, PB):
                L = (b + 1) * P
                for h in range(H):
                    r = slice(64 * (h % 2), 64 * (h % 2) + 64)
                    if n >= 3:
                        pe.wait_ge(S("relu_done"), n - 2)
                    base = 2 + 2 * (n % 3)
                    for o0 in range(0, L, 512):
                        w = min(512, L - o0)
                        l = mm(bank(base, w=2)[:, o0:o0 + w], iqT[r, h // 2, tok(b)], ikT[r, o0:o0 + w])
                    l.then_inc(S("logit_done"), 1)
                    n += 1
            pe.wait_ge(S("relu_done"), n)
            pe.wait_ge(S("iqs_in"), 16 * H)
            pe.wait_ge(S("sw_made"), NS + 1)

            def sum_heads(st_):
                pe.wait_ge(S("relu_done"), n + st_ + 1)
                for o0, w in ((0, 512), (512, 512), (1024, 128)):
                    l = mm(bank(5, w=3)[:, o0:o0 + w], SW[:, st_], rl[:, st_ % 2, o0:o0 + w],
                           start=st_ == 0, stop=st_ == NS - 1)
                l.then_inc(S("heads_summed"), 1)

            for st_ in range(NS):
                pe.wait_ge(S(f"ikc_in{st_ % 4}"), 16 * (st_ // 4 + 1))
                if st_:
                    pe.wait_ge(S("relu_done"), n + st_)
                q = iqS[0:HD, st_]
                for o0 in (0, 512):
                    mm(bank(2, w=3)[:, o0:o0 + 512], q, ikcT[0:HD, st_ % 4, o0:o0 + 512])
                mm(bank(4, P), q, ikT[0:HD, NP:NTOK]).then_inc(S("logit_done"), 1)
                if st_:
                    sum_heads(st_ - 1)
            sum_heads(NS - 1)

            pe.wait_ge(S("score_done"), PB - 1)
            pe.wait_ge(S("state_made"), 2)

            def glu(j, e, first):
                pe.wait_ge(S(f"wglu_in{e}"), (j // 2) * 16 + 16)
                for g, done, made, b0 in ((1, "glu_b_done", "sigb_made", 3), (0, "glu_a_done", "a_made", 0)):
                    for c in range(NG):
                        if not first:
                            pe.wait_ge(S(made), (j - 1) * NG + c + 1)
                        for k in range(KD):
                            l = mm(bank(b0 + c, G), wglu[:, e, g, k], hT[:, k, tok(c, G)],
                                   start=k == 0, stop=k == KD - 1)
                        l.then_inc(S(done), 1)

            for j in range(CT):
                glu(j, j % 2, j == 0)
            pe.wait_ge(S("us_made"), 1)
            for j in range(CT):
                nc.tensor.transpose(bank(6)[:, j * P:(j + 1) * P], us[:, j], ident)
            for j in range(CT):
                l = nc.tensor.transpose(bank(7)[0:HIST, j * P:(j + 1) * P], uT[:, j, NP:NP + HIST], ident)
            l.then_inc(S("u_turned"), 1)
            pe.wait_ge(S("sigb_made"), NG * CT)
            pe.wait_ge(S("a_made"), NG * CT)

            def turn(c, t, j, first):
                pe.wait_ge(S("qn_made"), c * NT + t + 1)
                if not first:
                    pe.wait_ge(S("turn_made"), c * NT + t - 2)
                for p in range(HP):
                    l = nc.tensor.transpose(bank(3 + j)[:, p * P:(p + 1) * P], qn[:, j, p * P:(p + 1) * P], ident)
                l.then_inc(S("qk_turned"), 1)

            def project(c, i, before):
                for j in range(3):
                    n = c * NT + i * 3 + j
                    pe.wait_ge(S(f"hs_in{j}"), (c * NG + i + 1) * 16)
                    if not (c == 0 and before is None):
                        pe.wait_ge(S("qkv_evac"), n - 2)
                    for k in range(KD):
                        l = mm(bank(j), hs[:, j, k], wqkv[c % 2][:, k], start=k == 0, stop=k == KD - 1)
                    l.then_inc(S("qkv_done"), 1)
                    if j == 0 and before is not None:
                        bc, bt = before
                        if bc < 2:
                            turn(bc, bt, 2, bc == 0 and isinstance(bt, int) and bt < 3)
                    if j > 0 and c < 2:
                        turn(c, i * 3 + j - 1, j - 1, c == 0 and before is None)

            for c in range(3):
                pe.wait_ge(S(f"wqkv_in{c % 2}"), 16 * (c // 2 + 1))
                project(c, 0, None if c == 0 else (c - 1, NT - 1))
                if c == 0:
                    project(c, 1, (c, 2))
                    project(c, 2, (c, 5))
                else:
                    with pe.Fori(1, NG) as i:
                        project(c, i, (c, i * 3 - 1))

            def gate(i, first):
                for e in range(2):
                    pe.wait_ge(S(f"wgate_in{e}"), i * 16 + 16)
                    for c in range(NG):
                        if not first:
                            pe.wait_ge(S("gate_made"), (i * 2 + e - 2) * NG + c + 1)
                        for k in range(KD):
                            l = mm(bank(3 * e + c, G), wgate[:, e, k], hT[:, k, tok(c, G)],
                                   start=k == 0, stop=k == KD - 1)
                        l.then_inc(S("gate_done"), 1)

            pe.wait_ge(S("qkv_evac"), 3 * NT)
            pe.wait_ge(S("turn_made"), 2 * NT)
            gate(0, True)
            with pe.Fori(1, KD - NG) as i:
                gate(i, False)
            pe.wait_ge(S("uo_made"), 2)
            pe.wait_ge(S("conv_made"), CT - 1)
            pe.wait_ge(S("conv_pool_made"), 1)
            for c in range(NG):
                if c:
                    pe.wait_ge(S("d_made"), CT * c)
                for j in range(CT):
                    l = mm(bank(6, G), ones, cT[:, j, tok(c, G)], start=j == 0, stop=j == CT - 1)
                l.then_inc(S("csum_done"), 1)
                gate(KD - NG + c, False)
                pe.wait_ge(S("sq_made"), c + 1)
                if c:
                    pe.wait_ge(S("std_made"), c)
                for j in range(CT):
                    l = mm(bank(7, G), ones, sqc[:, j, tok(c, G)], start=j == 0, stop=j == CT - 1)
                l.then_inc(S("sqsum_done"), 1)
            pe.wait_ge(S("gate_made"), 2 * KD * NG)

            pe.wait_ge(S("std_made"), NG)
            N = len(units)

            def rows(h):
                return slice(64 * (h % 2), 64 * (h % 2) + 64)

            def logits(n):
                b, h = units[n]
                L = (b + 1) * P
                if n >= 2:
                    pe.wait_ge(S("biased"), n - 1)
                for o0 in range(0, L, 512):
                    w = min(512, L - o0)
                    l = mm(bank(2 * (n % 2), w=2)[:, o0:o0 + w], qT[rows(h), h // 2, tok(b)],
                           kT[rows(h), h // 2, o0:o0 + w])
                l.then_inc(S("qk_done"), 1)

            def turn_p(n):
                pe.wait_ge(S("p_made"), n + 1)
                if n:
                    pe.wait_ge(S("pT_made"), n)
                for k in range(units[n][0] + 1):
                    l = nc.tensor.transpose(bank(4, w=2)[:, tok(k)], lpP[n % 3][:, tok(k)], ident)
                l.then_inc(S("p_turned"), 1)

            def weighted(n):
                b, h = units[n]
                pe.wait_ge(S("pT_made"), n + 1)
                if n == 0:
                    pe.wait_ge(S("vN_in_first"), 16 * 2)
                if (b, h) == (2, 0):
                    pe.wait_ge(S("vN_in"), 16 * (NT - 2))
                if h % 2 == 0 and n >= 4:
                    pe.wait_ge(S("attn_made"), n // 2 - 1)
                for k in range(b + 1):
                    l = mm(bank(6 + (n // 2) % 2)[rows(h), 0:P], vN[:, k, h * HD:(h + 1) * HD],
                           pT[:, n % 2, tok(k)], start=k == 0, stop=k == b)
                l.then_inc(S("pv_done"), 1)

            for n in range(N + 3):
                if n < N:
                    logits(n)
                if n >= 3:
                    weighted(n - 3)
                if 2 <= n <= N + 1:
                    turn_p(n - 2)

            def logits_s(st_):
                pe.wait_ge(S(f"kc_in{st_ % 2}"), 16 * (st_ // 2 + 1))
                if st_ >= 1:
                    pe.wait_ge(S("biased"), N + st_)
                for o0, w in ((0, 512), (512, 512), (PAST, P)):
                    dst = bank(1, w=3)[:, o0:o0 + w]
                    for c in range(HP):
                        keys = kcT[st_ % 2][:, c, o0:o0 + w] if o0 < PAST else kT[:, c, NP:NTOK]
                        l = mm(dst, qbd[:, st_, c], keys, start=c == 0, stop=c == HP - 1)
                l.then_inc(S("qk_done"), 1)

            def turn_ps(st_):
                pe.wait_ge(S("p_made"), N + st_ + 1)
                pe.wait_ge(S("pT_made"), N + st_)
                for k in range(9):
                    dst = bank(4, w=2)[:, tok(k)] if k < 8 else bank(6, P)
                    l = nc.tensor.transpose(dst, lp[:, st_ % 2, tok(k)], ident)
                l.then_inc(S("p_turned"), 1)

            def weighted_s(st_):
                pe.wait_ge(S("pT_made"), N + st_ + 1)
                pe.wait_ge(S(f"vc_in{st_ % 2}"), 16 * (st_ // 2 + 1))
                pe.wait_ge(S("attn_made"), N // 2 + 5 * st_)
                for c in range(HP):
                    for k in range(9):
                        v = vc[:, st_ % 2, k] if k < 8 else vN[:, NT - 1]
                        l = mm(bank(7)[:, c * P:(c + 1) * P], v[:, c * P:(c + 1) * P], pT[:, st_ % 2, tok(k)],
                               start=k == 0, stop=k == 8)
                l.then_inc(S("pvS_done"), 1)

            pe.wait_ge(S("attn_made"), N // 2)
            pe.wait_ge(S("qbd_made"), H)
            for st_ in range(NS + 1):
                if st_:
                    turn_ps(st_ - 1)
                if st_ < NS:
                    logits_s(st_)
                if st_:
                    weighted_s(st_ - 1)


            def branches(i, first):
                for e in range(2):
                    if not (first and e == 0):
                        pe.wait_ge(S("merge_split"), i * 2 + e + 1 + 2 * NG)
                    for c in range(NG):
                        if not (first and e == 0):
                            pe.wait_ge(S("merged"), (i * 2 + e - 1) * NG + c + 1)
                        else:
                            pe.wait_ge(S("merge_split"), 3 + 2 * c)
                        for g, hi, lo in ((0, attnhi, attnlo), (1, chi, clo)):
                            for k in range(HP):
                                l = mm3(bank(3 * g + c, G), wabhi[:, e, 4 * g + k], wablo[:, e, 4 * g + k],
                                        hi[:, k, tok(c, G)], lo[:, k, tok(c, G)], k == 0, k == HP - 1)
                        l.then_inc(S("ab_done"), 1)

            branches(0, True)
            with pe.Fori(1, KD // 2) as i:
                branches(i, False)

            def turn_h2(t, j, first):
                pe.wait_ge(S("h2_made"), t + 1)
                if not first:
                    pe.wait_ge(S("h2T_split"), t * 2)
                for k in range(KD):
                    l = nc.tensor.transpose(bank(6, w=2)[:, tok(k)], xs[:, j, k * P:(k + 1) * P], ident)
                l.then_inc(S("h2_turned"), 1)

            def out_tile(i, first):
                for j in range(3):
                    t = i * 3 + j
                    pe.wait_ge(S(f"hs2_in{j}"), i * 16 + 16)
                    if not first:
                        pe.wait_ge(S("x1_made"), (t - 2) * 2)
                    for f in range(2):
                        for k in range(KD):
                            l = mm(bank(2 * j + f), hs2[:, j, k], wout[:, k, 512 * f:512 * f + 512],
                                   start=k == 0, stop=k == KD - 1)
                    l.then_inc(S("wo_done"), 1)
                    if not (first and j == 0):
                        turn_h2(t - 1, (j + 2) % 3, first and j == 1)

            pe.wait_ge(S("wout_in"), 16)
            pe.wait_ge(S("merged"), KD * NG)
            out_tile(0, True)
            with pe.Fori(1, NG) as i:
                out_tile(i, False)
            turn_h2(NT - 1, 2, False)

            def gate_up(g, ct, e):
                pe.wait_ge(S("wgu_split"), g * FT + ct + 1)
                for f, made, done in ((0, "silu_made", "g_done"), (1, "f_made", "u_done")):
                    if not (isinstance(ct, int) and ct == 0):
                        pe.wait_ge(S(made), g * FT + ct)
                    for k in range(KD):
                        c = slice((8 * f + k) * P, (8 * f + k + 1) * P)
                        l = mm3(bank(6 + f, G), wguhi[:, e, c], wgulo[:, e, c], h2hi[:, k, tok(g, G)],
                                h2lo[:, k, tok(g, G)], k == 0, k == KD - 1)
                    l.then_inc(S(done), 1)

            def down(g, ct, e, first=False, last=False):
                pe.wait_ge(S("wd_split"), g * FT + ct + 1)
                pe.wait_ge(S("f_split"), g * FT + ct + 1)
                if first and not (isinstance(g, int) and g == 0):
                    pe.wait_ge(S("y_made"), g * 6)
                for tt in range(3):
                    for f in range(2):
                        c = slice(512 * f, 512 * f + 512)
                        l = mm3(bank(2 * tt + f), fhi[:, e, tok(tt)], flo[:, e, tok(tt)], wdhi[:, e, c], wdlo[:, e, c],
                                first, last)
                l.then_inc(S("down_done"), 1)

            pe.wait_ge(S("h2T_split"), 2 * NT)
            pe.wait_ge(S("x1_made"), 2 * NT)
            def group(g):
                gate_up(g, 0, 0)
                gate_up(g, 1, 1)
                down(g, 0, 0, first=True)
                with pe.Fori(1, FT // 2) as i:
                    gate_up(g, i * 2, 0)
                    down(g, i * 2 - 1, 1)
                    gate_up(g, i * 2 + 1, 1)
                    down(g, i * 2, 0)
                down(g, FT - 1, 1, last=True)

            group(0)
            with pe.Fori(1, NG) as g:
                group(g)

        @block.scalar
        def _(act):
            ac = nc.scalar.activation

            def x_squares(i, first=False):
                for j in range(3):
                    act.wait_ge(S(f"x_in{j}"), i * 16 + 16)
                    if not first:
                        act.wait_ge(S("h_turned"), i * 3 + j - 2)
                    ac(hb[:, j], xb[:, j], ACT.Square, accum_out=ss[:, j:j + 1]).then_inc(S("ss_made"), 1)

            def norm_group(i, last=False):
                for j in range(3):
                    act.wait_ge(S("h_turned"), i * 3 + j + 1)
                    for c in range(2):
                        ac(hT[:, 4 * c:4 * c + 4, tok(i * 3 + j)], bank(2 * j + c).rearrange("p (k t) -> p k t", k=4),
                           ACT.Copy).then_inc(S("hT_made"), 1)
                if not last:
                    x_squares(i + 1)
                for c in range(HP + 1):
                    act.wait_ge(S("iq_done"), i * (HP + 1) + c + 1)
                    if c < HP:
                        l = ac(iqT[:, c, tok(i, G)], bank(6 + c % 2, G), ACT.Copy)
                    else:
                        l = ac(ikwT[0:72, tok(i, G)], bank(6 + c % 2, G)[0:72], ACT.Copy)
                    l.then_inc(S("iq_made"), 1)

            x_squares(0, True)
            norm_group(0)
            with act.Fori(1, NG - 1) as i:
                norm_group(i)
            norm_group(NG - 1, last=True)
            act.wait_ge(S("state_turned"), 1)
            for c in range(2):
                ac(uT[:, :, UP:].rearrange("p j (s t) -> p j s t", s=NS)[:, :, 4 * c:4 * c + 4, 0:HIST],
                   bank(c).rearrange("p (j t) -> p j t", j=CT)[:, :, 0:120].rearrange("p j (s t) -> p j s t", s=4),
                   ACT.Copy).then_inc(S("state_made"), 1)
            act.wait_ge(S("ikw_turned"), 1)
            ac(ikwN[:, 0:5], bank(2, 360).rearrange("p (t c) -> p t c", c=72), ACT.Copy).then_inc(S("ikwN_made"), 1)
            ac(ikwN[:, 5:9], bank(3, 288).rearrange("p (t c) -> p t c", c=72), ACT.Copy).then_inc(S("ikwN_made"), 1)

            act.wait_ge(S("ikn_turned"), 1)
            for c in range(3):
                w = min(512, NTOK - 512 * c)
                ac(ikT[:, 512 * c:512 * c + w], bank(2 + c, w), ACT.Copy).then_inc(S("ikT_made"), 1)
            n = 0
            act.wait_ge(S("iw_made"), 1)
            for b in range(2, PB):
                for h in range(H):
                    act.wait_ge(S("logit_done"), n + 1)
                    if n >= 2:
                        act.wait_ge(S("term_added"), n - 1)
                    ac(rl[:, n % 2, 0:(b + 1) * P], bank(2 + 2 * (n % 3), w=2)[:, 0:(b + 1) * P], ACT.Relu)\
                        .then_inc(S("relu_done"), 1)
                    act.wait_ge(S("relu_done"), n + 1)
                    ac(rl[:, n % 2, 0:(b + 1) * P], rl[:, n % 2, 0:(b + 1) * P], ACT.Copy, scale=iwN[:, b, h:h + 1])\
                        .then_inc(S("term_made"), 1)
                    n += 1
            act.wait_ge(S("term_added"), n)
            for st_ in range(NS):
                act.wait_ge(S("logit_done"), n + st_ + 1)
                if st_ >= 2:
                    act.wait_ge(S("heads_summed"), st_ - 1)
                ac(rl[:, st_ % 2], bank(2, w=3, n=128), ACT.Relu).then_inc(S("relu_done"), 1)

            act.wait_ge(S("heads_summed"), NS)
            ac(scoreS, bank(5, w=3, n=P), ACT.Copy).then_inc(S("scoreS_copied"), 1)

            act.wait_ge(S("bias_out"), 16)
            for j in range(CT):
                if j:
                    act.wait_ge(S("u_made"), 2 * j)
                else:
                    act.wait_ge(S("ikn_turned"), 1)
                for c in range(NG):
                    act.wait_ge(S("glu_b_done"), j * NG + c + 1)
                    ac(sigb[:, c], bank(3 + c, G), ACT.Sigmoid).then_inc(S("sigb_made"), 1)
                for c in range(NG):
                    act.wait_ge(S("glu_a_done"), j * NG + c + 1)
                    ac(acopy[:, c], bank(c, G), ACT.Copy).then_inc(S("a_made"), 1)
            act.wait_ge(S("u_turned"), 1)
            ac(uo, bank(6), ACT.Copy).then_inc(S("uo_made"), 1)
            ac(ut[0:HIST], bank(7)[0:HIST], ACT.Copy).then_inc(S("uo_made"), 1)

            def turned(c, t, j):
                act.wait_ge(S("qk_turned"), c * NT + t + 1)
                if c == 0:
                    act.dma_start(O["k"][tok(t), :], qn[:, j]).then_inc(S(f"k_out{j}"), 16)
                ac((kT if c == 0 else qT)[:, :, tok(t)], bank(3 + j).rearrange("p (c t) -> p c t", c=HP), ACT.Copy)\
                    .then_inc(S("turn_made"), 1)

            def evac(c, i, before):
                for j in range(3):
                    n = c * NT + i * 3 + j
                    act.wait_ge(S("qkv_done"), n + 1)
                    if not (c == 0 and before is None):
                        if c < 2 or before[0] < 2:
                            act.wait_ge(S("qn_made"), n - 2)
                        else:
                            act.wait_ge(S(f"v_out{j}"), i * 16)
                    l = ac(raw[:, j], bank(j), ACT.Copy)
                    if c < 2:
                        l.then_inc(S("raw_made"), 1)
                        act.wait_ge(S("raw_made"), n + 1)
                        for h in range(H):
                            l = ac(bank(j)[:, h * HD:(h + 1) * HD], bank(j)[:, h * HD:(h + 1) * HD], ACT.Square,
                                   accum_out=ssq[:, j * H + h:j * H + h + 1])
                    l.then_inc(S("qkv_evac"), 1)
                    if c == 2:
                        act.wait_ge(S("qkv_evac"), n + 1)
                        act.dma_start(O["v"][tok(i * 3 + j), :], raw[:, j]).then_inc(S(f"v_out{j}"), 16)
                    if j == 0 and before is not None and before[0] < 2:
                        turned(before[0], before[1], 2)
                    if j > 0 and c < 2:
                        turned(c, i * 3 + j - 1, j - 1)

            for c in range(3):
                evac(c, 0, None if c == 0 else (c - 1, NT - 1))
                with act.Fori(1, NG) as i:
                    evac(c, i, (c, i * 3 - 1))

            def gate(i, first):
                for e in range(2):
                    if not first:
                        act.wait_ge(S(f"gate_out{e}"), i * 16)
                    for c in range(NG):
                        act.wait_ge(S("gate_done"), (i * 2 + e) * NG + c + 1)
                        ac(gb[:, e, tok(c, G)], bank(3 * e + c, G), ACT.Sigmoid).then_inc(S("gate_made"), 1)
                    act.wait_ge(S("gate_made"), (i * 2 + e + 1) * NG)
                    act.dma_start(A["gate_scr"][bass.ds(i * 2 + e, 1)].rearrange("o p t -> p (o t)"), gb[:, e])\
                        .then_inc(S(f"gate_out{e}"), 16)

            gate(0, True)
            with act.Fori(1, KD - NG) as i:
                gate(i, False)
            for j in range(3):
                act.wait_ge(S(f"v_out{j}"), 16 * NG)

            def std(c):
                act.wait_ge(S("sqsum_done"), c + 1)
                ac(acc[:, tok(c, G)], bank(7, G), ACT.Sqrt, scale=1.0 / CH, bias=epsc).then_inc(S("std_made"), 1)

            for c in range(NG):
                act.wait_ge(S("d_made"), CT * (c + 1))
                ac(sqc[:, :, tok(c, G)], cT[:, :, tok(c, G)], ACT.Square).then_inc(S("sq_made"), 1)
                gate(KD - NG + c, False)
                std(c)
            for c in range(NG):
                act.wait_ge(S("dn_made"), c + 1)
                for j in range(CT):
                    ac(cT[:, j, tok(c, G)], cT[:, j, tok(c, G)], ACT.Silu, scale=lng[:, j:j + 1],
                       bias=lnb[:, j:j + 1]).then_inc(S("c_made"), 1)

            N = len(units)

            def exps(n, dst, e):
                act.wait_ge(S("nmx_made"), n + 1)
                ac(dst, dst, ACT.Exp, bias=nmx[:, e:e + 1], accum_out=sm[:, e:e + 1]).then_inc(S("exp_done"), 1)

            for e in range(2):
                act.wait_ge(S(f"gate_out{e}"), 16 * KD)
            for n in range(N + 3):
                if n < N:
                    exps(n, lpP[n % 3][:, 0:(units[n][0] + 1) * P], n % 3)
                if n >= 3 and n % 2 == 0:
                    b, h = units[n - 3]
                    act.wait_ge(S("pv_done"), n - 2)
                    ac(attnT[:, h // 2, tok(b)], bank(6 + ((n - 3) // 2) % 2, P), ACT.Copy).then_inc(S("attn_made"), 1)
                if 2 <= n <= N + 1:
                    m = n - 2
                    L = (units[m][0] + 1) * P
                    act.wait_ge(S("p_turned"), m + 1)
                    if m >= 2:
                        act.wait_ge(S("pv_done"), m - 1)
                    ac(pT[:, m % 2, 0:L], bank(4, w=2)[:, 0:L], ACT.Copy).then_inc(S("pT_made"), 1)

            for st_ in range(NS + 1):
                if st_:
                    act.wait_ge(S("p_turned"), N + st_)
                    if st_ >= 3:
                        act.wait_ge(S("pvS_done"), st_ - 2)
                    ac(pT[:, (st_ - 1) % 2], bank(4, w=3, n=P), ACT.Copy).then_inc(S("pT_made"), 1)
                if st_ < NS:
                    exps(N + st_, lp[:, st_ % 2], st_ % 2)

            act.wait_ge(S("attn_made"), N // 2 + 5 * NS)

            def wab_high(i, e, first=False):
                act.wait_ge(S(f"wab_in{e}"), i * 16 + 16)
                if not first:
                    act.wait_ge(S("ab_done"), (i * 2 + e - 1) * NG)
                ac(wabhi[:, e], wab[:, e], ACT.Copy).then_inc(S("merge_high"), 1)

            for c in range(NG):
                ac(attnhi[:, :, tok(c, G)], attnT[:, :, tok(c, G)], ACT.Copy).then_inc(S("merge_high"), 1)
                ac(chi[:, :, tok(c, G)], cT[:, :, tok(c, G)], ACT.Copy).then_inc(S("merge_high"), 1)
                if c == 0:
                    wab_high(0, 0, True)
            wab_high(0, 1, True)
            with act.Fori(1, KD // 2) as i:
                for e in range(2):
                    wab_high(i, e)

            def turned_h2(t):
                act.wait_ge(S("h2_turned"), t + 1)
                for f in range(2):
                    ac(h2hi[:, 4 * f:4 * f + 4, tok(t)], bank(6 + f).rearrange("p (k t) -> p k t", k=4), ACT.Copy)\
                        .then_inc(S("h2T_made"), 1)

            def squares(i, first):
                for j in range(3):
                    t = i * 3 + j
                    act.wait_ge(S("x1_made"), (t + 1) * 2)
                    ac(xs[:, j], x1[:, bass.ds(t, 1)].rearrange("p o d -> p (o d)"), ACT.Square,
                       accum_out=ss[:, j:j + 1]).then_inc(S("ss_made"), 1)
                    if not (first and j == 0):
                        turned_h2(t - 1)

            squares(0, True)
            with act.Fori(1, NG) as i:
                squares(i, False)
            turned_h2(NT - 1)
            def gu_high(m, e):
                act.wait_ge(S(f"wgu_in{e}"), m * 16)
                ac(wguhi[:, e], wraw[:, e], ACT.Copy).then_inc(S("wgu_high"), 1)

            act.wait_ge(S("h2_turned"), NT)
            gu_high(1, 0)
            with act.Fori(0, NG) as g:
                with act.Fori(0, FT // 2) as i:
                    for e in range(2):
                        u = g * FT + i * 2 + e
                        act.wait_ge(S("g_done"), u + 1)
                        ac(sg[:, e], bank(6, G), ACT.Silu).then_inc(S("silu_made"), 1)
                        gu_high(g * (FT // 2) + i + 1 + e, 1 - e)
                        act.wait_ge(S("f_made"), u + 1)
                        ac(fhi[:, e], sg[:, e], ACT.Copy).then_inc(S("f_high"), 1)
                        act.wait_ge(S(f"wd_in{e}"), (g * (FT // 2) + i) * 16 + 16)
                        ac(wdhi[:, e], wdraw[:, e], ACT.Copy).then_inc(S("wd_high"), 1)

        @block.vector
        def _(dve):
            ve = nc.vector

            def low(lo, x, hi):
                return ve.tensor_tensor(lo, x, hi.bitcast(F32), ALU.subtract)

            ch = Chain(dve, S("dve_chain"))
            ve.memset(ones, 1.0).then_inc(S("filled"), 1)
            ve.memset(uT[:, :, 0:HIST], 0.0).then_inc(S("filled"), 1)
            ch.add(ve.memset(SW, 0.0))
            dve.wait_ge(S("first_in"), 16 * 2)

            def norm_group(i):
                for j in range(3):
                    dve.wait_ge(S("rstd_made"), i * 3 + j + 1)
                    ve.scalar_tensor_tensor(hb[:, j], xb[:, j], rstd[:, j:j + 1], gmix, ALU.mult, ALU.mult)\
                        .then_inc(S("h_made"), 1)

            norm_group(0)
            dve.wait_ge(S("bias_done"), 1)
            ch.link(ve.tensor_copy(bfar[0:H], bank(7, 1)[0:H]))
            ve.tensor_scalar(brow[0:H], bank(7, RN)[0:H], bfar[0:H], None, ALU.subtract).then_inc(S("brow_made"), 1)

            with dve.Fori(1, NG) as i:
                norm_group(i)
            dve.wait_ge(S("ikwN_made"), 2)
            ve.tensor_scalar(iwN, ikwN[:, :, HD:72], ISC, None, ALU.mult).then_inc(S("iw_made"), 1)
            ch.link(ve.tensor_tensor(ikn[:, :, 0:HD], ikwN[:, :, 0:HD], ikwN[:, :, 0:HD], ALU.mult))
            ve.tensor_reduce(ssq[:, 0:NT], ikn[:, :, 0:HD], AX.X, ALU.add).then_inc(S("ssik_made"), 1)
            dve.wait_ge(S("rik_made"), 1)
            ch.link(ve.tensor_tensor(ikwN[:, :, 0:HD], ikwN[:, :, 0:HD],
                                     rsq[:, 0:NT].unsqueeze(2).to_broadcast([P, NT, HD]), ALU.mult))
            for c in range(2):
                ve.tensor_tensor(ikn[:, :, 64 * c:64 * c + 64], ikwN[:, :, 0:HD],
                                 ikg.unsqueeze(1).to_broadcast([P, NT, HD]), ALU.mult).then_inc(S("ikn_made"), 1)
            dve.wait_ge(S("iws_in"), 16 * H)
            ch.wait()
            for st_ in range(NS):
                ve.tensor_scalar(SW[:, st_, st_ * QS:(st_ + 1) * QS], delta, iwS[:, st_:st_ + 1], None, ALU.mult)\
                    .then_inc(S("sw_made"), 1)
            ve.memset(m8, 0.0).then_inc(S("sw_made"), 1)
            dve.wait_ge(S("sw_made"), NS + 1)
            for b, sc in [(b, score[b]) for b in range(2, PB)] + [(PB, scoreS)]:
                dve.wait_ge(S("score_done"), b - 1)
                for _ in range(TOPK // 8):
                    ch.link(ve.max(m8, sc))
                    ch.link(ve.match_replace(sc, m8, sc, TAKEN))
                ve.tensor_scalar(sc, sc, TAKEN, NEG, ALU.is_gt, ALU.mult).then_inc(S("mask_made"), 1)
            dve.wait_ge(S("u_turned"), 1)
            dve.wait_ge(S("u_made"), 2 * CT)
            for j in range(CT - 1):
                op = acc[:, 0:NP]
                os_ = acc[:, NP:NTOK].rearrange("p (s q) -> p s q", s=NS)
                for d in range(CK):
                    up, usamp, w = uT[:, j, d:d + NP], uSamp[:, j, :, d:d + QS], cw[:, j, d:d + 1]
                    if d == 0:
                        ch.add(ve.tensor_scalar(op, up, w, cb[:, j:j + 1], ALU.mult, ALU.add))
                        ch.add(ve.tensor_scalar(os_, usamp, w, cb[:, j:j + 1], ALU.mult, ALU.add))
                    else:
                        ch.add(ve.scalar_tensor_tensor(op, up, w, op, ALU.mult, ALU.add))
                        ch.add(ve.scalar_tensor_tensor(os_, usamp, w, os_, ALU.mult, ALU.add))
                    ch.wait()
                ve.tensor_copy(cT[:, j], acc).then_inc(S("conv_made"), 1)
                dve.wait_ge(S("conv_made"), j + 1)
            def over_std(c):
                dve.wait_ge(S("std_made"), c + 1)
                a = acc[:, tok(c, G)]
                ch.link(ve.reciprocal(a, a))
                ve.tensor_tensor(cT[:, :, tok(c, G)], cT[:, :, tok(c, G)],
                                 a.unsqueeze(1).to_broadcast([P, CT, G]), ALU.mult).then_inc(S("dn_made"), 1)

            for c in range(NG):
                dve.wait_ge(S("csum_done"), c + 1)
                for j in range(CT):
                    ve.scalar_tensor_tensor(cT[:, j, tok(c, G)], bank(6, G), -1.0 / CH, cT[:, j, tok(c, G)],
                                            ALU.mult, ALU.add).then_inc(S("d_made"), 1)
                if c:
                    over_std(c - 1)
            over_std(NG - 1)

            dve.wait_ge(S("gate_done"), 2 * KD * NG)
            ve.memset(biasS, 0.0).then_inc(S("biasS_zero"), 1)
            N = len(units)

            def normalize(n, p, e):
                dve.wait_ge(S("exp_done"), n + 1)
                ch.link(ve.reciprocal(rc[:, e:e + 1], sm[:, e:e + 1]))
                ve.tensor_scalar(p, p, rc[:, e:e + 1], None, ALU.mult).then_inc(S("p_made"), 1)

            def bias_max(dst, src, add, e, start):
                return ve.tensor_tensor_reduce(dst, src, add, 1.0, start, ALU.add, ALU.max, mx[:, e:e + 1])

            def negate(n, e):
                dve.wait_ge(S("biased"), n + 1)
                ve.tensor_scalar(nmx[:, e:e + 1], mx[:, e:e + 1], -1.0, None, ALU.mult)\
                    .then_inc(S("nmx_made"), 1)

            for n in range(N + 1):
                if n < N:
                    b, h = units[n]
                    e, L = n % 3, (b + 1) * P
                    far = max(L - 2 * P, 0)
                    src = bank(2 * (n % 2), w=2)
                    dve.wait_ge(S("qk_done"), n + 1)
                    if n >= 3:
                        dve.wait_ge(S("p_turned"), n - 2)
                        dve.wait_ge(S("nmx_made"), n - 2)
                    start = -3e38
                    if far:
                        ch.link(bias_max(lpP[e][:, 0:far], src[:, 0:far], score[b][:, 0:far], 3 + e, -3e38))
                        start = mx[:, 3 + e:4 + e]
                    dve.wait_ge(S("nb_made"), n + 1)
                    bias_max(lpP[e][:, far:L], src[:, far:L], nb[n % 2][:, 2 * P - (L - far):2 * P], e, start)\
                        .then_inc(S("biased"), 1)
                    negate(n, e)
                if n:
                    normalize(n - 1, lpP[(n - 1) % 3][:, 0:(units[n - 1][0] + 1) * P], (n - 1) % 3)
            dve.wait_ge(S("nb_made"), N)
            dve.wait_ge(S("p_turned"), N)
            ch.link(ve.memset(qbd, 0.0))
            for h in range(H):
                r = slice(64 * (h % 2), 64 * (h % 2) + 64)
                ve.tensor_copy(qbd[r, :, h // 2, h * QS:(h + 1) * QS],
                               qT[r, h // 2, NP:NTOK].rearrange("p (s q) -> p s q", s=NS)).then_inc(S("qbd_made"), 1)

            def outputs(st_):
                dve.wait_ge(S("pvS_done"), st_ + 1)
                for par in range(2):
                    r = slice(64 * par, 64 * par + 64)
                    t = slice(NP + st_ * QS, NP + (st_ + 1) * QS)
                    o = bank(7)[r, QS * par:QS * par + 480].rearrange("p (c x) -> p c x", x=160)
                    ve.tensor_copy(attnT[r, 0:3, t], o[:, :, 0:QS]).then_inc(S("attn_made"), 1)
                    ve.tensor_copy(attnT[r, 3, t], bank(7)[r, 480 + QS * par:496 + QS * par])\
                        .then_inc(S("attn_made"), 1)
                ve.memset(m8, 0.0).then_inc(S("attn_made"), 1)

            for st_ in range(NS + 1):
                n = N + st_
                if st_:
                    normalize(n - 1, lp[:, (st_ - 1) % 2], (st_ - 1) % 2)
                if st_ < NS:
                    dve.wait_ge(S("qk_done"), n + 1)
                    dve.wait_ge(S("p_turned"), n - 1)
                    dve.wait_ge(S("maskS_made"), st_ + 1)
                    bias_max(lp[:, st_ % 2], bank(1, w=3, n=P), maskS[:, st_ % 2], st_ % 2, -3e38)\
                        .then_inc(S("biased"), 1)
                    negate(n, st_ % 2)
                if st_:
                    outputs(st_ - 1)

            def wab_low(m, e, first=False):
                dve.wait_ge(S("merge_high"), m + 1 + 2 * NG if not first else 3)
                low(wablo[:, e], wab[:, e], wabhi[:, e]).then_inc(S("merge_split"), 1)

            dve.wait_ge(S("attn_made"), N // 2 + 5 * NS)
            for c in range(NG):
                t = tok(c, G)
                for f, (lo, x, hi) in enumerate(((attnlo, attnT, attnhi), (clo, cT, chi))):
                    dve.wait_ge(S("merge_high"), 2 * c + (c > 0) + f + 1)
                    low(lo[:, :, t], x[:, :, t], hi[:, :, t]).then_inc(S("merge_split"), 1)
                if c == 0:
                    wab_low(0, 0, True)

            def gated(i, first=False, last=False):
                for e in range(2):
                    if not (last and e == 1):
                        wab_low(i * 2 + e + 1, 1 - e)
                    for g in range(2):
                        dve.wait_ge(S(f"gt_in{e}{g}"), i * 16 + 16)
                    for c in range(NG):
                        m = (i * 2 + e) * NG + c
                        q = (e * NG + c) % 2
                        dve.wait_ge(S("ab_done"), m + 1)
                        if not (first and e == 0 and c < 2):
                            dve.wait_ge(S("merged"), m - 1)
                        for g in range(2):
                            ve.tensor_tensor(part[:, q, g], bank(3 * g + c, G), gt[:, e, g, tok(c, G)], ALU.mult)\
                                .then_inc(S("parts"), 1)
                        dve.wait_ge(S("parts"), m * 2 + 2)
                        ve.tensor_tensor(mergedT[:, bass.ds(i * 2 + e, 1), tok(c, G)], part[:, q, 0:1],
                                         part[:, q, 1:2], ALU.add).then_inc(S("merged"), 1)

            gated(0, True)
            with dve.Fori(1, KD // 2 - 1) as i:
                gated(i)
            gated(KD // 2 - 1, last=True)

            dve.wait_ge(S("gffn_in"), 16)

            def normed(t, j):
                dve.wait_ge(S("rstd_made"), NT + t + 1)
                ve.scalar_tensor_tensor(xs[:, j], x1[:, bass.ds(t, 1)].rearrange("p o d -> p (o d)"),
                                        rstd[:, j:j + 1], gmix, ALU.mult, ALU.mult).then_inc(S("h2_made"), 1)

            def h2_low(t):
                dve.wait_ge(S("h2T_made"), t * 2 + 2)
                for f in range(2):
                    low(h2lo[:, 4 * f:4 * f + 4, tok(t)], bank(6 + f).rearrange("p (k t) -> p k t", k=4),
                        h2hi[:, 4 * f:4 * f + 4, tok(t)]).then_inc(S("h2T_split"), 1)

            def residual(i, first):
                for j in range(3):
                    t = i * 3 + j
                    dve.wait_ge(S("wo_done"), t + 1)
                    dve.wait_ge(S(f"xs_in{j}"), i * 16 + 16)
                    for f in range(2):
                        r = slice(512 * f, 512 * f + 512)
                        ve.tensor_tensor(x1[:, bass.ds(t, 1), r], bank(2 * j + f).unsqueeze(1),
                                         xs[:, j:j + 1, r], ALU.add).then_inc(S("x1_made"), 1)
                    if not (first and j == 0):
                        h2_low(t - 1)
                    normed(t, j)

            residual(0, True)
            with dve.Fori(1, NG) as i:
                residual(i, False)
            h2_low(NT - 1)
            def gu_low(m, e):
                dve.wait_ge(S("wgu_high"), m)
                low(wgulo[:, e], wraw[:, e], wguhi[:, e]).then_inc(S("wgu_split"), 1)

            dve.wait_ge(S("wo_done"), NT)
            gu_low(1, 0)

            def hidden(g, first):
                with dve.Fori(0, FT // 2) as i:
                    for e in range(2):
                        u = g * FT + i * 2 + e
                        dve.wait_ge(S("u_done"), u + 1)
                        dve.wait_ge(S("silu_made"), u + 1)
                        ve.tensor_tensor(sg[:, e], sg[:, e], bank(7, G), ALU.mult).then_inc(S("f_made"), 1)
                        gu_low(u + 2, 1 - e)
                        dve.wait_ge(S("f_high"), u + 1)
                        low(flo[:, e], sg[:, e], fhi[:, e]).then_inc(S("f_split"), 1)
                        dve.wait_ge(S("wd_high"), u + 1)
                        low(wdlo[:, e], wdraw[:, e], wdhi[:, e]).then_inc(S("wd_split"), 1)
                dve.wait_ge(S("down_done"), (g + 1) * FT)
                for tt in range(3):
                    if not first:
                        dve.wait_ge(S(f"y_out{tt}"), g * 16)
                    for f in range(2):
                        r = slice(512 * f, 512 * f + 512)
                        ve.tensor_tensor(ys[:, tt:tt + 1, r], bank(2 * tt + f).unsqueeze(1),
                                         x1[:, bass.ds(g * 3 + tt, 1), r], ALU.add).then_inc(S("y_made"), 1)

            hidden(0, True)
            with dve.Fori(1, NG) as g:
                hidden(g, False)

        @block.gpsimd
        def _(pool):
            gp = nc.gpsimd
            ch = Chain(pool, S("pool_chain"))
            ch.add(gp.memset(mhalf, -0.5))
            ch.add(gp.memset(epsc, EPS))
            ch.add(gp.memset(eps8, EPS))
            ch.add(gp.memset(per_d, 1.0 / D))
            ch.add(gp.memset(per_hd, 1.0 / HD))
            ch.wait()

            def norm_group(i):
                for j in range(3):
                    pool.wait_ge(S("ss_made"), i * 3 + j + 1)
                    ch.link(gp.tensor_tensor(ms[:, j:j + 1], ss[:, j:j + 1], per_d, ALU.mult))
                    ch.link(gp.tensor_tensor(ms[:, j:j + 1], ms[:, j:j + 1], epsc, ALU.add))
                    gp.tensor_tensor(rstd[:, j:j + 1], ms[:, j:j + 1], mhalf[:, 0:1], ALU.pow)\
                        .then_inc(S("rstd_made"), 1)

            norm_group(0)
            with pool.Fori(1, NG) as i:
                ch.loop(i - 1, 6)
                norm_group(i)
            ch.done(NG - 1)
            pool.wait_ge(S("const_in"), 16 * NCONST)
            ch.link(gp.tensor_scalar(qg, qg, HD ** -0.5, 0.0, ALU.mult, ALU.add))
            pool.wait_ge(S("ssik_made"), 1)
            ch.link(gp.tensor_scalar(msq[:, 0:NT], ssq[:, 0:NT], 1.0 / HD, EPS, ALU.mult, ALU.add))
            gp.tensor_tensor(rsq[:, 0:NT], msq[:, 0:NT], mhalf[:, 0:NT], ALU.pow).then_inc(S("rik_made"), 1)
            n = 0
            for b in range(2, PB):
                L = (b + 1) * P
                for h in range(H):
                    pool.wait_ge(S("term_made"), n + 1)
                    if h == 0:
                        l = gp.tensor_copy(score[b], rl[:, n % 2, 0:L])
                    else:
                        pool.wait_ge(S("term_added"), n)
                        l = gp.tensor_tensor(score[b], rl[:, n % 2, 0:L], score[b], ALU.add)
                    l.then_inc(S("term_added"), 1)
                    n += 1
                pool.wait_ge(S("term_added"), n)
                gp.memset(score[b][0:CHUNK, L - CHUNK:L], NEG).then_inc(S("score_done"), 1)
            pool.wait_ge(S("scoreS_copied"), 1)
            gp.tensor_tensor(scoreS[:, PAST:LS], scoreS[:, PAST:LS], newneg, ALU.add).then_inc(S("score_done"), 1)
            pool.wait_ge(S("state_made"), 2)
            for j in range(CT):
                pool.wait_ge(S("a_made"), NG * (j + 1))
                pool.wait_ge(S("sigb_made"), NG * (j + 1))
                a, b = (v.rearrange("p c t -> p (c t)") for v in (acopy, sigb))
                gp.tensor_tensor(uT[:, j, HIST:UP], a[:, 0:NP], b[:, 0:NP], ALU.mult).then_inc(S("u_made"), 1)
                gp.tensor_tensor(uSamp[:, j, :, HIST:US], a[:, NP:NTOK].rearrange("p (s q) -> p s q", s=NS),
                                 b[:, NP:NTOK].rearrange("p (s q) -> p s q", s=NS), ALU.mult).then_inc(S("u_made"), 1)
            pool.wait_ge(S("u_made"), 2 * CT)
            for j in range(CT):
                l = gp.tensor_copy(us[:, j].rearrange("p (s q) -> p s q", s=NS), uSamp[:, j, :, HIST:US])
            l.then_inc(S("us_made"), 1)

            def qk_norm(c, i, first):
                for j in range(3):
                    n = c * NT + i * 3 + j
                    pool.wait_ge(S("qkv_evac"), n + 1)
                    if c < 2:
                        q3 = raw[:, j].rearrange("p (h d) -> p h d", h=H)
                        r = slice(j * H, (j + 1) * H)
                        ch.link(gp.tensor_tensor(msq[:, r], ssq[:, r], per_hd, ALU.mult))
                        ch.link(gp.tensor_tensor(msq[:, r], msq[:, r], eps8, ALU.add))
                        ch.link(gp.tensor_tensor(rsq[:, r], msq[:, r], mhalf[:, 0:H], ALU.pow))
                        ch.link(gp.tensor_tensor(q3, q3, rsq[:, r].unsqueeze(2).to_broadcast([P, H, HD]), ALU.mult))
                        if not (c == 0 and first):
                            pool.wait_ge(S("qk_turned"), n - 2)
                            if c == 0:
                                pool.wait_ge(S(f"k_out{j}"), i * 16)
                            else:
                                pool.wait_ge(S(f"k_out{j}"), NG * 16)
                        gp.tensor_tensor(qn[:, j], raw[:, j], kg if c == 0 else qg, ALU.mult).then_inc(S("qn_made"), 1)

            for c in range(2):
                qk_norm(c, 0, True)
                with pool.Fori(1, NG) as i:
                    ch.loop(i - 1, 12)
                    qk_norm(c, i, False)
                ch.done(NG - 1)
            pool.wait_ge(S("u_turned"), 1)
            pool.wait_ge(S("out_state"), 48)
            j = CT - 1
            for d in range(CK):
                if d >= 2:
                    ch.wait()
                for x, t, a in ((uT[:, j, d:d + NP], tap[:, 0:NP], acc_pool[:, 0:NP]),
                                (uSamp[:, j, :, d:d + QS], tap[:, NP:NTOK].rearrange("p (s q) -> p s q", s=NS),
                                 acc_pool[:, NP:NTOK].rearrange("p (s q) -> p s q", s=NS))):
                    w = cw[:, j, d:d + 1]
                    if d == 0:
                        ch.add(gp.tensor_scalar(a, x, w, cb[:, j:j + 1], ALU.mult, ALU.add))
                    else:
                        ch.add(gp.tensor_scalar(t, x, w, None, ALU.mult))
                ch.wait()
                if d:
                    ch.add(gp.tensor_tensor(acc_pool, tap, acc_pool, ALU.add))
            ch.wait()
            gp.tensor_copy(cT[:, j], acc_pool).then_inc(S("conv_pool_made"), 1)
            pool.wait_ge(S("conv_made"), CT - 1)
            ch.link(gp.memset(mask0, 0.0))
            ch.link(gp.memset(mask0[0:CHUNK, 2 * P - CHUNK:2 * P], NEG))
            pool.wait_ge(S("near_in"), 16 * H)
            for n, (b, h) in enumerate(units):
                if n >= 2:
                    pool.wait_ge(S("biased"), n - 1)
                if b >= 2:
                    pool.wait_ge(S("mask_made"), b - 1)
                m = mask0 if b < 2 else score[b][:, (b - 1) * P:(b + 1) * P]
                gp.tensor_tensor(nb[n % 2], m, near[:, h], ALU.add).then_inc(S("nb_made"), 1)
            pool.wait_ge(S("biasS_in"), 16 * 2 * H)
            for st_ in range(NS):
                pool.wait_ge(S(f"maskS_in{st_ % 2}"), 16 * (st_ // 2 + 1))
                gp.tensor_tensor(maskS[:, st_ % 2], maskS[:, st_ % 2], biasS, ALU.add).then_inc(S("maskS_made"), 1)

            def norm2_group(i):
                for j in range(3):
                    pool.wait_ge(S("ss_made"), NT + i * 3 + j + 1)
                    ch.link(gp.tensor_tensor(ms[:, j:j + 1], ss[:, j:j + 1], per_d, ALU.mult))
                    ch.link(gp.tensor_tensor(ms[:, j:j + 1], ms[:, j:j + 1], epsc, ALU.add))
                    gp.tensor_tensor(rstd[:, j:j + 1], ms[:, j:j + 1], mhalf[:, 0:1], ALU.pow)\
                        .then_inc(S("rstd_made"), 1)

            with pool.Fori(0, NG) as i:
                ch.loop(i, 6)
                norm2_group(i)
            ch.done(NG)


def layouts(i):
    w_in = i["w_in"][0]
    o_iq = 3 * AW
    cat = lambda *a: np.ascontiguousarray(np.concatenate(a, axis=0))
    con = np.ascontiguousarray
    k_first = lambda w: con(w.reshape(-1, P, w.shape[1]).transpose(1, 0, 2))
    cols = lambda w: con(w.reshape(-1, P, w.shape[1] // P, P).transpose(2, 1, 0, 3))
    o_ik = o_iq + IDXC
    o_glu = o_ik + HD + H
    out = {
        "x": cat(i["x_prompt"][0], i["x_sample"].reshape(-1, D)),
        "ident": np.eye(P, dtype=np.float32),
        "delta": con(np.tile(np.eye(QS, dtype=np.float32), (H, 1))),
        "newneg": np.where(np.kron(np.eye(NS), np.ones((QS, QS))) > 0, 0.0, NEG).astype(np.float32),
        "onehot": bucket_rows(),
        "rel_bias": con(i["rel_bias"]),
        "cache_k": con(i["cache_k"][0].reshape(NS, PAST, HP, P).transpose(0, 3, 2, 1)),
        "cache_v": con(i["cache_v"][0].reshape(NS, PAST, AW)),
        "norm_mix_g": con(i["norm_mix_g"][0]),
        "qg": con(np.tile(i["q_norm_g"][0], H)),
        "kg": con(np.tile(i["k_norm_g"][0], H)),
        "idx_k_norm_g": con(i["idx_k_norm_g"][0]),
        "w_iq": k_first(w_in[:, o_iq:o_ik]),
        "w_ikw": k_first(w_in[:, o_ik:o_glu]),
        "conv_w": con(i["conv_dw_w"][0, :, 0].T.reshape(CT, P, CK).transpose(1, 0, 2)),
        "conv_b": con(i["conv_dw_b"][0].reshape(CT, P).T),
        "conv_ln_g": con(i["conv_ln_g"][0].reshape(CT, P).T),
        "conv_ln_b": con(i["conv_ln_b"][0].reshape(CT, P).T),
        "w_glu": con(np.stack([cols(w_in[:, o_glu:o_glu + CH]), cols(w_in[:, o_glu + CH:o_glu + 2 * CH])], axis=2)),
        "w_qkv": con(np.stack([k_first(w_in[:, o:o + AW]) for o in (AW, 0, 2 * AW)])),
        "w_gates": cols(w_in[:, o_glu + 2 * CH:]),
        "w_ab": cols(cat(i["w_attn_out"][0], i["w_conv_out"][0])),
        "w_out": k_first(i["w_out"][0]),
        "norm_ffn_g": con(i["norm_ffn_g"][0]),
        "w_ffn": con(np.concatenate([cols(i["w_ffn_gate"][0]).reshape(FT, P, D), cols(i["w_ffn_up"][0]).reshape(FT, P, D),
                                     i["w_ffn_down"][0].reshape(FT, P, D)], axis=2)[list(range(FT)) + [0]]),
        "state": con(i["state_conv"][0].reshape(NS * HIST, CH)),
        "cache_ik": con(i["cache_idx_k"][0].transpose(0, 2, 1)),
    }
    return out


SCRATCH = {"iw_scr": (P, H), "gate_scr": (2 * KD, P, NTOK), "bias_scr": (H, P, RN), "mask_scr": (P, LS)}
OUTS = {"y": (NTOK, D), "k": (NTOK, AW), "v": (NTOK, AW), "ik": (NTOK, HD),
        "conv_prompt": (HIST, CH), "conv_sample": (NS * HIST, CH)}


def kernel(**inputs):
    import concourse.bacc as bacc
    from concourse.bass_utils import run_bass_kernel_spmd

    nc = bacc.Bacc("TRN2", target_bir_lowering=False, num_devices=1)
    arrays = {f"in_{k}": v for k, v in layouts({k: np.asarray(v) for k, v in inputs.items()}).items()}
    A = {k[3:]: nc.dram_tensor(k, v.shape, mybir.dt.from_np(v.dtype), kind="ExternalInput").ap()
         for k, v in arrays.items()}
    A.update({k: nc.dram_tensor(k, sh, F32, kind="Internal").ap() for k, sh in SCRATCH.items()})
    O = {k: nc.dram_tensor(f"out_{k}", sh, F32, kind="ExternalOutput").ap() for k, sh in OUTS.items()}
    build(nc, A, O)
    r = run_bass_kernel_spmd(nc, [arrays], core_ids=[0]).results[0]
    y, k, v, ik, cp, cs = (r[f"out_{n}"] for n in ("y", "k", "v", "ik", "conv_prompt", "conv_sample"))
    return (y[:NP].reshape(1, NP, D), y[NP:].reshape(NS, QS, D),
            k[:NP].reshape(1, 1, NP, H, HD), v[:NP].reshape(1, 1, NP, H, HD), ik[:NP].reshape(1, 1, NP, HD),
            cp.reshape(1, 1, HIST, CH),
            k[NP:].reshape(1, NS, QS, H, HD), v[NP:].reshape(1, NS, QS, H, HD), ik[NP:].reshape(1, NS, QS, HD),
            cs.reshape(1, NS, HIST, CH))
```

```python
import math
from contextlib import ExitStack

import numpy as np
import concourse.bass as bass
from concourse import mybir

F32 = mybir.dt.float32
F32R = mybir.dt.float32r
ALU = mybir.AluOpType
ACT = mybir.ActivationFunctionType
AX = mybir.AxisListType

P = 128
D = 1024
NP = 1024
NS, QS = 8, 16
PAST = 1024
NTOK = NP + NS * QS
NT = NTOK // P
PB = NP // P
G = 384
NG = NTOK // G
H, HD = 8, 64
HP = H // 2
AW = H * HD
CH = 512
CT = CH // P
CK = 31
HIST = CK - 1
FF = -(-8 * D // (3 * 256)) * 256
FT = FF // P
KD = D // P
TOPK = 256
CHUNK = 64
NB = 32
EPS = 1e-6
NEG = -1e30
TAKEN = -3e38
LS = PAST + NS * QS
RMIN = -(2 * P - 1)
RN = 3 * P
IDXC = H * HD
ISC = (HD ** -0.5) * (H ** -0.5)
UP = HIST + NP
US = HIST + QS
UW = UP + NS * US


SLAB = 53184
CONVO = 17088


def bucket_rows():
    rel = np.arange(RMIN, RMIN + RN)
    n = np.abs(rel)
    nf = np.maximum(n, 1).astype(np.float32)
    large = 8 + (np.log(nf / np.float32(8)) / np.float32(math.log(16)) * np.float32(8)).astype(np.int32)
    b = np.where(rel > 0, 16, 0) + np.where(n < 8, n, np.minimum(large, 15))
    return (b[None, :] == np.arange(NB)[:, None]).astype(np.float32)


class Chain:

    def __init__(self, eng, sem):
        self.eng, self.sem, self.n, self.base, self.i, self.per = eng, sem, 0, 0, None, 0

    def add(self, ins):
        ins.then_inc(self.sem, 1)
        self.n += 1

    def loop(self, i, per):
        self.base, self.n, self.i, self.per = self.base + self.n, 0, i, per

    def done(self, trips):
        assert self.n == self.per, (self.n, self.per)
        self.base, self.n, self.i = self.base + trips * self.per, 0, None

    def wait(self):
        at = self.base + self.n
        self.eng.wait_ge(self.sem, at if self.i is None else self.i * self.per + at)

    def link(self, ins):
        self.add(ins)
        self.wait()


def build(nc, A, O):
    with ExitStack() as ctx:
        sbuf0 = -(-nc.sbuf_base // 32) * 32
        ps = ctx.enter_context(nc.psum_tensor("ps", [P, 8 * 512], F32))

        def sem(name):
            return ctx.enter_context(nc.semaphore(name))

        at = [0]
        bufs = [0]

        def take(n, off=None):
            if off is None:
                off = at[0]
                at[0] += n
            return place(n, off, F32)

        def take_r(n, off):
            return place(n, off, F32R)

        def place(n, off, dtype):
            assert off + n <= SLAB
            bufs[0] += 1
            return nc.alloc_sbuf_tensor_at(f"buf{bufs[0]}", [P, n], dtype, offset=sbuf0 + 4 * off)[:]

        def bank(b, n=512, w=1):
            return ps[:, 512 * b:512 * (b + w - 1) + n]

        ident = take(P)
        ones = take(P)
        gmix = take(D)
        o_g = at[0]
        qg, kg = take(AW), take(AW)
        ikg = take(HD)
        small = take(400)
        iwN = take(NT * H).rearrange("p (t h) -> p t h", t=NT)
        delta = take(QS)
        newneg = take(P)
        mhalf = small[:, 0:16]
        ss = small[:, 16:32]
        ms = small[:, 32:48]
        rstd = small[:, 48:64]
        iwS = small[:, 64:72]
        cw = small[:, 72:72 + CT * CK].rearrange("p (j k) -> p j k", j=CT)
        cb = small[:, 196:200]
        lng = small[:, 200:204]
        lnb = small[:, 204:208]
        mx = small[:, 208:224]
        nmx = small[:, 224:240]
        sm = small[:, 240:256]
        rc = small[:, 256:272]
        m8 = small[:, 272:280]
        epsc = small[:, 280:281]
        per_d = small[:, 281:282]
        eps8 = small[:, 384:392]
        per_hd = small[:, 392:400]
        ssq = small[:, 288:320]
        msq = small[:, 320:352]
        rsq = small[:, 352:384]
        o_h = at[0]
        hT = take(KD * NTOK).rearrange("p (k t) -> p k t", k=KD)
        o_q = at[0]
        qT = take(HP * NTOK).rearrange("p (c t) -> p c t", c=HP)
        o_k = at[0]
        kT = take(HP * NTOK).rearrange("p (c t) -> p c t", c=HP)
        score = {b: take((b + 1) * P) for b in range(2, PB)}
        scoreS = take(LS)
        uT = take(CT * UW).rearrange("p (j t) -> p j t", j=CT)
        o_w = at[0]

        iqT = take(HP * NTOK, o_q).rearrange("p (c t) -> p c t", c=HP)
        wiq = take(KD * IDXC, o_k).rearrange("p (k c) -> p k c", k=KD)
        xb = take(3 * D, o_w).rearrange("p (s d) -> p s d", s=3)
        hb = take(3 * D, o_w + 3 * D).rearrange("p (s d) -> p s d", s=3)
        o = o_w + 6 * D
        ikcT = take(4 * PAST, o_w + 8 * PAST).rearrange("p (s t) -> p s t", s=4)
        o += 6 * PAST
        ikT = take(NTOK, o)
        o += NTOK
        rl = take(2 * LS, o_w + CONVO + NTOK).rearrange("p (s t) -> p s t", s=2)
        ikwN = take(NT * 72, o_w + 3 * LS).rearrange("p (t c) -> p t c", t=NT)
        ikn = take(NT * P, o_w + 3 * LS + NT * 72).rearrange("p (t c) -> p t c", t=NT)
        assert 3 * LS + NT * 72 + NT * P <= 6 * D
        iqS = take(H * P, o).rearrange("p (s h q) -> p s h q", s=NS, h=H)
        o += H * P
        wikw = take(KD * 72, o).rearrange("p (k c) -> p k c", k=KD)
        o += KD * 72
        SW = take(NS * P, o).rearrange("p (s t) -> p s t", s=NS)
        o += NS * P
        st = take(2 * CH, o).rearrange("p (s c) -> p s c", s=2)
        o += 2 * CH
        ikwT = take(NTOK, o)
        o += NTOK

        hhi = take_r(KD * NTOK, o_w).rearrange("p (k t) -> p k t", k=KD)
        hlo = take_r(KD * NTOK, o_h).rearrange("p (k t) -> p k t", k=KD)
        wcol = take(4 * KD * P, o_k).rearrange("p (s k c) -> p s k c", s=4, k=KD)
        wcollo = take_r(4 * KD * P, o_k).rearrange("p (s k c) -> p s k c", s=4, k=KD)
        wcolhi = take_r(4 * KD * P, o_q).rearrange("p (s k c) -> p s k c", s=4, k=KD)
        gb = take(2 * NTOK, o_w + KD * NTOK).rearrange("p (s t) -> p s t", s=2)
        wqkv = [take(KD * AW, o_w + KD * NTOK + 2 * NTOK).rearrange("p (k c) -> p k c", k=KD),
                take(KD * AW, o_w).rearrange("p (k c) -> p k c", k=KD)]
        o = o_w + KD * AW
        hs = take(3 * D, o).rearrange("p (s k t) -> p s k t", s=3, k=KD)
        raw = take(3 * AW, o + 3 * D).rearrange("p (s c) -> p s c", s=3)
        qn = take(3 * AW, o + 3 * D + 3 * AW).rearrange("p (s c) -> p s c", s=3)
        sqc = take(CT * NTOK, o_w + KD * D).rearrange("p (j t) -> p j t", j=CT)
        o = o_w + CONVO
        sigb = take(NTOK, o).rearrange("p (c t) -> p c t", c=NG)
        acc = take(NTOK, o)
        acc_pool = take(NTOK, o_w + (KD + 2) * NTOK + KD * AW)
        tap = take(NTOK, o + 2 * NTOK)
        acopy = take(NTOK, o + NTOK).rearrange("p (c t) -> p c t", c=NG)
        us = take(CT * P, o + NTOK).rearrange("p (j t) -> p j t", j=CT)
        uo = take(CH, o + NTOK + CH)
        ut = take(CH, o + NTOK + 2 * CH)
        uSamp = uT[:, :, UP:].rearrange("p j (s t) -> p j s t", s=NS)
        cT = uT[:, :, 0:NTOK]
        NLOG = (PB - 2) * H

        onehot = take(RN, o_w + CONVO + NTOK)
        relb = take(H, o_w + CONVO + NTOK + RN)
        brow = take(RN, o_w + CONVO + NTOK + RN + H)
        bfar = take(1, o_w + CONVO + NTOK + 2 * RN + H)
        vN = take(NT * AW, o_h).rearrange("p (t c) -> p t c", t=NT)
        attnT = take(HP * NTOK, o_h + NT * AW).rearrange("p (c t) -> p c t", c=HP)
        lp = take(2 * LS, o_w).rearrange("p (s t) -> p s t", s=2)
        pT = take(2 * LS, o_w + 2 * LS).rearrange("p (s t) -> p s t", s=2)
        biasS = take(LS, o_w + 4 * LS)
        o = o_w + 5 * LS
        kcT = [take(HP * PAST, b).rearrange("p (c t) -> p c t", c=HP) for b in (o, o + 16 * AW)]
        vc = [take(8 * AW, b).rearrange("p (k c) -> p k c", k=8) for b in (o + 8 * AW, o_h)]
        o += 24 * AW
        lpP = [lp[:, 0], lp[:, 1], take(NP, o_g)]
        assert NP <= 2 * AW
        near = take(H * 2 * P, o + 2 * H * QS).rearrange("p (h j) -> p h j", h=H)
        maskS = take(2 * LS, o).rearrange("p (s t) -> p s t", s=2)
        nb = [gmix[:, 2 * P * e:2 * P * (e + 1)] for e in range(2)]
        mask0 = gmix[:, 4 * P:6 * P]
        o_s = o_k + HP * NTOK
        qbd = take(NS * HP * P, o_s).rearrange("p (s c m) -> p s c m", s=NS, c=HP)
        mergedT = take(KD * NTOK, o_q).rearrange("p (k t) -> p k t", k=KD)
        o = o_w + 5 * LS
        wab = take(2 * KD * P, o).rearrange("p (s k c) -> p s k c", s=2, k=KD)
        gt = take(4 * NTOK, o + 2 * KD * P).rearrange("p (s g t) -> p s g t", s=2, g=2)
        part = take(2 * 2 * G, o_w + LS + 2 * KD * P).rearrange("p (s g t) -> p s g t", s=2, g=2)
        attnhi = take_r(HP * NTOK, o_h).rearrange("p (c t) -> p c t", c=HP)
        attnlo = take_r(HP * NTOK, o_h + NT * AW).rearrange("p (c t) -> p c t", c=HP)
        chi = take_r(CT * NTOK, o_s).rearrange("p (j t) -> p j t", j=CT)
        clo = take_r(CT * UW, o_w - CT * UW).rearrange("p (j t) -> p j t", j=CT)[:, :, 0:NTOK]
        wabhi = take_r(2 * KD * P, o_w + LS).rearrange("p (s k c) -> p s k c", s=2, k=KD)
        wablo = take_r(2 * KD * P, o_w + 5 * LS).rearrange("p (s k c) -> p s k c", s=2, k=KD)
        wout = take(KD * D, o + 2 * KD * P + 4 * NTOK).rearrange("p (k c) -> p k c", k=KD)
        hs2 = take(3 * D, o_w - 3 * D).rearrange("p (s k t) -> p s k t", s=3, k=KD)
        xs = take(3 * D, o_w + KD * NTOK).rearrange("p (s d) -> p s d", s=3)
        x1 = take(NT * D, o_h).rearrange("p (t d) -> p t d", t=NT)
        h2hi = take_r(KD * NTOK, o_w).rearrange("p (k t) -> p k t", k=KD)
        h2lo = take_r(KD * NTOK, o_q).rearrange("p (k t) -> p k t", k=KD)
        o = o_s
        wraw = take(2 * 2 * D, o).rearrange("p (s n) -> p s n", s=2)
        wguhi = take_r(2 * 2 * D, o + 4 * D).rearrange("p (s n) -> p s n", s=2)
        sg = take(2 * G, o + 8 * D).rearrange("p (s t) -> p s t", s=2)
        fhi = take_r(2 * G, o + 8 * D + 2 * G).rearrange("p (s t) -> p s t", s=2)
        flo = take_r(2 * G, o + 8 * D + 4 * G).rearrange("p (s t) -> p s t", s=2)
        assert o + 8 * D + 6 * G <= o_w
        o = o_w + KD * NTOK
        ys = take(3 * D, o).rearrange("p (s d) -> p s d", s=3)
        wgulo = take_r(2 * 2 * D, o + 3 * D).rearrange("p (s n) -> p s n", s=2)
        wdraw = take(2 * D, o + 7 * D).rearrange("p (s n) -> p s n", s=2)
        wdlo = take_r(2 * D, o + 7 * D).rearrange("p (s n) -> p s n", s=2)
        wdhi = take_r(2 * D, o + 9 * D).rearrange("p (s n) -> p s n", s=2)
        units = [(b, h) for b in range(PB) for h in range(H)]

        s = {}

        def S(name):
            if name not in s:
                s[name] = sem(name)
            return s[name]

        block = ctx.enter_context(nc.Block())

        def tok(t, n=P):
            return bass.ds(t * n, n)

        NCONST = 15
        NGLU, NCOL = 2 * CT, 2 * CT + 2 * KD

        POOL_TAPS = CK // 2
        EARLY = 1

        LN_END = EARLY + 1 + 3 * 2 * NG + 1

        NEARLY = 6
        assert NEARLY < H and NEARLY * HP * P <= (PB - 3) * (PB + 4) // 2 * P

        def ln_step(n):
            first = EARLY + 1
            return {first + 3 * (2 * c + k): (k, c) for c in range(NG) for k in range(2)}.get(n)

        @block.sync
        def _(sp):
            def const(dst, src):
                sp.dma_start(dst, src).then_inc(S("const_in"), 16)

            sp.dma_start(ident, A["ident"]).then_inc(S("first_in"), 16)
            sp.dma_start(gmix, A["norm_mix_g"].partition_broadcast(P)).then_inc(S("first_in"), 16)
            for j in range(3):
                sp.dma_start(xb[:, j], A["x"][tok(j), :]).then_inc(S(f"x_in{j}"), 16)
            const(relb[0:NB], A["rel_bias"])
            const(onehot[0:NB], A["onehot"])
            const(wiq, A["w_iq"])
            const(wikw, A["w_ikw"])
            const(qg, A["qg"].partition_broadcast(P))
            const(kg, A["kg"].partition_broadcast(P))
            const(ikg, A["idx_k_norm_g"].partition_broadcast(P))
            const(delta, A["delta"])
            const(newneg, A["newneg"])
            const(cw, A["conv_w"])
            const(cb, A["conv_b"])
            const(lng, A["conv_ln_g"])
            const(lnb, A["conv_ln_b"])
            for c in range(2):
                const(st[0:120, c], A["state"][120 * c:120 * c + 120, :])
            with sp.Fori(1, NG) as i:
                for j in range(3):
                    sp.wait_ge(S("h_made"), i * 3 + j - 2)
                    sp.dma_start(xb[:, j], A["x"][tok(i * 3 + j), :]).then_inc(S(f"x_in{j}"), 16)
            for t in range(NT):
                sp.wait_ge(S("hT_made"), 2 * t + 2)
                sp.dma_start(A["hT_scr"][t].rearrange("p (k t) -> p k t", k=KD), hT[:, :, tok(t)])\
                    .then_inc(S("hT_out"), 16)
            for st_ in range(4):
                sp.dma_start(ikcT[0:HD, st_], A["cache_ik"][st_]).then_inc(S(f"ikc_in{st_}"), 16)

            sp.wait_ge(S("brow_made"), 1)
            sp.dma_start(A["bias_scr"], brow[0:H].unsqueeze(1).to_broadcast([H, P, RN])).then_inc(S("bias_out"), 16)

            sp.wait_ge(S("ikn_made"), 2)
            sp.dma_start(O["ik"].rearrange("(t p) d -> p t d", p=P), ikn[:, :, 0:HD]).then_inc(S("ik_out"), 16)
            sp.wait_ge(S("iw_made"), 1)
            sp.dma_start(A["iw_scr"], iwN[:, NT - 1]).then_inc(S("iw_out"), 16)
            sp.wait_ge(S("iw_out"), 16)
            for h in range(H):
                sp.dma_start(iwS[h * QS:(h + 1) * QS, :],
                             A["iw_scr"].rearrange("(s q) h -> h q s", q=QS)[h],
                             allow_slow_non_contiguous=True).then_inc(S("iws_in"), 16)
            sp.wait_ge(S("iq_made"), NG * (HP + 1))
            for h in range(H):
                sp.dma_start(iqS[0:HD, :, h], iqT[64 * (h % 2):64 * (h % 2) + 64, h // 2, NP:NTOK]
                             .rearrange("p (s q) -> p s q", s=NS)).then_inc(S("iqs_in"), 16)
            sp.wait_ge(S("iq_done"), NG * (HP + 1))

            def col_in(i, m):
                sp.dma_start(wcol[:, m], A["w_cols"][bass.ds(i * 4 + m, 1)].rearrange("o p k c -> p (o k) c"))\
                    .then_inc(S(f"wcol_in{m}"), 16)

            for m in range(4):
                col_in(0, m)
            for st_ in range(4, NS):
                sp.wait_ge(S("logit_done"), NLOG + st_ - 3)
                sp.dma_start(ikcT[0:HD, st_ - 4], A["cache_ik"][st_]).then_inc(S(f"ikc_in{st_ - 4}"), 16)
            sp.wait_ge(S("heads_summed"), NS)
            sp.dma_start(wqkv[0], A["w_qkv"][0]).then_inc(S("wqkv_in0"), 16)
            for m in range(4, 12):
                sp.wait_ge(S("col_done"), NG * (m - 3))
                col_in(m // 4, m % 4)
            so = O["conv_sample"].rearrange("(s t) c -> s t c", s=NS)
            sp.dma_start(so[:, 0:HIST - QS], A["state"].rearrange("(s t) c -> s t c", s=NS)[:, QS:HIST])\
                .then_inc(S("out_state"), 16)
            sp.wait_ge(S("uo_made"), 2)
            sp.dma_start(so[:, HIST - QS:HIST], uo).then_inc(S("out_state"), 16)
            sp.dma_start(O["conv_prompt"], ut[0:HIST]).then_inc(S("out_state"), 16)
            with sp.Fori(3, NCOL // 4) as i:
                for m in range(4):
                    sp.wait_ge(S("col_done"), NG * (i * 4 + m - 3))
                    col_in(i, m)

            def copy_h(c, i, first):
                for j in range(3):
                    if not first:
                        sp.wait_ge(S("qkv_done"), c * NT + i * 3 + j - 2)
                    sp.dma_start(hs[:, j], A["hT_scr"][bass.ds(i * 3 + j, 1)]
                                 .rearrange("o p (k t) -> p (o k) t", k=KD)).then_inc(S(f"hs_in{j}"), 16)

            sp.wait_ge(S("hT_out"), 16 * NT)
            sp.wait_ge(S("col_done"), NG * NCOL)
            for c in range(3):
                copy_h(c, 0, c == 0)
                if c == 0:
                    sp.dma_start(wqkv[1], A["w_qkv"][1]).then_inc(S("wqkv_in1"), 16)
                if c == 1:
                    sp.dma_start(wqkv[0], A["w_qkv"][2]).then_inc(S("wqkv_in0"), 16)
                with sp.Fori(1, NG) as i:
                    copy_h(c, i, False)
            def skewed(h):
                flat = A["bias_scr"].rearrange("h q r -> (h q r)")
                at0 = h * P * RN + P - 1
                return flat[at0:at0 + P * (RN - 1)].rearrange("(q r) -> q r", r=RN - 1)

            sp.wait_ge(S("mask_made"), PB - 1)
            sp.dma_start(A["mask_scr"], scoreS).then_inc(S("mask_out"), 16)
            sp.wait_ge(S("bias_out"), 16)
            sp.wait_ge(S("conv_pool_made"), 1)
            for h in range(H):
                sp.dma_start(near[:, h], skewed(h)[:, 0:2 * P]).then_inc(S("near_in"), 16)
            sp.wait_ge(S("biasS_zero"), 1)
            for h in range(H):
                r = slice(h * QS, (h + 1) * QS)
                sp.dma_start(biasS[r, PAST - P:PAST], skewed(h)[0:QS, 0:P]).then_inc(S("biasS_in"), 16)
                sp.dma_start(biasS[r, PAST:LS].rearrange("p (s q) -> p s q", s=NS),
                             skewed(h)[0:QS, P:P + QS].unsqueeze(1).to_broadcast([QS, NS, QS]))\
                    .then_inc(S("biasS_in"), 16)
            sp.wait_ge(S("dn_made"), CT)
            for e in range(2):
                sp.wait_ge(S(f"gate_out{e}"), 16 * KD)
            sp.wait_ge(S("mask_out"), 16)

            def stream_in(st_):
                if st_ >= 2:
                    sp.wait_ge(S("qk_done"), len(units) + st_ - 1)
                sp.dma_start(kcT[st_ % 2], A["cache_k"][st_]).then_inc(S(f"kc_in{st_ % 2}"), 16)

            def values_in(st_):
                if st_ >= 2:
                    sp.wait_ge(S("pvS_done"), st_ - 1)
                sp.dma_start(vc[st_ % 2], A["cache_v"][st_].rearrange("(k p) c -> p k c", p=P))\
                    .then_inc(S(f"vc_in{st_ % 2}"), 16)

            def mask_in(st_):
                if st_ >= 2:
                    sp.wait_ge(S("biased"), len(units) + st_ - 1)
                sp.dma_start(maskS[:, st_ % 2], A["mask_scr"][st_ * QS:(st_ + 1) * QS].unsqueeze(0)
                             .to_broadcast([H, QS, LS])).then_inc(S(f"maskS_in{st_ % 2}"), 16)

            stream_in(0)
            values_in(0)
            stream_in(1)
            sp.wait_ge(S("nb_made"), len(units))
            mask_in(0)
            mask_in(1)
            sp.wait_ge(S("pv_done"), len(units))
            for j in range(3):
                sp.wait_ge(S(f"v_out{j}"), 16 * NG)
            values_in(1)
            for st_ in range(2, NS):
                stream_in(st_)
                mask_in(st_)
                values_in(st_)
            def merge_in(i, e):
                ct = i * 2 + e
                sp.dma_start(wab[:, e], A["w_ab"][bass.ds(ct, 1)].rearrange("o p k c -> p (o k) c"))\
                    .then_inc(S(f"wab_in{e}"), 16)
                for g in range(2):
                    sp.dma_start(gt[:, e, g], A["gate_scr"][bass.ds(ct + g * KD, 1)].rearrange("o p t -> p (o t)"))\
                        .then_inc(S(f"gt_in{e}{g}"), 16)

            sp.wait_ge(S("qk_done"), len(units) + NS - 1)
            sp.wait_ge(S("pvS_done"), NS - 1)
            for e in range(2):
                merge_in(0, e)
            sp.dma_start(gmix, A["norm_ffn_g"].partition_broadcast(P)).then_inc(S("gffn_in"), 16)
            sp.wait_ge(S("attn_made"), len(units) // 2 + 5 * NS)
            sp.dma_start(wout, A["w_out"]).then_inc(S("wout_in"), 16)
            with sp.Fori(1, KD // 2) as i:
                for e in range(2):
                    sp.wait_ge(S("merged"), (i * 2 + e - 1) * NG)
                    merge_in(i, e)
            sp.wait_ge(S("merged"), KD * NG)

            def w_tile(ct):
                return A["w_ffn"][bass.ds(ct, 1)].rearrange("o p n -> p (o n)")

            def gu_in(ct, e):
                sp.dma_start(wraw[:, e], w_tile(ct)[:, 0:2 * D]).then_inc(S(f"wgu_in{e}"), 16)

            def merged_in(i, j):
                sp.dma_start(hs2[:, j], mergedT[:, :, tok(i * 3 + j)]).then_inc(S(f"hs2_in{j}"), 16)

            for j in range(3):
                sp.dma_start(xs[:, j], A["x"][tok(j), :]).then_inc(S(f"xs_in{j}"), 16)
            for j in range(3):
                merged_in(1, j)
            gu_in(0, 0)
            for i in range(1, NG):
                for j in range(3):
                    t = i * 3 + j
                    sp.wait_ge(S("h2_turned"), t - 2)
                    sp.dma_start(xs[:, j], A["x"][tok(t), :]).then_inc(S(f"xs_in{j}"), 16)
                    if i + 1 < NG:
                        sp.wait_ge(S("wo_done"), t + 1)
                        merged_in(i + 1, j)
            def pair_in(g, i, first=False):
                for e in range(2):
                    u = g * FT + i * 2 + e
                    if not (first and e == 0):
                        sp.wait_ge(S("wgu_split"), u)
                    gu_in(i * 2 + e + 1, 1 - e)
                    if not first:
                        sp.wait_ge(S("down_done"), u - 1)
                    sp.dma_start(wdraw[:, e], w_tile(i * 2 + e)[:, 2 * D:3 * D]).then_inc(S(f"wd_in{e}"), 16)

            def y_out(g):
                for tt in range(3):
                    sp.wait_ge(S("y_made"), g * 6 + tt * 2 + 2)
                    sp.dma_start(O["y"][tok(g * 3 + tt), :], ys[:, tt]).then_inc(S(f"y_out{tt}"), 16)

            sp.wait_ge(S("wo_done"), NT)
            pair_in(0, 0, True)
            with sp.Fori(1, FT // 2) as i:
                pair_in(0, i)
            with sp.Fori(1, NG) as g:
                pair_in(g, 0)
                y_out(g - 1)
                with sp.Fori(1, FT // 2) as i:
                    pair_in(g, i)
            y_out(NG - 1)
            sp.wait_ge(S("wgu_in0"), 16 * (NG * FT // 2 + 1))
            sp.wait_ge(S("ik_out"), 16)
            for j in range(3):
                sp.wait_ge(S(f"k_out{j}"), 16 * NG)
                sp.wait_ge(S(f"v_out{j}"), 16 * NG)
                sp.wait_ge(S(f"y_out{j}"), 16 * NG)

        @block.tensor
        def _(pe):
            mm = nc.tensor.matmul

            def mm3(dst, whi, wlo, xhi, xlo, start, stop):
                mm(dst, whi, xhi, start=start, stop=False)
                mm(dst, whi, xlo, start=False, stop=False)
                return mm(dst, wlo, xhi, start=False, stop=stop)

            pe.wait_ge(S("first_in"), 16 * 2)

            def norm_group(i, first):
                for j in range(3):
                    pe.wait_ge(S("h_made"), i * 3 + j + 1)
                    if not first:
                        pe.wait_ge(S("hT_made"), (i * 3 + j - 2) * 2)
                    for k in range(KD):
                        l = nc.tensor.transpose(bank(2 * j, w=2)[:, k * P:(k + 1) * P], hb[:, j, k * P:(k + 1) * P],
                                                ident)
                    l.then_inc(S("h_turned"), 1)
                pe.wait_ge(S("hT_made"), (i * 3 + 3) * 2)
                if first:
                    pe.wait_ge(S("const_in"), 16 * NCONST)
                    mm(bank(7, RN)[0:H], relb[0:NB], onehot[0:NB]).then_inc(S("bias_done"), 1)
                    pe.wait_ge(S("brow_made"), 1)
                for c in range(HP + 1):
                    if not (first and c < 2):
                        pe.wait_ge(S("iq_made"), i * (HP + 1) + c - 1)
                    for k in range(KD):
                        if c < HP:
                            w, dst = wiq[:, k, c * P:(c + 1) * P], bank(6 + c % 2, G)
                        else:
                            w, dst = wikw[:, k, :], bank(6 + c % 2, G)[0:72]
                        l = mm(dst, w, hT[:, k, tok(i, G)], start=k == 0, stop=k == KD - 1)
                    l.then_inc(S("iq_done"), 1)

            norm_group(0, True)
            with pe.Fori(1, NG) as i:
                pe.wait_ge(S("iq_made"), i * (HP + 1))
                norm_group(i, False)
            pe.wait_ge(S("hT_made"), 2 * NT)
            for c in range(2):
                for j in range(CT):
                    l = nc.tensor.transpose(bank(c)[:, j * P:j * P + 120], st[0:120, c, j * P:(j + 1) * P],
                                            ident[0:120, 0:120])
            l.then_inc(S("state_turned"), 1)
            pe.wait_ge(S("iq_made"), NG * (HP + 1))
            for t in range(NT):
                l = nc.tensor.transpose(bank(2 + t // 5)[:, (t % 5) * 72:(t % 5) * 72 + 72],
                                        ikwT[0:72, tok(t)], ident[0:72, 0:72])
            l.then_inc(S("ikw_turned"), 1)

            pe.wait_ge(S("ikn_made"), 2)
            for t in range(NT):
                l = nc.tensor.transpose(bank(2, w=3)[:, t * P:(t + 1) * P], ikn[:, t], ident)
            l.then_inc(S("ikn_turned"), 1)
            pe.wait_ge(S("ikT_made"), 3)

            n = 0
            for b in range(2, PB):
                L = (b + 1) * P
                for h in range(H):
                    r = slice(64 * (h % 2), 64 * (h % 2) + 64)
                    if n >= 3:
                        pe.wait_ge(S("relu_done"), n - 2)
                    base = 2 + 2 * (n % 3)
                    for o0 in range(0, L, 512):
                        w = min(512, L - o0)
                        l = mm(bank(base, w=2)[:, o0:o0 + w], iqT[r, h // 2, tok(b)], ikT[r, o0:o0 + w])
                    l.then_inc(S("logit_done"), 1)
                    n += 1
            pe.wait_ge(S("relu_done"), n)
            pe.wait_ge(S("iqs_in"), 16 * H)
            pe.wait_ge(S("sw_made"), NS + 1)

            def sum_heads(st_):
                pe.wait_ge(S("relu_done"), n + st_ + 1)
                for o0, w in ((0, 512), (512, 512), (1024, 128)):
                    l = mm(bank(5, w=3)[:, o0:o0 + w], SW[:, st_], rl[:, st_ % 2, o0:o0 + w],
                           start=st_ == 0, stop=st_ == NS - 1)
                l.then_inc(S("heads_summed"), 1)

            for st_ in range(NS):
                pe.wait_ge(S(f"ikc_in{st_ % 4}"), 16 * (st_ // 4 + 1))
                if st_:
                    pe.wait_ge(S("relu_done"), n + st_)
                q = iqS[0:HD, st_]
                for o0 in (0, 512):
                    mm(bank(2, w=3)[:, o0:o0 + 512], q, ikcT[0:HD, st_ % 4, o0:o0 + 512])
                mm(bank(4, P), q, ikT[0:HD, NP:NTOK]).then_inc(S("logit_done"), 1)
                if st_:
                    sum_heads(st_ - 1)
            sum_heads(NS - 1)

            pe.wait_ge(S("scoreS_copied"), 1)
            pe.wait_ge(S("state_made"), 2)

            def columns(i, m, first=False):
                t = i * 4 + m
                pe.wait_ge(S("col_split"), t + 1)
                for c in range(NG):
                    if first and m < 2:
                        pe.wait_ge(S("h_split"), c + 1)
                    else:
                        pe.wait_ge(S("col_evac"), (t - 2) * NG + c + 1)
                    for k in range(KD):
                        l = mm3(bank(3 * (1 - m % 2) + c, G), wcolhi[:, m, k], wcollo[:, m, k],
                                hhi[:, k, tok(c, G)], hlo[:, k, tok(c, G)], k == 0, k == KD - 1)
                    l.then_inc(S("col_done"), 1)

            for t in range(NGLU):
                columns(t // 4, t % 4, t < 4)
            columns(2, 0)
            pe.wait_ge(S("us_made"), 1)
            for j in range(CT):
                nc.tensor.transpose(bank(6)[:, j * P:(j + 1) * P], us[:, j], ident)
            for j in range(CT):
                l = nc.tensor.transpose(bank(7)[0:HIST, j * P:(j + 1) * P], uT[:, j, NP:NP + HIST], ident)
            l.then_inc(S("u_turned"), 1)
            for m in range(1, 4):
                columns(2, m)
            with pe.Fori(3, NCOL // 4) as i:
                for m in range(4):
                    columns(i, m)
            pe.wait_ge(S("col_evac"), NG * NCOL)

            def turn(c, t, j, first):
                pe.wait_ge(S("qn_made"), c * NT + t + 1)
                if not first:
                    pe.wait_ge(S("turn_made"), c * NT + t - 2)
                for p in range(HP):
                    l = nc.tensor.transpose(bank(3 + j)[:, p * P:(p + 1) * P], qn[:, j, p * P:(p + 1) * P], ident)
                l.then_inc(S("qk_turned"), 1)

            def project(c, i, before):
                for j in range(3):
                    n = c * NT + i * 3 + j
                    pe.wait_ge(S(f"hs_in{j}"), (c * NG + i + 1) * 16)
                    if not (c == 0 and before is None):
                        pe.wait_ge(S("qkv_evac"), n - 2)
                    for k in range(KD):
                        l = mm(bank(j), hs[:, j, k], wqkv[c % 2][:, k], start=k == 0, stop=k == KD - 1)
                    l.then_inc(S("qkv_done"), 1)
                    if j == 0 and before is not None:
                        bc, bt = before
                        if bc < 2:
                            turn(bc, bt, 2, bc == 0 and isinstance(bt, int) and bt < 3)
                    if j > 0 and c < 2:
                        turn(c, i * 3 + j - 1, j - 1, c == 0 and before is None)

            for c in range(3):
                pe.wait_ge(S(f"wqkv_in{c % 2}"), 16 * (c // 2 + 1))
                project(c, 0, None if c == 0 else (c - 1, NT - 1))
                if c == 0:
                    project(c, 1, (c, 2))
                    project(c, 2, (c, 5))
                else:
                    with pe.Fori(1, NG) as i:
                        project(c, i, (c, i * 3 - 1))

            pe.wait_ge(S("qkv_evac"), 3 * NT)
            pe.wait_ge(S("turn_made"), 2 * NT)
            pe.wait_ge(S("uo_made"), 2)

            def layer_sums(k, c):
                if k == 0:
                    pe.wait_ge(S("conv_made"), CT)
                    if c:
                        pe.wait_ge(S("d_made"), CT * c)
                else:
                    pe.wait_ge(S("sq_made"), c + 1)
                    if c:
                        pe.wait_ge(S("std_made"), c)
                for j in range(CT):
                    l = mm(bank(1 + 2 * k, G), ones, (cT if k == 0 else sqc)[:, j, tok(c, G)],
                           start=j == 0, stop=j == CT - 1)
                l.then_inc(S("csum_done" if k == 0 else "sqsum_done"), 1)

            N = len(units)

            def rows(h):
                return slice(64 * (h % 2), 64 * (h % 2) + 64)

            def logits(n):
                b, h = units[n]
                L = (b + 1) * P
                if n >= 2:
                    pe.wait_ge(S("biased"), n - 1)
                for o0 in range(0, L, 512):
                    w = min(512, L - o0)
                    l = mm(bank(2 * (n % 2), w=2)[:, o0:o0 + w], qT[rows(h), h // 2, tok(b)],
                           kT[rows(h), h // 2, o0:o0 + w])
                l.then_inc(S("qk_done"), 1)

            def turn_p(n):
                pe.wait_ge(S("p_made"), n + 1)
                if n:
                    pe.wait_ge(S("pT_made"), n)
                for k in range(units[n][0] + 1):
                    l = nc.tensor.transpose(bank(4, w=2)[:, tok(k)], lpP[n % 3][:, tok(k)], ident)
                l.then_inc(S("p_turned"), 1)

            def weighted(n):
                b, h = units[n]
                pe.wait_ge(S("pT_made"), n + 1)
                if h % 2 == 0 and n >= 4:
                    pe.wait_ge(S("attn_made"), n // 2 - 1)
                for k in range(b + 1):
                    l = mm(bank(6 + (n // 2) % 2)[rows(h), 0:P], vN[:, k, h * HD:(h + 1) * HD],
                           pT[:, n % 2, tok(k)], start=k == 0, stop=k == b)
                l.then_inc(S("pv_done"), 1)

            def logits_s(st_):
                pe.wait_ge(S(f"kc_in{st_ % 2}"), 16 * (st_ // 2 + 1))
                pe.wait_ge(S("qbd_made"), 4 * (st_ + 1))
                pe.wait_ge(S("biased"), N)
                if st_ >= 1:
                    pe.wait_ge(S("biased"), N + st_)
                for o0, w in ((0, 512), (512, 512), (PAST, P)):
                    dst = bank(1, w=3)[:, o0:o0 + w]
                    for c in range(HP):
                        keys = kcT[st_ % 2][:, c, o0:o0 + w] if o0 < PAST else kT[:, c, NP:NTOK]
                        l = mm(dst, qbd[:, st_, c], keys, start=c == 0, stop=c == HP - 1)
                l.then_inc(S("qk_done"), 1)

            for n in range(N + 3):
                if n == 4 * H:
                    pe.wait_ge(S("d_made"), NG * CT)
                    pe.wait_ge(S("std_made"), NG)
                if n < N:
                    logits(n)
                if ln_step(n):
                    layer_sums(*ln_step(n))
                if n >= 3:
                    weighted(n - 3)
                if 2 <= n <= N + 1:
                    turn_p(n - 2)
                if n == N:
                    logits_s(0)

            def turn_ps(st_):
                pe.wait_ge(S("p_made"), N + st_ + 1)
                pe.wait_ge(S("pT_made"), N + st_)
                if st_ == 0:
                    pe.wait_ge(S("attn_made"), N // 2)
                for k in range(9):
                    dst = bank(4, w=2)[:, tok(k)] if k < 8 else bank(6, P)
                    l = nc.tensor.transpose(dst, lp[:, (st_ + 1) % 2, tok(k)], ident)
                l.then_inc(S("p_turned"), 1)

            def weighted_s(st_):
                pe.wait_ge(S("pT_made"), N + st_ + 1)
                pe.wait_ge(S(f"vc_in{st_ % 2}"), 16 * (st_ // 2 + 1))
                pe.wait_ge(S("attn_made"), N // 2 + 5 * st_)
                for c in range(HP):
                    for k in range(9):
                        v = vc[st_ % 2][:, k] if k < 8 else vN[:, NT - 1]
                        l = mm(bank(7)[:, c * P:(c + 1) * P], v[:, c * P:(c + 1) * P], pT[:, st_ % 2, tok(k)],
                               start=k == 0, stop=k == 8)
                l.then_inc(S("pvS_done"), 1)

            for st_ in range(NS + 1):
                if st_:
                    turn_ps(st_ - 1)
                if 0 < st_ < NS:
                    logits_s(st_)
                if st_:
                    weighted_s(st_ - 1)


            def branches(i, first):
                for e in range(2):
                    if not (first and e == 0):
                        pe.wait_ge(S("merge_split"), i * 2 + e + 1 + 2 * NG)
                    for c in range(NG):
                        if not (first and e == 0):
                            pe.wait_ge(S("merged"), (i * 2 + e - 1) * NG + c + 1)
                        for g, hi, lo in ((1, chi, clo), (0, attnhi, attnlo)):
                            if first and e == 0:
                                pe.wait_ge(S("merge_split"), NG + 1 if g else NG + 2 + c)
                            for k in range(HP):
                                l = mm3(bank(3 * g + c, G), wabhi[:, e, 4 * g + k], wablo[:, e, 4 * g + k],
                                        hi[:, k, tok(c, G)], lo[:, k, tok(c, G)], k == 0, k == HP - 1)
                        l.then_inc(S("ab_done"), 1)

            branches(0, True)
            with pe.Fori(1, KD // 2) as i:
                branches(i, False)

            def turn_h2(t, j, first):
                pe.wait_ge(S("h2_made"), t + 1)
                if not first:
                    pe.wait_ge(S("h2T_split"), t * 2)
                for k in range(KD):
                    l = nc.tensor.transpose(bank(6, w=2)[:, tok(k)], xs[:, j, k * P:(k + 1) * P], ident)
                l.then_inc(S("h2_turned"), 1)

            def out_tile(i, first):
                for j in range(3):
                    t = i * 3 + j
                    if not first:
                        pe.wait_ge(S(f"hs2_in{j}"), i * 16)
                    if not first:
                        pe.wait_ge(S("x1_made"), (t - 2) * 2)
                    for f in range(2):
                        for k in range(KD):
                            m = mergedT[:, k, tok(t)] if first else hs2[:, j, k]
                            l = mm(bank(2 * j + f), m, wout[:, k, 512 * f:512 * f + 512],
                                   start=k == 0, stop=k == KD - 1)
                        if f == 0 and not (first and j == 0):
                            turn_h2(t - 1, (j + 2) % 3, first and j == 1)
                    l.then_inc(S("wo_done"), 1)

            pe.wait_ge(S("wout_in"), 16)
            pe.wait_ge(S("merged"), KD * NG)
            out_tile(0, True)
            with pe.Fori(1, NG) as i:
                out_tile(i, False)

            def gate_up(g, ct, e):
                pe.wait_ge(S("wgu_split"), g * FT + ct + 1)
                for f, made, done in ((0, "silu_made", "g_done"), (1, "f_made", "u_done")):
                    if not (isinstance(ct, int) and ct == 0):
                        pe.wait_ge(S(made), g * FT + ct)
                    for k in range(KD):
                        c = slice((8 * f + k) * P, (8 * f + k + 1) * P)
                        l = mm3(bank(6 + f, G), wguhi[:, e, c], wgulo[:, e, c], h2hi[:, k, tok(g, G)],
                                h2lo[:, k, tok(g, G)], k == 0, k == KD - 1)
                    l.then_inc(S(done), 1)

            def down(g, ct, e, first=False, last=False):
                pe.wait_ge(S("wd_split"), g * FT + ct + 1)
                pe.wait_ge(S("f_split"), g * FT + ct + 1)
                if first and not (isinstance(g, int) and g == 0):
                    pe.wait_ge(S("y_made"), g * 6)
                for tt in range(3):
                    for f in range(2):
                        c = slice(512 * f, 512 * f + 512)
                        l = mm3(bank(2 * tt + f), fhi[:, e, tok(tt)], flo[:, e, tok(tt)], wdhi[:, e, c], wdlo[:, e, c],
                                first, last)
                l.then_inc(S("down_done"), 1)

            def group(g):
                if isinstance(g, int):
                    pe.wait_ge(S("h2T_split"), 2 * NT - 2)
                    gate_up(g, 0, 0)
                    pe.wait_ge(S("f_made"), 1)
                    turn_h2(NT - 1, 2, False)
                    pe.wait_ge(S("h2T_split"), 2 * NT)
                    pe.wait_ge(S("x1_made"), 2 * NT)
                else:
                    gate_up(g, 0, 0)
                gate_up(g, 1, 1)
                down(g, 0, 0, first=True)
                with pe.Fori(1, FT // 2) as i:
                    gate_up(g, i * 2, 0)
                    down(g, i * 2 - 1, 1)
                    gate_up(g, i * 2 + 1, 1)
                    down(g, i * 2, 0)
                down(g, FT - 1, 1, last=True)

            group(0)
            with pe.Fori(1, NG) as g:
                group(g)

        @block.scalar
        def _(act):
            ac = nc.scalar.activation

            def x_squares(i, first=False):
                for j in range(3):
                    act.wait_ge(S(f"x_in{j}"), i * 16 + 16)
                    if not first:
                        act.wait_ge(S("h_turned"), i * 3 + j - 2)
                    ac(hb[:, j], xb[:, j], ACT.Square, accum_out=ss[:, j:j + 1]).then_inc(S("ss_made"), 1)

            def norm_group(i, last=False):
                for j in range(3):
                    act.wait_ge(S("h_turned"), i * 3 + j + 1)
                    for c in range(2):
                        ac(hT[:, 4 * c:4 * c + 4, tok(i * 3 + j)], bank(2 * j + c).rearrange("p (k t) -> p k t", k=4),
                           ACT.Copy).then_inc(S("hT_made"), 1)
                if not last:
                    x_squares(i + 1)
                for c in range(HP + 1):
                    act.wait_ge(S("iq_done"), i * (HP + 1) + c + 1)
                    if c < HP:
                        l = ac(iqT[:, c, tok(i, G)], bank(6 + c % 2, G), ACT.Copy)
                    else:
                        l = ac(ikwT[0:72, tok(i, G)], bank(6 + c % 2, G)[0:72], ACT.Copy)
                    l.then_inc(S("iq_made"), 1)

            x_squares(0, True)
            norm_group(0)
            with act.Fori(1, NG - 1) as i:
                norm_group(i)
            norm_group(NG - 1, last=True)
            act.wait_ge(S("state_turned"), 1)
            for c in range(2):
                ac(uT[:, :, UP:].rearrange("p j (s t) -> p j s t", s=NS)[:, :, 4 * c:4 * c + 4, 0:HIST],
                   bank(c).rearrange("p (j t) -> p j t", j=CT)[:, :, 0:120].rearrange("p j (s t) -> p j s t", s=4),
                   ACT.Copy).then_inc(S("state_made"), 1)
            act.wait_ge(S("ikw_turned"), 1)
            ac(ikwN[:, 0:5], bank(2, 360).rearrange("p (t c) -> p t c", c=72), ACT.Copy).then_inc(S("ikwN_made"), 1)
            ac(ikwN[:, 5:9], bank(3, 288).rearrange("p (t c) -> p t c", c=72), ACT.Copy).then_inc(S("ikwN_made"), 1)

            act.wait_ge(S("ikn_turned"), 1)
            for c in range(3):
                w = min(512, NTOK - 512 * c)
                ac(ikT[:, 512 * c:512 * c + w], bank(2 + c, w), ACT.Copy).then_inc(S("ikT_made"), 1)
            n = 0
            act.wait_ge(S("iw_made"), 1)
            act.wait_ge(S("bias_out"), 16)
            for b in range(2, PB):
                for h in range(H):
                    act.wait_ge(S("logit_done"), n + 1)
                    if n >= 2:
                        act.wait_ge(S("term_added"), n - 1)
                    ac(rl[:, n % 2, 0:(b + 1) * P], bank(2 + 2 * (n % 3), w=2)[:, 0:(b + 1) * P], ACT.Relu)\
                        .then_inc(S("relu_done"), 1)
                    act.wait_ge(S("relu_done"), n + 1)
                    ac(rl[:, n % 2, 0:(b + 1) * P], rl[:, n % 2, 0:(b + 1) * P], ACT.Copy, scale=iwN[:, b, h:h + 1])\
                        .then_inc(S("term_made"), 1)
                    n += 1
            def col_high(i, m):
                act.wait_ge(S(f"wcol_in{m}"), i * 16 + 16)
                ac(wcolhi[:, m], wcol[:, m], ACT.Copy).then_inc(S("col_high"), 1)

            act.wait_ge(S("term_added"), n)
            act.wait_ge(S("iqs_in"), 16 * H)
            for m in range(3):
                col_high(0, m)
            for st_ in range(NS):
                act.wait_ge(S("logit_done"), n + st_ + 1)
                if st_ >= 2:
                    act.wait_ge(S("heads_summed"), st_ - 1)
                ac(rl[:, st_ % 2], bank(2, w=3, n=128), ACT.Relu).then_inc(S("relu_done"), 1)
                c = st_ - (NS - NG)
                if c >= 0:
                    ac(hhi[:, :, tok(c, G)], hT[:, :, tok(c, G)], ACT.Copy).then_inc(S("h_high"), 1)

            act.wait_ge(S("heads_summed"), NS)
            ac(scoreS, bank(5, w=3, n=P), ACT.Copy).then_inc(S("scoreS_copied"), 1)

            def columns(i, m, glu):
                t = i * 4 + m
                e = m % 2
                if glu and t >= 2:
                    act.wait_ge(S("u_made"), 2 * (t // 2))
                if not glu and not (isinstance(t, int) and t < NGLU + 2):
                    act.wait_ge(S(f"gate_out{e}"), (i * 2 + m // 2 - NGLU // 2) * 16)
                for c in range(NG):
                    act.wait_ge(S("col_done"), t * NG + c + 1)
                    if glu:
                        l = ac((acopy if e else sigb)[:, c], bank(3 * (1 - e) + c, G), ACT.Copy if e else ACT.Sigmoid)
                    else:
                        l = ac(gb[:, e, tok(c, G)], bank(3 * (1 - e) + c, G), ACT.Sigmoid)
                    l.then_inc(S("col_evac"), 1)
                if not glu:
                    act.wait_ge(S("col_evac"), (t + 1) * NG)
                    act.dma_start(A["gate_scr"][bass.ds(t - NGLU, 1)].rearrange("o p t -> p (o t)"), gb[:, e])\
                        .then_inc(S(f"gate_out{e}"), 16)

            for t in range(NGLU + 4):
                columns(t // 4, t % 4, t < NGLU)
                col_high((t + 3) // 4, (t + 3) % 4)
                if t == NGLU:
                    act.wait_ge(S("u_turned"), 1)
                    ac(uo, bank(6), ACT.Copy).then_inc(S("uo_made"), 1)
                    ac(ut[0:HIST], bank(7)[0:HIST], ACT.Copy).then_inc(S("uo_made"), 1)
            with act.Fori(3, NCOL // 4 - 1) as i:
                for m in range(4):
                    columns(i, m, False)
                    col_high(i + (m + 3) // 4, (m + 3) % 4)
            for m in range(4):
                columns(NCOL // 4 - 1, m, False)
                if m == 0:
                    col_high(NCOL // 4 - 1, 3)

            def turned(c, t, j):
                act.wait_ge(S("qk_turned"), c * NT + t + 1)
                if c == 0:
                    act.dma_start(O["k"][tok(t), :], qn[:, j]).then_inc(S(f"k_out{j}"), 16)
                ac((kT if c == 0 else qT)[:, :, tok(t)], bank(3 + j).rearrange("p (c t) -> p c t", c=HP), ACT.Copy)\
                    .then_inc(S("turn_made"), 1)

            def evac(c, i, before):
                for j in range(3):
                    n = c * NT + i * 3 + j
                    act.wait_ge(S("qkv_done"), n + 1)
                    if not (c == 0 and before is None):
                        if c < 2:
                            act.wait_ge(S("qn_made"), n - 2)
                    if c < 2:
                        l = ac(raw[:, j], bank(j), ACT.Copy)
                    else:
                        l = ac(vN[:, bass.ds(i * 3 + j, 1)], bank(j).unsqueeze(1), ACT.Copy)
                    if c < 2:
                        l.then_inc(S("raw_made"), 1)
                        act.wait_ge(S("raw_made"), n + 1)
                        for h in range(H):
                            l = ac(bank(j)[:, h * HD:(h + 1) * HD], bank(j)[:, h * HD:(h + 1) * HD], ACT.Square,
                                   accum_out=ssq[:, j * H + h:j * H + h + 1])
                    l.then_inc(S("qkv_evac"), 1)
                    if c == 2:
                        act.wait_ge(S("qkv_evac"), n + 1)
                        act.dma_start(O["v"][tok(i * 3 + j), :],
                                      vN[:, bass.ds(i * 3 + j, 1)].rearrange("p o c -> p (o c)"))\
                            .then_inc(S(f"v_out{j}"), 16)
                    if j == 0 and before is not None and before[0] < 2:
                        turned(before[0], before[1], 2)
                    if j > 0 and c < 2:
                        turned(c, i * 3 + j - 1, j - 1)

            for c in range(3):
                evac(c, 0, None if c == 0 else (c - 1, NT - 1))
                with act.Fori(1, NG) as i:
                    evac(c, i, (c, i * 3 - 1))

            def layer_norm(k, c):
                if k == 0:
                    act.wait_ge(S("d_made"), CT * (c + 1))
                    ac(sqc[:, :, tok(c, G)], cT[:, :, tok(c, G)], ACT.Square).then_inc(S("sq_made"), 1)
                else:
                    act.wait_ge(S("sqsum_done"), c + 1)
                    ac(acc[:, tok(c, G)], bank(3, G), ACT.Copy).then_inc(S("std_made"), 1)
                    if c == NG - 1:
                        act.wait_ge(S("std_made"), NG)
                        ac(acc, acc, ACT.Sqrt, scale=1.0 / CH, bias=epsc).then_inc(S("std_made"), 1)

            def swish():
                act.wait_ge(S("dn_made"), CT)
                for j in range(CT):
                    ac(cT[:, j], cT[:, j], ACT.Silu, scale=lng[:, j:j + 1], bias=lnb[:, j:j + 1])\
                        .then_inc(S("c_made"), 1)

            N = len(units)

            def exps(n, dst, e):
                act.wait_ge(S("nmx_made"), n + 1)
                ac(dst, dst, ACT.Exp, bias=nmx[:, e:e + 1], accum_out=sm[:, e:e + 1]).then_inc(S("exp_done"), 1)

            for n in range(N + 3):
                if ln_step(n - 1):
                    layer_norm(*ln_step(n - 1))
                if n >= 3 and n % 2 == 0:
                    b, h = units[n - 3]
                    act.wait_ge(S("pv_done"), n - 2)
                    ac(attnT[:, h // 2, tok(b)], bank(6 + ((n - 3) // 2) % 2, P), ACT.Copy).then_inc(S("attn_made"), 1)
                if 2 <= n <= N + 1:
                    m = n - 2
                    L = (units[m][0] + 1) * P
                    act.wait_ge(S("p_turned"), m + 1)
                    if m >= 2:
                        act.wait_ge(S("pv_done"), m - 1)
                    ac(pT[:, m % 2, 0:L], bank(4, w=2)[:, 0:L], ACT.Copy).then_inc(S("pT_made"), 1)
                if n < N:
                    exps(n, lpP[n % 3][:, 0:(units[n][0] + 1) * P], n % 3)

            for st_ in range(NS + 1):
                if st_:
                    act.wait_ge(S("p_turned"), N + st_)
                    if st_ >= 3:
                        act.wait_ge(S("pvS_done"), st_ - 2)
                    ac(pT[:, (st_ - 1) % 2], bank(4, w=3, n=P), ACT.Copy).then_inc(S("pT_made"), 1)
                if st_ < NS:
                    exps(N + st_, lp[:, (st_ + 1) % 2], st_ % 2)
                if st_ == 1:
                    swish()

            def wab_high(i, e, first=False):
                act.wait_ge(S(f"wab_in{e}"), i * 16 + 16)
                if not first:
                    act.wait_ge(S("ab_done"), (i * 2 + e - 1) * NG)
                ac(wabhi[:, e], wab[:, e], ACT.Copy).then_inc(S("merge_high"), 1)

            act.wait_ge(S("qk_done"), N + NS)
            act.wait_ge(S("c_made"), CT)
            for c in range(NG):
                ac(chi[:, :, tok(c, G)], cT[:, :, tok(c, G)], ACT.Copy).then_inc(S("merge_high"), 1)
            wab_high(0, 0, True)
            act.wait_ge(S("attn_made"), N // 2 + 5 * NS)
            for c in range(NG):
                ac(attnhi[:, :, tok(c, G)], attnT[:, :, tok(c, G)], ACT.Copy).then_inc(S("merge_high"), 1)
            wab_high(0, 1, True)
            with act.Fori(1, KD // 2) as i:
                for e in range(2):
                    wab_high(i, e)

            def turned_h2(t):
                act.wait_ge(S("h2_turned"), t + 1)
                for f in range(2):
                    ac(h2hi[:, 4 * f:4 * f + 4, tok(t)], bank(6 + f).rearrange("p (k t) -> p k t", k=4), ACT.Copy)\
                        .then_inc(S("h2T_made"), 1)

            def squares(i, first):
                for j in range(3):
                    t = i * 3 + j
                    if not (first and j == 0):
                        turned_h2(t - 1)
                    act.wait_ge(S("x1_made"), (t + 1) * 2)
                    ac(xs[:, j], x1[:, bass.ds(t, 1)].rearrange("p o d -> p (o d)"), ACT.Square,
                       accum_out=ss[:, j:j + 1]).then_inc(S("ss_made"), 1)

            def gu_high(m, e):
                act.wait_ge(S(f"wgu_in{e}"), m * 16)
                ac(wguhi[:, e], wraw[:, e], ACT.Copy).then_inc(S("wgu_high"), 1)

            gu_high(1, 0)
            squares(0, True)
            with act.Fori(1, NG) as i:
                squares(i, False)
            def hidden(g, i, e, first=False):
                u = g * FT + i * 2 + e
                if not first:
                    act.wait_ge(S("u_done"), u)
                gu_high(g * (FT // 2) + i + 1 + e, 1 - e)
                act.wait_ge(S("g_done"), u + 1)
                ac(sg[:, e], bank(6, G), ACT.Silu).then_inc(S("silu_made"), 1)
                act.wait_ge(S("f_made"), u + 1)
                ac(fhi[:, e], sg[:, e], ACT.Copy).then_inc(S("f_high"), 1)
                if first:
                    turned_h2(NT - 1)
                act.wait_ge(S(f"wd_in{e}"), (g * (FT // 2) + i) * 16 + 16)
                ac(wdhi[:, e], wdraw[:, e], ACT.Copy).then_inc(S("wd_high"), 1)

            hidden(0, 0, 0, True)
            hidden(0, 0, 1)
            with act.Fori(1, FT // 2) as i:
                for e in range(2):
                    hidden(0, i, e)
            with act.Fori(1, NG) as g:
                with act.Fori(0, FT // 2) as i:
                    for e in range(2):
                        hidden(g, i, e)

        @block.vector
        def _(dve):
            ve = nc.vector

            def low(lo, x, hi):
                return ve.tensor_tensor(lo, x, hi.bitcast(F32), ALU.subtract)

            ch = Chain(dve, S("dve_chain"))
            ve.memset(ones, 1.0).then_inc(S("filled"), 1)
            ve.memset(uT[:, :, 0:HIST], 0.0).then_inc(S("filled"), 1)
            ch.add(ve.memset(SW, 0.0))
            dve.wait_ge(S("first_in"), 16 * 2)

            def norm_group(i):
                for j in range(3):
                    dve.wait_ge(S("rstd_made"), i * 3 + j + 1)
                    ve.scalar_tensor_tensor(hb[:, j], xb[:, j], rstd[:, j:j + 1], gmix, ALU.mult, ALU.mult)\
                        .then_inc(S("h_made"), 1)

            norm_group(0)
            dve.wait_ge(S("bias_done"), 1)
            ch.link(ve.tensor_copy(bfar[0:H], bank(7, 1)[0:H]))
            ve.tensor_scalar(brow[0:H], bank(7, RN)[0:H], bfar[0:H], None, ALU.subtract).then_inc(S("brow_made"), 1)

            with dve.Fori(1, NG) as i:
                norm_group(i)
            dve.wait_ge(S("ikwN_made"), 2)
            ve.tensor_scalar(iwN, ikwN[:, :, HD:72], ISC, None, ALU.mult).then_inc(S("iw_made"), 1)
            ch.link(ve.tensor_tensor(ikn[:, :, 0:HD], ikwN[:, :, 0:HD], ikwN[:, :, 0:HD], ALU.mult))
            ve.tensor_reduce(ssq[:, 0:NT], ikn[:, :, 0:HD], AX.X, ALU.add).then_inc(S("ssik_made"), 1)
            dve.wait_ge(S("rik_made"), 1)
            ch.link(ve.tensor_tensor(ikwN[:, :, 0:HD], ikwN[:, :, 0:HD],
                                     rsq[:, 0:NT].unsqueeze(2).to_broadcast([P, NT, HD]), ALU.mult))
            for c in range(2):
                ve.tensor_tensor(ikn[:, :, 64 * c:64 * c + 64], ikwN[:, :, 0:HD],
                                 ikg.unsqueeze(1).to_broadcast([P, NT, HD]), ALU.mult).then_inc(S("ikn_made"), 1)
            dve.wait_ge(S("iws_in"), 16 * H)
            ch.wait()
            for st_ in range(NS):
                ve.tensor_scalar(SW[:, st_, st_ * QS:(st_ + 1) * QS], delta, iwS[:, st_:st_ + 1], None, ALU.mult)\
                    .then_inc(S("sw_made"), 1)
            ve.memset(m8, 0.0).then_inc(S("sw_made"), 1)
            dve.wait_ge(S("sw_made"), NS + 1)
            for b, sc in [(b, score[b]) for b in range(2, PB)] + [(PB, scoreS)]:
                dve.wait_ge(S("score_done"), b - 1)
                for _ in range(TOPK // 8):
                    ch.link(ve.max(m8, sc))
                    ch.link(ve.match_replace(sc, m8, sc, TAKEN))
                ve.tensor_scalar(sc, sc, TAKEN, NEG, ALU.is_gt, ALU.mult).then_inc(S("mask_made"), 1)
            dve.wait_ge(S("u_turned"), 1)
            dve.wait_ge(S("u_made"), 2 * CT)

            def conv_tap(j, d):
                outs = (acc[:, 0:NP], acc[:, NP:NTOK].rearrange("p (s q) -> p s q", s=NS))
                w = cw[:, j, d:d + 1]
                for x, out in ((uT[:, j, d:d + NP], outs[0]), (uSamp[:, j, :, d:d + QS], outs[1])):
                    if d == 0:
                        ch.add(ve.tensor_scalar(out, x, w, cb[:, j:j + 1], ALU.mult, ALU.add))
                    elif (j, d) == (CT - 1, POOL_TAPS):
                        ch.add(ve.tensor_scalar(out, x, w, None, ALU.mult))
                    else:
                        ch.add(ve.scalar_tensor_tensor(out, x, w, out, ALU.mult, ALU.add))
                ch.wait()
                if (j, d) == (CT - 1, CK - 1):
                    dve.wait_ge(S("conv_pool_made"), 1)
                    ve.tensor_tensor(cT[:, j], acc, acc_pool, ALU.add).then_inc(S("conv_made"), 1)
                    dve.wait_ge(S("conv_made"), j + 1)
                elif d == CK - 1:
                    ve.tensor_copy(cT[:, j], acc).then_inc(S("conv_made"), 1)
                    dve.wait_ge(S("conv_made"), j + 1)

            all_taps = [(j, d) for j in range(CT) for d in range(POOL_TAPS if j == CT - 1 else 0, CK)]
            late = all_taps[-EARLY:]
            for j, d in all_taps[:-EARLY]:
                conv_tap(j, d)
            def less_mean(c):
                dve.wait_ge(S("csum_done"), c + 1)
                for j in range(CT):
                    ve.scalar_tensor_tensor(cT[:, j, tok(c, G)], bank(1, G), -1.0 / CH, cT[:, j, tok(c, G)],
                                            ALU.mult, ALU.add).then_inc(S("d_made"), 1)

            def over_std(j):
                dve.wait_ge(S("std_made"), NG + 1)
                if j < NG:
                    ch.link(ve.reciprocal(acc[:, tok(j, G)], acc[:, tok(j, G)]))
                else:
                    ve.tensor_tensor(cT[:, j - NG], cT[:, j - NG], acc, ALU.mult).then_inc(S("dn_made"), 1)

            dve.wait_ge(S("qkv_done"), 3 * NT)
            ve.memset(biasS, 0.0).then_inc(S("biasS_zero"), 1)
            N = len(units)

            def normalize(n, p, e):
                dve.wait_ge(S("exp_done"), n + 1)
                ch.link(ve.reciprocal(rc[:, e:e + 1], sm[:, e:e + 1]))
                ve.tensor_scalar(p, p, rc[:, e:e + 1], None, ALU.mult).then_inc(S("p_made"), 1)

            def bias_max(dst, src, add, e, start):
                return ve.tensor_tensor_reduce(dst, src, add, 1.0, start, ALU.add, ALU.max, mx[:, e:e + 1])

            def negate(n, e):
                dve.wait_ge(S("biased"), n + 1)
                ve.tensor_scalar(nmx[:, e:e + 1], mx[:, e:e + 1], -1.0, None, ALU.mult)\
                    .then_inc(S("nmx_made"), 1)

            def diagonal(st_):
                ch.link(ve.memset(qbd[:, st_], 0.0))
                for par in range(2):
                    r = slice(64 * par, 64 * par + 64)
                    t = slice(NP + st_ * QS, NP + (st_ + 1) * QS)
                    d = qbd[r, st_].rearrange("p c m -> p (c m)")
                    ve.tensor_copy(d[:, QS * par:QS * par + 480].rearrange("p (c x) -> p c x", x=160)[:, :, 0:QS],
                                   qT[r, 0:3, t]).then_inc(S("qbd_made"), 1)
                    ve.tensor_copy(d[:, 480 + QS * par:496 + QS * par], qT[r, 3, t]).then_inc(S("qbd_made"), 1)

            for n in range(N + 1):
                if N - NEARLY <= n < N:
                    diagonal(n - (N - NEARLY))
                if n < N:
                    b, h = units[n]
                    e, L = n % 3, (b + 1) * P
                    far = max(L - 2 * P, 0)
                    src = bank(2 * (n % 2), w=2)
                    dve.wait_ge(S("qk_done"), n + 1)
                    if n >= 3:
                        dve.wait_ge(S("p_turned"), n - 2)
                        dve.wait_ge(S("nmx_made"), n - 2)
                    start = -3e38
                    if far:
                        ch.link(bias_max(lpP[e][:, 0:far], src[:, 0:far], score[b][:, 0:far], 3 + e, -3e38))
                        start = mx[:, 3 + e:4 + e]
                    dve.wait_ge(S("nb_made"), n + 1)
                    bias_max(lpP[e][:, far:L], src[:, far:L], nb[n % 2][:, 2 * P - (L - far):2 * P], e, start)\
                        .then_inc(S("biased"), 1)
                    negate(n, e)
                if late:
                    conv_tap(*late.pop(0))
                if ln_step(n) and ln_step(n)[0] == 0:
                    less_mean(ln_step(n)[1])
                if LN_END <= n < LN_END + NG + CT:
                    over_std(n - LN_END)
                if n:
                    normalize(n - 1, lpP[(n - 1) % 3][:, 0:(units[n - 1][0] + 1) * P], (n - 1) % 3)
            dve.wait_ge(S("nb_made"), N)
            dve.wait_ge(S("biased"), N)
            for st_ in range(NEARLY, NS):
                diagonal(st_)

            def outputs(st_):
                dve.wait_ge(S("pvS_done"), st_ + 1)
                for par in range(2):
                    r = slice(64 * par, 64 * par + 64)
                    t = slice(NP + st_ * QS, NP + (st_ + 1) * QS)
                    o = bank(7)[r, QS * par:QS * par + 480].rearrange("p (c x) -> p c x", x=160)
                    ve.tensor_copy(attnT[r, 0:3, t], o[:, :, 0:QS]).then_inc(S("attn_made"), 1)
                    ve.tensor_copy(attnT[r, 3, t], bank(7)[r, 480 + QS * par:496 + QS * par])\
                        .then_inc(S("attn_made"), 1)
                ve.memset(m8, 0.0).then_inc(S("attn_made"), 1)

            def wab_low(m, e, first=False):
                dve.wait_ge(S("merge_high"), NG + 1 if first else m + 1 + 2 * NG)
                low(wablo[:, e], wab[:, e], wabhi[:, e]).then_inc(S("merge_split"), 1)

            def conv_low():
                for c in range(NG):
                    dve.wait_ge(S("merge_high"), c + 1)
                    low(clo[:, :, tok(c, G)], cT[:, :, tok(c, G)], chi[:, :, tok(c, G)]).then_inc(S("merge_split"), 1)
                wab_low(0, 0, True)

            for st_ in range(NS + 1):
                n = N + st_
                if st_ < NS:
                    dve.wait_ge(S("qk_done"), n + 1)
                    dve.wait_ge(S("p_turned"), n - 1)
                    dve.wait_ge(S("maskS_made"), st_ + 1)
                    bias_max(lp[:, (st_ + 1) % 2], bank(1, w=3, n=P), maskS[:, st_ % 2], st_ % 2, -3e38)\
                        .then_inc(S("biased"), 1)
                    negate(n, st_ % 2)
                    normalize(n, lp[:, (st_ + 1) % 2], st_ % 2)
                if st_ == NS:
                    conv_low()
                if st_:
                    outputs(st_ - 1)

            dve.wait_ge(S("attn_made"), N // 2 + 5 * NS)
            for c in range(NG):
                dve.wait_ge(S("merge_high"), NG + 2 + c)
                low(attnlo[:, :, tok(c, G)], attnT[:, :, tok(c, G)], attnhi[:, :, tok(c, G)])\
                    .then_inc(S("merge_split"), 1)

            def gated(i, first=False, last=False):
                for e in range(2):
                    if not (last and e == 1):
                        wab_low(i * 2 + e + 1, 1 - e)
                    for g in range(2):
                        dve.wait_ge(S(f"gt_in{e}{g}"), i * 16 + 16)
                    for c in range(NG):
                        m = (i * 2 + e) * NG + c
                        q = (e * NG + c) % 2
                        dve.wait_ge(S("ab_done"), m + 1)
                        if not (first and e == 0 and c < 2):
                            dve.wait_ge(S("merged"), m - 1)
                        for g in range(2):
                            ve.tensor_tensor(part[:, q, g], bank(3 * g + c, G), gt[:, e, g, tok(c, G)], ALU.mult)\
                                .then_inc(S("parts"), 1)
                        dve.wait_ge(S("parts"), m * 2 + 2)
                        ve.tensor_tensor(mergedT[:, bass.ds(i * 2 + e, 1), tok(c, G)], part[:, q, 0:1],
                                         part[:, q, 1:2], ALU.add).then_inc(S("merged"), 1)

            gated(0, True)
            with dve.Fori(1, KD // 2 - 1) as i:
                gated(i)
            gated(KD // 2 - 1, last=True)

            dve.wait_ge(S("gffn_in"), 16)

            def normed(t, j):
                dve.wait_ge(S("rstd_made"), NT + t + 1)
                ve.scalar_tensor_tensor(xs[:, j], x1[:, bass.ds(t, 1)].rearrange("p o d -> p (o d)"),
                                        rstd[:, j:j + 1], gmix, ALU.mult, ALU.mult).then_inc(S("h2_made"), 1)

            def h2_low(t):
                dve.wait_ge(S("h2T_made"), t * 2 + 2)
                for f in range(2):
                    low(h2lo[:, 4 * f:4 * f + 4, tok(t)], bank(6 + f).rearrange("p (k t) -> p k t", k=4),
                        h2hi[:, 4 * f:4 * f + 4, tok(t)]).then_inc(S("h2T_split"), 1)

            def gu_low(m, e):
                dve.wait_ge(S("wgu_high"), m)
                low(wgulo[:, e], wraw[:, e], wguhi[:, e]).then_inc(S("wgu_split"), 1)

            def residual(i, first, last=False):
                for j in range(3):
                    t = i * 3 + j
                    if not (first and j == 0):
                        h2_low(t - 1)
                    dve.wait_ge(S("wo_done"), t + 1)
                    if last and j == 2:
                        gu_low(1, 0)
                    dve.wait_ge(S(f"xs_in{j}"), i * 16 + 16)
                    for f in range(2):
                        r = slice(512 * f, 512 * f + 512)
                        ve.tensor_tensor(x1[:, bass.ds(t, 1), r], bank(2 * j + f).unsqueeze(1),
                                         xs[:, j:j + 1, r], ALU.add).then_inc(S("x1_made"), 1)
                    normed(t, j)

            residual(0, True)
            with dve.Fori(1, NG - 1) as i:
                residual(i, False)
            residual(NG - 1, False, last=True)
            def hidden_tile(g, i, e, first=False):
                u = g * FT + i * 2 + e
                gu_low(u + 2, 1 - e)
                dve.wait_ge(S("u_done"), u + 1)
                dve.wait_ge(S("silu_made"), u + 1)
                ve.tensor_tensor(sg[:, e], sg[:, e], bank(7, G), ALU.mult).then_inc(S("f_made"), 1)
                dve.wait_ge(S("f_high"), u + 1)
                low(flo[:, e], sg[:, e], fhi[:, e]).then_inc(S("f_split"), 1)
                if first:
                    h2_low(NT - 1)
                dve.wait_ge(S("wd_high"), u + 1)
                low(wdlo[:, e], wdraw[:, e], wdhi[:, e]).then_inc(S("wd_split"), 1)

            def hidden(g, first):
                if first:
                    hidden_tile(g, 0, 0, True)
                    hidden_tile(g, 0, 1)
                with dve.Fori(1 if first else 0, FT // 2) as i:
                    for e in range(2):
                        hidden_tile(g, i, e)
                dve.wait_ge(S("down_done"), (g + 1) * FT)
                for tt in range(3):
                    if not first:
                        dve.wait_ge(S(f"y_out{tt}"), g * 16)
                    for f in range(2):
                        r = slice(512 * f, 512 * f + 512)
                        ve.tensor_tensor(ys[:, tt:tt + 1, r], bank(2 * tt + f).unsqueeze(1),
                                         x1[:, bass.ds(g * 3 + tt, 1), r], ALU.add).then_inc(S("y_made"), 1)

            hidden(0, True)
            with dve.Fori(1, NG) as g:
                hidden(g, False)

        @block.gpsimd
        def _(pool):
            gp = nc.gpsimd
            ch = Chain(pool, S("pool_chain"))
            ch.add(gp.memset(mhalf, -0.5))
            ch.add(gp.memset(epsc, EPS))
            ch.add(gp.memset(eps8, EPS))
            ch.add(gp.memset(per_d, 1.0 / D))
            ch.add(gp.memset(per_hd, 1.0 / HD))
            ch.wait()

            def norm_group(i):
                for j in range(3):
                    pool.wait_ge(S("ss_made"), i * 3 + j + 1)
                    ch.link(gp.tensor_tensor(ms[:, j:j + 1], ss[:, j:j + 1], per_d, ALU.mult))
                    ch.link(gp.tensor_tensor(ms[:, j:j + 1], ms[:, j:j + 1], epsc, ALU.add))
                    gp.tensor_tensor(rstd[:, j:j + 1], ms[:, j:j + 1], mhalf[:, 0:1], ALU.pow)\
                        .then_inc(S("rstd_made"), 1)

            norm_group(0)
            with pool.Fori(1, NG) as i:
                ch.loop(i - 1, 6)
                norm_group(i)
            ch.done(NG - 1)
            pool.wait_ge(S("const_in"), 16 * NCONST)
            ch.link(gp.tensor_scalar(qg, qg, HD ** -0.5, 0.0, ALU.mult, ALU.add))
            pool.wait_ge(S("ssik_made"), 1)
            ch.link(gp.tensor_scalar(msq[:, 0:NT], ssq[:, 0:NT], 1.0 / HD, EPS, ALU.mult, ALU.add))
            gp.tensor_tensor(rsq[:, 0:NT], msq[:, 0:NT], mhalf[:, 0:NT], ALU.pow).then_inc(S("rik_made"), 1)
            n = 0
            for b in range(2, PB):
                L = (b + 1) * P
                for h in range(H):
                    pool.wait_ge(S("term_made"), n + 1)
                    if h == 0:
                        l = gp.tensor_copy(score[b], rl[:, n % 2, 0:L])
                    else:
                        pool.wait_ge(S("term_added"), n)
                        l = gp.tensor_tensor(score[b], rl[:, n % 2, 0:L], score[b], ALU.add)
                    l.then_inc(S("term_added"), 1)
                    n += 1
                pool.wait_ge(S("term_added"), n)
                gp.memset(score[b][0:CHUNK, L - CHUNK:L], NEG).then_inc(S("score_done"), 1)
            def low(lo, x, hi):
                return gp.tensor_tensor(lo, x, hi.bitcast(F32), ALU.subtract)

            def col_low(t):
                pool.wait_ge(S("col_high"), t + 1)
                low(wcollo[:, t % 4], wcol[:, t % 4], wcolhi[:, t % 4]).then_inc(S("col_split"), 1)

            for m in range(3):
                col_low(m)
            pool.wait_ge(S("hT_out"), 16 * NT)
            for c in range(NG):
                pool.wait_ge(S("h_high"), c + 1)
                low(hlo[:, :, tok(c, G)], hT[:, :, tok(c, G)], hhi[:, :, tok(c, G)]).then_inc(S("h_split"), 1)
            pool.wait_ge(S("scoreS_copied"), 1)
            gp.tensor_tensor(scoreS[:, PAST:LS], scoreS[:, PAST:LS], newneg, ALU.add).then_inc(S("score_done"), 1)
            def conv_tap(j, d):
                w = cw[:, j, d:d + 1]
                if d == 0:
                    outs = (acc_pool[:, 0:NP], acc_pool[:, NP:NTOK].rearrange("p (s q) -> p s q", s=NS))
                else:
                    outs = (tap[:, 0:NP], tap[:, NP:NTOK].rearrange("p (s q) -> p s q", s=NS))
                ch.wait()
                for x, out in ((uT[:, j, d:d + NP], outs[0]), (uSamp[:, j, :, d:d + QS], outs[1])):
                    if d == 0:
                        ch.add(gp.tensor_scalar(out, x, w, cb[:, j:j + 1], ALU.mult, ALU.add))
                    else:
                        ch.add(gp.tensor_scalar(out, x, w, None, ALU.mult))
                if d:
                    ch.wait()
                    l = gp.tensor_tensor(acc_pool, tap, acc_pool, ALU.add)
                    if d == POOL_TAPS - 1:
                        l.then_inc(S("conv_pool_made"), 1)
                    else:
                        ch.add(l)

            pool.wait_ge(S("state_made"), 2)
            taps = 0
            for t in range(NCOL - 3):
                col_low(t + 3)
                if t < NGLU and t % 2:
                    j = t // 2
                    pool.wait_ge(S("col_evac"), NG * (t + 1))
                    a, b = (v.rearrange("p c t -> p (c t)") for v in (acopy, sigb))
                    gp.tensor_tensor(uT[:, j, HIST:UP], a[:, 0:NP], b[:, 0:NP], ALU.mult).then_inc(S("u_made"), 1)
                    gp.tensor_tensor(uSamp[:, j, :, HIST:US], a[:, NP:NTOK].rearrange("p (s q) -> p s q", s=NS),
                                     b[:, NP:NTOK].rearrange("p (s q) -> p s q", s=NS), ALU.mult)\
                        .then_inc(S("u_made"), 1)
                if t == NGLU - 1:
                    pool.wait_ge(S("u_made"), 2 * CT)
                    for j in range(CT):
                        l = gp.tensor_copy(us[:, j].rearrange("p (s q) -> p s q", s=NS), uSamp[:, j, :, HIST:US])
                    l.then_inc(S("us_made"), 1)
                if t == NGLU + 1:
                    pool.wait_ge(S("u_turned"), 1)
                    pool.wait_ge(S("out_state"), 48)
                if t > NGLU:
                    conv_tap(CT - 1, taps)
                    taps += 1
            for e in range(2):
                pool.wait_ge(S(f"gate_out{e}"), 16 * KD)

            def qk_norm(c, i, first):
                for j in range(3):
                    n = c * NT + i * 3 + j
                    pool.wait_ge(S("qkv_evac"), n + 1)
                    if c < 2:
                        q3 = raw[:, j].rearrange("p (h d) -> p h d", h=H)
                        r = slice(j * H, (j + 1) * H)
                        ch.link(gp.tensor_tensor(msq[:, r], ssq[:, r], per_hd, ALU.mult))
                        ch.link(gp.tensor_tensor(msq[:, r], msq[:, r], eps8, ALU.add))
                        ch.link(gp.tensor_tensor(rsq[:, r], msq[:, r], mhalf[:, 0:H], ALU.pow))
                        ch.link(gp.tensor_tensor(q3, q3, rsq[:, r].unsqueeze(2).to_broadcast([P, H, HD]), ALU.mult))
                        if not (c == 0 and first):
                            pool.wait_ge(S("qk_turned"), n - 2)
                            if c == 0:
                                pool.wait_ge(S(f"k_out{j}"), i * 16)
                            else:
                                pool.wait_ge(S(f"k_out{j}"), NG * 16)
                        gp.tensor_tensor(qn[:, j], raw[:, j], kg if c == 0 else qg, ALU.mult).then_inc(S("qn_made"), 1)

            for c in range(2):
                qk_norm(c, 0, True)
                with pool.Fori(1, NG) as i:
                    ch.loop(i - 1, 12)
                    qk_norm(c, i, False)
                ch.done(NG - 1)
            while taps < POOL_TAPS:
                conv_tap(CT - 1, taps)
                taps += 1
            ch.link(gp.memset(mask0, 0.0))
            ch.link(gp.memset(mask0[0:CHUNK, 2 * P - CHUNK:2 * P], NEG))
            pool.wait_ge(S("near_in"), 16 * H)
            for n, (b, h) in enumerate(units):
                if n >= 2:
                    pool.wait_ge(S("biased"), n - 1)
                if b >= 2:
                    pool.wait_ge(S("mask_made"), b - 1)
                m = mask0 if b < 2 else score[b][:, (b - 1) * P:(b + 1) * P]
                gp.tensor_tensor(nb[n % 2], m, near[:, h], ALU.add).then_inc(S("nb_made"), 1)
            pool.wait_ge(S("biasS_in"), 16 * 2 * H)
            for st_ in range(NS):
                pool.wait_ge(S(f"maskS_in{st_ % 2}"), 16 * (st_ // 2 + 1))
                gp.tensor_tensor(maskS[:, st_ % 2], maskS[:, st_ % 2], biasS, ALU.add).then_inc(S("maskS_made"), 1)

            def norm2_group(i):
                for j in range(3):
                    pool.wait_ge(S("ss_made"), NT + i * 3 + j + 1)
                    ch.link(gp.tensor_tensor(ms[:, j:j + 1], ss[:, j:j + 1], per_d, ALU.mult))
                    ch.link(gp.tensor_tensor(ms[:, j:j + 1], ms[:, j:j + 1], epsc, ALU.add))
                    gp.tensor_tensor(rstd[:, j:j + 1], ms[:, j:j + 1], mhalf[:, 0:1], ALU.pow)\
                        .then_inc(S("rstd_made"), 1)

            with pool.Fori(0, NG) as i:
                ch.loop(i, 6)
                norm2_group(i)
            ch.done(NG)


def layouts(i):
    w_in = i["w_in"][0]
    o_iq = 3 * AW
    cat = lambda *a: np.ascontiguousarray(np.concatenate(a, axis=0))
    con = np.ascontiguousarray
    k_first = lambda w: con(w.reshape(-1, P, w.shape[1]).transpose(1, 0, 2))
    cols = lambda w: con(w.reshape(-1, P, w.shape[1] // P, P).transpose(2, 1, 0, 3))
    o_ik = o_iq + IDXC
    o_glu = o_ik + HD + H
    out = {
        "x": cat(i["x_prompt"][0], i["x_sample"].reshape(-1, D)),
        "ident": np.eye(P, dtype=np.float32),
        "delta": con(np.tile(np.eye(QS, dtype=np.float32), (H, 1))),
        "newneg": np.where(np.kron(np.eye(NS), np.ones((QS, QS))) > 0, 0.0, NEG).astype(np.float32),
        "onehot": bucket_rows(),
        "rel_bias": con(i["rel_bias"]),
        "cache_k": con(i["cache_k"][0].reshape(NS, PAST, HP, P).transpose(0, 3, 2, 1)),
        "cache_v": con(i["cache_v"][0].reshape(NS, PAST, AW)),
        "norm_mix_g": con(i["norm_mix_g"][0]),
        "qg": con(np.tile(i["q_norm_g"][0], H)),
        "kg": con(np.tile(i["k_norm_g"][0], H)),
        "idx_k_norm_g": con(i["idx_k_norm_g"][0]),
        "w_iq": k_first(w_in[:, o_iq:o_ik]),
        "w_ikw": k_first(w_in[:, o_ik:o_glu]),
        "conv_w": con(i["conv_dw_w"][0, :, 0].T.reshape(CT, P, CK).transpose(1, 0, 2)),
        "conv_b": con(i["conv_dw_b"][0].reshape(CT, P).T),
        "conv_ln_g": con(i["conv_ln_g"][0].reshape(CT, P).T),
        "conv_ln_b": con(i["conv_ln_b"][0].reshape(CT, P).T),
        "w_cols": cat(np.stack([cols(w_in[:, o_glu + CH:o_glu + 2 * CH]), cols(w_in[:, o_glu:o_glu + CH])], axis=1)
                      .reshape(2 * CT, P, KD, P), cols(w_in[:, o_glu + 2 * CH:])),
        "w_qkv": con(np.stack([k_first(w_in[:, o:o + AW]) for o in (AW, 0, 2 * AW)])),
        "w_ab": cols(cat(i["w_attn_out"][0], i["w_conv_out"][0])),
        "w_out": k_first(i["w_out"][0]),
        "norm_ffn_g": con(i["norm_ffn_g"][0]),
        "w_ffn": con(np.concatenate([cols(i["w_ffn_gate"][0]).reshape(FT, P, D), cols(i["w_ffn_up"][0]).reshape(FT, P, D),
                                     i["w_ffn_down"][0].reshape(FT, P, D)], axis=2)[list(range(FT)) + [0]]),
        "state": con(i["state_conv"][0].reshape(NS * HIST, CH)),
        "cache_ik": con(i["cache_idx_k"][0].transpose(0, 2, 1)),
    }
    return out


SCRATCH = {"hT_scr": (NT, P, KD * P), "iw_scr": (P, H), "gate_scr": (2 * KD, P, NTOK), "bias_scr": (H, P, RN), "mask_scr": (P, LS)}
OUTS = {"y": (NTOK, D), "k": (NTOK, AW), "v": (NTOK, AW), "ik": (NTOK, HD),
        "conv_prompt": (HIST, CH), "conv_sample": (NS * HIST, CH)}


def kernel(**inputs):
    import concourse.bacc as bacc
    from concourse.bass_utils import run_bass_kernel_spmd

    nc = bacc.Bacc("TRN2", target_bir_lowering=False, num_devices=1)
    arrays = {f"in_{k}": v for k, v in layouts({k: np.asarray(v) for k, v in inputs.items()}).items()}
    A = {k[3:]: nc.dram_tensor(k, v.shape, mybir.dt.from_np(v.dtype), kind="ExternalInput").ap()
         for k, v in arrays.items()}
    A.update({k: nc.dram_tensor(k, sh, F32, kind="Internal").ap() for k, sh in SCRATCH.items()})
    O = {k: nc.dram_tensor(f"out_{k}", sh, F32, kind="ExternalOutput").ap() for k, sh in OUTS.items()}
    build(nc, A, O)
    r = run_bass_kernel_spmd(nc, [arrays], core_ids=[0]).results[0]
    y, k, v, ik, cp, cs = (r[f"out_{n}"] for n in ("y", "k", "v", "ik", "conv_prompt", "conv_sample"))
    return (y[:NP].reshape(1, NP, D), y[NP:].reshape(NS, QS, D),
            k[:NP].reshape(1, 1, NP, H, HD), v[:NP].reshape(1, 1, NP, H, HD), ik[:NP].reshape(1, 1, NP, HD),
            cp.reshape(1, 1, HIST, CH),
            k[NP:].reshape(1, NS, QS, H, HD), v[NP:].reshape(1, NS, QS, H, HD), ik[NP:].reshape(1, NS, QS, HD),
            cs.reshape(1, NS, HIST, CH))
```
